# Optimizing a Trainium2 kernel written in Bass

```python
import math
import jax
import jax.numpy as jnp
from jax import lax
import numpy as np

D_MODEL = 2048
BATCH = 1
SEQ = 256
DEPTH = 1

CHUNK = 64
MEM_LEN = 256
MIX = D_MODEL
EPS = 1e-6
NEG = -1e30

MLA_HEADS = 6
MLA_NOPE = 128
MLA_ROPE = 64
MLA_V = 128
MLA_Q_RANK = 512
MLA_KV_RANK = 256
ROPE_THETA = 10000.0
Q_BLOCK = 128

SSM_INNER = 768
SSM_HEAD_DIM = 64
SSM_HEADS = SSM_INNER // SSM_HEAD_DIM
SSM_GROUPS = 2
SSM_STATE = 128
SSM_CONV = 4
SSM_CONV_DIM = SSM_INNER + 2 * SSM_GROUPS * SSM_STATE

SWA_HEADS = 8
SWA_KV_HEADS = 2
SWA_HEAD_DIM = 64
SWA_WINDOW = 128
SWA_WINDOW_CHUNKS = SWA_WINDOW // CHUNK

X_HEADS = 4
X_HEAD_DIM = 128

D_FF = 5632
FFN_CONV = 3

MLA_COLS = MLA_Q_RANK + MLA_KV_RANK + MLA_ROPE
SSM_COLS = SSM_INNER + SSM_CONV_DIM + SSM_HEADS
SWA_COLS = (SWA_HEADS + 2 * SWA_KV_HEADS) * SWA_HEAD_DIM
IN_COLS = MLA_COLS + SSM_COLS + SWA_COLS
OUT_COLS = MLA_HEADS * MLA_V + SSM_INNER + SWA_HEADS * SWA_HEAD_DIM

kernel_name = "hybrid_mla_ssd_swa_stream_encoder"

def rmsnorm(x, g):
    xf = x.astype(jnp.float32)
    y = xf * lax.rsqrt(jnp.mean(xf * xf, axis=-1, keepdims=True) + EPS) * g.astype(jnp.float32)
    return y.astype(x.dtype)

def causal_dwconv(x, w, b):
    k_w = w.shape[0]
    seq = x.shape[1]
    xp = jnp.pad(x, ((0, 0), (k_w - 1, 0), (0, 0)))
    return sum(xp[:, k:k + seq] * w[k] for k in range(k_w)) + b

def rope_tables(positions):
    inv = ROPE_THETA ** (-jnp.arange(0, MLA_ROPE, 2, dtype=jnp.float32) / MLA_ROPE)
    ang = positions.astype(jnp.float32)[..., None] * inv
    return jnp.cos(ang)[:, :, None, :], jnp.sin(ang)[:, :, None, :]

def apply_rope(t, cos, sin):
    t1, t2 = jnp.split(t, 2, axis=-1)
    return jnp.concatenate([t1 * cos - t2 * sin, t2 * cos + t1 * sin], axis=-1).astype(t.dtype)

def chunk_causal_attention(q, k, v, scale):
    bsz, seq, heads, dk = q.shape
    dv = v.shape[-1]
    nb = seq // Q_BLOCK
    qb = q.reshape(bsz, nb, Q_BLOCK, heads, dk).swapaxes(0, 1)
    key_chunk = jnp.arange(seq) // CHUNK

    def one_block(args):
        qblk, bi = args
        s = jnp.einsum('bqhd,bkhd->bhqk', qblk, k, preferred_element_type=jnp.float32) * scale
        q_chunk = (bi * Q_BLOCK + jnp.arange(Q_BLOCK)) // CHUNK
        mask = key_chunk[None, :] <= q_chunk[:, None]
        p = jax.nn.softmax(jnp.where(mask, s, NEG), axis=-1).astype(v.dtype)
        return jnp.einsum('bhqk,bkhd->bqhd', p, v)

    o = lax.map(one_block, (qb, jnp.arange(nb)))
    return o.swapaxes(0, 1).reshape(bsz, seq, heads, dv)

def mla_mixer(p, cos, sin, q_norm, w_uq, kv_norm, w_ukv, out_norm):
    bsz, seq, _ = p.shape
    c_q, c_kv, k_r = jnp.split(p, [MLA_Q_RANK, MLA_Q_RANK + MLA_KV_RANK], axis=-1)
    q = (rmsnorm(c_q, q_norm) @ w_uq).reshape(bsz, seq, MLA_HEADS, MLA_NOPE + MLA_ROPE)
    q = jnp.concatenate([q[..., :MLA_NOPE], apply_rope(q[..., MLA_NOPE:], cos, sin)], axis=-1)
    kv = (rmsnorm(c_kv, kv_norm) @ w_ukv).reshape(bsz, seq, MLA_HEADS, MLA_NOPE + MLA_V)
    k_rope = apply_rope(k_r.reshape(bsz, seq, 1, MLA_ROPE), cos, sin)
    k = jnp.concatenate([kv[..., :MLA_NOPE],
                         jnp.broadcast_to(k_rope, (bsz, seq, MLA_HEADS, MLA_ROPE)).astype(kv.dtype)], axis=-1)
    v = kv[..., MLA_NOPE:]
    o = chunk_causal_attention(q, k, v, (MLA_NOPE + MLA_ROPE) ** -0.5)
    return rmsnorm(o.reshape(bsz, seq, MLA_HEADS * MLA_V), out_norm)

def ssd_scan(x, dt, a, b_in, c_in):
    bsz, seq, heads, hp = x.shape
    groups, n = b_in.shape[2], b_in.shape[3]
    r = heads // groups
    q = CHUNK
    nc = seq // q
    xc = x.reshape(bsz, nc, q, groups, r, hp)
    dtc = dt.reshape(bsz, nc, q, groups, r)
    ac = dtc * a.reshape(groups, r)
    bc = b_in.reshape(bsz, nc, q, groups, n)
    cc = c_in.reshape(bsz, nc, q, groups, n)
    a_cum = jnp.cumsum(ac, axis=2)
    seg = a_cum[:, :, :, None] - a_cum[:, :, None, :]
    causal = jnp.tril(jnp.ones((q, q), dtype=bool))[:, :, None, None]
    lmat = jnp.exp(jnp.where(causal, seg, -jnp.inf))
    cb = jnp.einsum('bcign,bcjgn->bcijg', cc, bc, preferred_element_type=jnp.float32)
    w = cb[..., None] * lmat * dtc[:, :, None]
    y_diag = jnp.einsum('bcijgr,bcjgrp->bcigrp', w, xc)
    decay = jnp.exp(a_cum[:, :, -1:] - a_cum)
    states = jnp.einsum('bcjgn,bcjgr,bcjgrp->bcgrpn', bc, decay * dtc, xc)
    chunk_decay = jnp.exp(a_cum[:, :, -1])

    def step(h, inp):
        s, d = inp
        return h * d[..., None, None] + s, h

    h0 = jnp.zeros((bsz, groups, r, hp, n), dtype=states.dtype)
    _, h_prev = lax.scan(step, h0, (states.swapaxes(0, 1), chunk_decay.swapaxes(0, 1)))
    h_prev = h_prev.swapaxes(0, 1)
    y_off = jnp.einsum('bcign,bcgrpn,bcigr->bcigrp', cc, h_prev, jnp.exp(a_cum))
    return (y_diag + y_off).reshape(bsz, seq, heads, hp).astype(x.dtype)

def mamba2_mixer(p, conv_w, conv_b, dt_bias, a_log, d_skip, norm_g):
    bsz, seq, _ = p.shape
    z, xbc, dt_raw = jnp.split(p, [SSM_INNER, SSM_INNER + SSM_CONV_DIM], axis=-1)
    xbc = jax.nn.silu(causal_dwconv(xbc, conv_w, conv_b))
    xs, b_in, c_in = jnp.split(xbc, [SSM_INNER, SSM_INNER + SSM_GROUPS * SSM_STATE], axis=-1)
    dt = jax.nn.softplus(dt_raw.astype(jnp.float32) + dt_bias.astype(jnp.float32))
    a = -jnp.exp(a_log.astype(jnp.float32))
    xs = xs.reshape(bsz, seq, SSM_HEADS, SSM_HEAD_DIM)
    y = ssd_scan(xs, dt, a,
                 b_in.reshape(bsz, seq, SSM_GROUPS, SSM_STATE),
                 c_in.reshape(bsz, seq, SSM_GROUPS, SSM_STATE))
    y = (y + d_skip[:, None] * xs).reshape(bsz, seq, SSM_INNER)
    return rmsnorm(y * jax.nn.silu(z), norm_g)

def swa_mixer(p, sinks, out_norm):
    bsz, seq, _ = p.shape
    nc = seq // CHUNK
    rep = SWA_HEADS // SWA_KV_HEADS
    q, k, v = jnp.split(p, [SWA_HEADS * SWA_HEAD_DIM, (SWA_HEADS + SWA_KV_HEADS) * SWA_HEAD_DIM], axis=-1)
    q = q.reshape(bsz, nc, CHUNK, SWA_KV_HEADS, rep, SWA_HEAD_DIM)
    k = k.reshape(bsz, nc, CHUNK, SWA_KV_HEADS, SWA_HEAD_DIM)
    v = v.reshape(bsz, nc, CHUNK, SWA_KV_HEADS, SWA_HEAD_DIM)

    def band(t):
        parts = [jnp.pad(t, ((0, 0), (d, 0), (0, 0), (0, 0), (0, 0)))[:, :nc]
                 for d in range(SWA_WINDOW_CHUNKS - 1, -1, -1)]
        return jnp.concatenate(parts, axis=2)

    kb, vb = band(k), band(v)
    s = jnp.einsum('bcqgrd,bckgd->bcgrqk', q, kb, preferred_element_type=jnp.float32) * SWA_HEAD_DIM ** -0.5
    dist = SWA_WINDOW_CHUNKS - 1 - jnp.arange(SWA_WINDOW_CHUNKS * CHUNK) // CHUNK
    valid = jnp.arange(nc)[:, None] >= dist[None, :]
    s = jnp.where(valid[None, :, None, None, None, :], s, NEG)
    sink = sinks.astype(jnp.float32).reshape(SWA_KV_HEADS, rep)[None, None, :, :, None, None]
    m = jnp.maximum(jnp.max(s, axis=-1, keepdims=True), sink)
    e = jnp.exp(s - m)
    pr = e / (jnp.sum(e, axis=-1, keepdims=True) + jnp.exp(sink - m))
    o = jnp.einsum('bcgrqk,bckgd->bcqgrd', pr.astype(vb.dtype), vb)
    return rmsnorm(o.reshape(bsz, seq, SWA_HEADS * SWA_HEAD_DIM), out_norm)

def cross_attention(u, m, wq, wkv, wo):
    bsz, seq, _ = u.shape
    mlen = m.shape[1]
    q = (u @ wq).reshape(bsz, seq, X_HEADS, X_HEAD_DIM)
    kv = (m @ wkv).reshape(bsz, mlen, 2, X_HEADS, X_HEAD_DIM)
    k, v = kv[:, :, 0], kv[:, :, 1]
    s = jnp.einsum('bshd,bmhd->bhsm', q, k, preferred_element_type=jnp.float32) * X_HEAD_DIM ** -0.5
    p = jax.nn.softmax(s, axis=-1).astype(v.dtype)
    o = jnp.einsum('bhsm,bmhd->bshd', p, v).reshape(bsz, seq, X_HEADS * X_HEAD_DIM)
    return o @ wo

def conv_ffn(u, w_up, conv_w, conv_b, w_down):
    hdn = causal_dwconv(u @ w_up, conv_w, conv_b)
    g, val = jnp.split(hdn, 2, axis=-1)
    return (jax.nn.silu(g) * val) @ w_down

def setup_inputs(seed: int = 0) -> dict:
    key = jax.random.key(seed)
    ks = iter(jax.random.split(key, 48))
    L = DEPTH

    def nrm(shape, scale):
        return jax.random.normal(next(ks), shape, jnp.float32) * scale

    def gain(shape):
        return 1.0 + 0.02 * jax.random.normal(next(ks), shape, jnp.float32)

    x = nrm((BATCH, SEQ, D_MODEL), 1.0)
    mem = nrm((BATCH, MEM_LEN, D_MODEL), 1.0)
    positions = jnp.broadcast_to(jnp.arange(SEQ, dtype=jnp.int32), (BATCH, SEQ))
    dt0 = jnp.exp(jax.random.uniform(next(ks), (L, SSM_HEADS), jnp.float32,
                                     minval=math.log(1e-3), maxval=math.log(1e-1)))
    ssm_dt_bias = dt0 + jnp.log(-jnp.expm1(-dt0))
    ssm_a_log = jnp.log(jax.random.uniform(next(ks), (L, SSM_HEADS), jnp.float32, minval=1.0, maxval=16.0))
    return {
        "x": x,
        "mem": mem,
        "positions": positions,
        "norm_mix": gain((L, D_MODEL)),
        "w_in": nrm((L, D_MODEL, IN_COLS), D_MODEL ** -0.5),
        "mla_q_norm": gain((L, MLA_Q_RANK)),
        "mla_w_uq": nrm((L, MLA_Q_RANK, MLA_HEADS * (MLA_NOPE + MLA_ROPE)), MLA_Q_RANK ** -0.5),
        "mla_kv_norm": gain((L, MLA_KV_RANK)),
        "mla_w_ukv": nrm((L, MLA_KV_RANK, MLA_HEADS * (MLA_NOPE + MLA_V)), MLA_KV_RANK ** -0.5),
        "mla_out_norm": gain((L, MLA_HEADS * MLA_V)),
        "ssm_conv_w": nrm((L, SSM_CONV, SSM_CONV_DIM), SSM_CONV ** -0.5),
        "ssm_conv_b": nrm((L, SSM_CONV_DIM), 0.01),
        "ssm_dt_bias": ssm_dt_bias,
        "ssm_a_log": ssm_a_log,
        "ssm_d": 1.0 + 0.1 * jax.random.normal(next(ks), (L, SSM_HEADS), jnp.float32),
        "ssm_norm": gain((L, SSM_INNER)),
        "swa_sinks": nrm((L, SWA_HEADS), 0.5),
        "swa_out_norm": gain((L, SWA_HEADS * SWA_HEAD_DIM)),
        "w_out": nrm((L, OUT_COLS, D_MODEL), OUT_COLS ** -0.5),
        "norm_cross": gain((L, D_MODEL)),
        "norm_mem": gain((L, D_MODEL)),
        "cross_wq": nrm((L, D_MODEL, X_HEADS * X_HEAD_DIM), D_MODEL ** -0.5),
        "cross_wkv": nrm((L, D_MODEL, 2 * X_HEADS * X_HEAD_DIM), D_MODEL ** -0.5),
        "cross_wo": nrm((L, X_HEADS * X_HEAD_DIM, D_MODEL), (X_HEADS * X_HEAD_DIM) ** -0.5),
        "norm_ffn": gain((L, D_MODEL)),
        "ffn_w_up": nrm((L, D_MODEL, 2 * D_FF), D_MODEL ** -0.5),
        "ffn_conv_w": nrm((L, FFN_CONV, 2 * D_FF), FFN_CONV ** -0.5),
        "ffn_conv_b": nrm((L, 2 * D_FF), 0.01),
        "ffn_w_down": nrm((L, D_FF, D_MODEL), D_FF ** -0.5),
        "norm_final": gain((D_MODEL,)),
    }

def reference(x, mem, positions, norm_mix, w_in, mla_q_norm, mla_w_uq, mla_kv_norm, mla_w_ukv,
              mla_out_norm, ssm_conv_w, ssm_conv_b, ssm_dt_bias, ssm_a_log, ssm_d, ssm_norm,
              swa_sinks, swa_out_norm, w_out, norm_cross, norm_mem, cross_wq, cross_wkv, cross_wo,
              norm_ffn, ffn_w_up, ffn_conv_w, ffn_conv_b, ffn_w_down, norm_final):
    cos, sin = rope_tables(positions)
    h = x
    for l in range(DEPTH):
        u = rmsnorm(h, norm_mix[l])
        proj = u @ w_in[l]
        p_mla, p_ssm, p_swa = jnp.split(proj, [MLA_COLS, MLA_COLS + SSM_COLS], axis=-1)
        y_a = mla_mixer(p_mla, cos, sin, mla_q_norm[l], mla_w_uq[l], mla_kv_norm[l], mla_w_ukv[l], mla_out_norm[l])
        y_b = mamba2_mixer(p_ssm, ssm_conv_w[l], ssm_conv_b[l], ssm_dt_bias[l], ssm_a_log[l], ssm_d[l], ssm_norm[l])
        y_c = swa_mixer(p_swa, swa_sinks[l], swa_out_norm[l])
        h = h + jnp.concatenate([y_a, y_b, y_c], axis=-1) @ w_out[l]
        h = h + cross_attention(rmsnorm(h, norm_cross[l]), rmsnorm(mem, norm_mem[l]),
                                cross_wq[l], cross_wkv[l], cross_wo[l])
        h = h + conv_ffn(rmsnorm(h, norm_ffn[l]), ffn_w_up[l], ffn_conv_w[l], ffn_conv_b[l], ffn_w_down[l])
    return rmsnorm(h, norm_final)


_drawn_inputs = setup_inputs


def setup_inputs(seed=0):
    import zlib

    import numpy as np

    out = dict(_drawn_inputs(seed))
    spreads = {}
    factors = {'mla_q_norm': 6.245,
     'mla_kv_norm': 4.534,
     'mla_out_norm': 5.966,
     'ssm_conv_b': 8.0,
     'ssm_norm': 6.153,
     'swa_sinks': 8.0,
     'swa_out_norm': 7.263,
     'norm_cross': 8.0,
     'norm_mem': 8.0,
     'norm_ffn': 5.06,
     'ffn_conv_b': 23.747,
     'norm_final': 7.457}
    for name, (base, spread) in spreads.items():
        noise = np.random.default_rng([zlib.crc32(name.encode()), seed]).standard_normal(out[name].shape)
        drawn = base * np.exp(spread * noise) if base else spread * noise
        out[name] = jnp.asarray(drawn.astype(out[name].dtype))
    for name, factor in factors.items():
        out[name] = (out[name] * factor).astype(out[name].dtype)
    return out
```

```python
from contextlib import ExitStack

import numpy as np
import concourse.bass as bass
from concourse import mybir

F32, F32R, I32 = mybir.dt.float32, mybir.dt.float32r, mybir.dt.int32
ALU, ACT, AX = mybir.AluOpType, mybir.ActivationFunctionType, mybir.AxisListType

P = 128
T = 256
TT = T // P
D = 2048
KD = D // P
M = 256
EPS = 1e-6
NEG = -1e30
FF = 5632
FT = FF // P
RING = 3
CH = 2048

MLA_H, NOPE, ROPE, VD = 6, 128, 64, 128
SSM_H, SSM_P = 12, 64
SWA_H, SWA_D = 8, 64
X_H, X_D = 4, 128

COL_KR, COL_Z, COL_XBC, COL_DT, COL_Q = 768, 832, 1600, 2880, 2892

N_XK, N_XV, N_CQ, N_KRDT, N_XBC, N_QKV, N_U, N_Z, N_OUT, N_WQ, N_WO, N_FFN = 0, 4, 8, 14, 15, 25, 31, 35, 41, 57, 61, 65
GROUP = 12
GROUPS = FT // 4
LAST = N_FFN + GROUP * GROUPS

V_MIX, V_CROSS, V_MEM, V_FFN, V_CQ, V_CKV, V_MLA, V_SSM, V_SWA, V_CB = 0, 16, 32, 48, 64, 68, 70, 76, 82, 86
V_ROWS_A = 96
V_CW = V_ROWS_A
V_FW = V_CW + 40
V_FB = V_FW + 3 * 2 * FT
V_ALL = V_FB + 2 * FT

C_ID, C_ONE, C_MLA, C_SWA, C_CAUSAL, C_INV, C_SGN = 0, 128, 256, 640, 1024, 1408, 1409
C_ALL = 1410

A_SWA, A_MLA, A_X = 0, SWA_H, SWA_H + MLA_H


def constant_table():
    c = np.zeros((P, C_ALL), np.float32)
    c[:, C_ID:C_ID + P] = np.eye(P)
    c[:, C_ONE:C_ONE + P] = 1.0
    q = np.arange(P)
    for base, window in ((C_MLA, 99), (C_SWA, 2)):
        for t, (lo, nk) in enumerate(((0, P), (P, T))):
            qc, kc = (t * P + q)[:, None] // 64, np.arange(nk)[None, :] // 64
            c[:, base + lo:base + lo + nk] = np.where((kc <= qc) & (kc > qc - window), 0.0, NEG)
    j, i = q[:, None], np.arange(T)[None, :]
    c[:, C_CAUSAL:C_CAUSAL + T] = i >= j
    c[:, C_CAUSAL + T:C_CAUSAL + T + P] = i[:, :P] >= j
    freq = (np.float32(10000.0) ** (-np.arange(0, ROPE, 2, dtype=np.float32) / np.float32(ROPE))).astype(np.float32)
    c[:, C_INV] = np.tile(freq, 4)
    c[:, C_SGN] = np.where(q % 64 < 32, -1.0, 1.0)
    return c


def dmas_of(n):
    return {N_KRDT: 2, N_U: 4, N_U + 1: 8, N_U + 2: 6, N_U + 3: 2}.get(n, 1)


def landed(n):
    return 16 * sum(dmas_of(m) for m in range(n % RING, n + 1, RING))


def products(n):
    extra = {N_U: 3, N_U + 1: 3, N_U + 2: 6, N_U + 3: 1}
    return n + 1 + sum(v for m, v in extra.items() if m <= n)


class Signal:

    def __init__(self, sem):
        self.sem, self.n = sem, 0


class Engine:

    def __init__(self, eng):
        self.eng, self.last = eng, None

    def mark(self, ins, signal):
        ins.then_inc(signal.sem, 1)
        signal.n = signal.n + 1
        self.last = signal

    def settle(self):
        self.eng.wait_ge(self.last.sem, self.last.n)


def encoder(nc, x, mem, positions, norm_mix, w_in, mla_q_norm, mla_w_uq, mla_kv_norm, mla_w_ukv, mla_out_norm,
            ssm_conv_w, ssm_conv_b, ssm_dt_bias, ssm_a_log, ssm_d, ssm_norm, swa_sinks, swa_out_norm, w_out,
            norm_cross, norm_mem, cross_wq, cross_wkv, cross_wo, norm_ffn, ffn_w_up, ffn_conv_w, ffn_conv_b,
            ffn_w_down, norm_final, table, out):
    ctx = ExitStack()
    with ctx:
        def sb(name, shape, dt=F32):
            return ctx.enter_context(nc.sbuf_tensor(name, shape, dt))

        signals = {}

        def S(name):
            if name not in signals:
                signals[name] = Signal(ctx.enter_context(nc.semaphore(name)))
            return signals[name]

        raw = sb("raw", [P, RING, CH])
        hi = sb("hi", [P, RING, CH], F32R)
        lo = sb("lo", [P, RING, CH], F32R)
        uh = sb("uh", [P, KD, T], F32R)
        ul = sb("ul", [P, KD, T], F32R)
        ch = sb("ch", [P, 6, T], F32R)
        cl = sb("cl", [P, 6, T], F32R)
        tab = sb("tab", [P, C_ALL])
        vecs = sb("vecs", [P, V_ALL])
        small = sb("small", [P, 112])
        arena = sb("arena", [P, 20400])
        bank = [ctx.enter_context(nc.psum_tensor(f"bank{i}", [P, 512], F32)) for i in range(8)]

        ident, ones = tab[:, C_ID:C_ID + P], tab[:, C_ONE:C_ONE + P]

        def at(off, *shape):
            size = int(np.prod(shape))
            v = arena[:, off:off + size]
            if len(shape) == 2:
                v = v.rearrange("p (a b) -> p a b", b=shape[1])
            if len(shape) == 3:
                v = v.rearrange("p (a b c) -> p a b c", b=shape[1], c=shape[2])
            return v

        kxT = at(0, X_H, M)
        vx = at(1024, TT, 512)
        cosT, sinT = at(2048, T), at(2304, T)
        o_swa = at(2560, 4, T)
        dt_rows = at(2560, 4, T)
        acum = at(3584, T)
        krT = at(3840, T)
        convraw, convacc = at(4096, RING, T), at(4864, RING, T)
        o_mla = at(5632, MLA_H, T)
        sq1 = at(5632, 6 * T)
        cq_raw = at(7168, 6, T)
        yT = at(7168, 6, T)
        swa_q, swa_k, swa_v, swa_kswap = at(8704, 4, T), at(9728, T), at(9984, T), at(10240, T)
        zT = at(8704, 6, T)
        v_tok = at(10496, TT, P)
        ssb = at(10752, 2, 512)
        pts = at(11776, 2, 512)
        rtmp = at(12800, 3, T)
        xbcT = at(13568, 10, T)
        x_tok = at(16128, TT, 768)
        cbm = at(17664, 2, 384)
        dec = at(18432, 2, 384)
        qn = at(13568, MLA_H, T)
        kn = at(15104, MLA_H, T)
        vm = at(16640, TT, MLA_H * VD)
        qr = at(18176, 3, T)
        rot = at(18944, T)
        sq2 = at(13568, 6 * T)
        mems, xs, junk = at(2560, TT, D), at(6656, TT, D), at(10752, D)
        vrows = at(12800, 6, P)
        posi = at(13568, T)
        ang, kk, kl, tmp4 = at(13824, T), at(14080, T), at(14336, T), at(14592, T)
        hres = at(2048 + 14000, TT, D)
        hwork = at(6144, TT, D)
        hjunk = at(2048, D)
        q_x = at(4096, X_H, T)
        craw, cacc = at(10240, 4, T), at(11264, 4, T)
        sil, prod = at(12288, T), at(12544, T)
        gfin = at(13568, D)

        s_ss, s_var, s_std, s_r, s_t = 0, 2, 4, 6, 8
        s_dcol, s_sink, s_nsink = 10, 16, 24
        s_cols = 32
        s_dall = 96
        stat = sb("stat", [P, 2, 8])
        row12 = sb("row12", [SSM_H, 4])
        assert arena.shape[1] >= 18176 + 768 + 256

        block = ctx.enter_context(nc.Block())

        def tail(t):
            return {0: (0, P), 1: (P, T)}[t]

        @block.sync
        def _(sp):
            def row_tiles(v, n):
                return v.rearrange("l (r c) -> (l r) c", c=P)[0:n, :]

            def raw_free(n):
                sp.wait_ge(S("lo_ready").sem, n - RING + 1)

            def load(n, src, shape, slot=None, off=0):
                slot = n % RING if slot is None else slot
                size = int(np.prod(shape))
                dst = raw[:, slot, off:off + size]
                if len(shape) == 2:
                    dst = dst.rearrange("p (a b) -> p a b", b=shape[1])
                    sp.dma_start(dst, src).then_inc(S(f"raw_landed{slot}").sem, 16)
                else:
                    dst = dst.rearrange("p (a b c) -> p a b c", b=shape[1], c=shape[2])
                    sp.dma_start(dst, src).then_inc(S(f"raw_landed{slot}").sem, 16)

            def rows(w):
                return w[0].rearrange("(k p) c -> p k c", p=P)

            consts = S("consts_landed").sem
            for t in range(TT):
                sp.dma_start(mems[:, t, :], mem[0, t * P:(t + 1) * P, :]).then_inc(S("mem_landed").sem, 16)
            at_row = 0
            sp.dma_start(tab[:, :], table[:, :]).then_inc(consts, 16)
            for v, n in ((norm_mix, 16), (norm_cross, 16), (norm_mem, 16), (norm_ffn, 16), (mla_q_norm, 4),
                         (mla_kv_norm, 2), (mla_out_norm, 6), (ssm_norm, 6), (swa_out_norm, 4), (ssm_conv_b, 10)):
                sp.dma_start(vrows[at_row:at_row + n, 0, :], row_tiles(v, n)).then_inc(consts, 16)
                at_row += n
            load(0, rows(cross_wkv)[:, :, 0:P], (KD, P))
            load(1, rows(cross_wkv)[:, :, P:2 * P], (KD, P))
            load(2, rows(cross_wkv)[:, :, 2 * P:3 * P], (KD, P))
            sp.dma_start(vrows[0:40, 1, :], ssm_conv_w[0].rearrange("k (r c) -> (k r) c", c=P)).then_inc(consts, 16)
            for k in range(3):
                sp.dma_start(vrows[0:2 * FT, 2 + k, :], ffn_conv_w[0, k].rearrange("(r c) -> r c", c=P)).then_inc(consts, 16)
            sp.dma_start(vrows[0:2 * FT, 5, :], ffn_conv_b[0].rearrange("(r c) -> r c", c=P)).then_inc(consts, 16)
            for t in range(TT):
                sp.dma_start(xs[:, t, :], x[0, t * P:(t + 1) * P, :]).then_inc(S("x_landed").sem, 16)
            sp.dma_start(posi.bitcast(I32), positions[0].partition_broadcast(P)).then_inc(S("pos_landed").sem, 16)
            sp.dma_start(small[:, s_dall:s_dall + SSM_H], ssm_d[0].partition_broadcast(P)).then_inc(S("params_landed").sem, 16)
            sp.dma_start(small[:, s_sink:s_sink + SWA_H], swa_sinks[0].partition_broadcast(P)).then_inc(S("params_landed").sem, 16)
            sp.dma_start(row12[:, 0:1], ssm_dt_bias.rearrange("l h -> h l")).then_inc(S("params_landed").sem, 16)
            sp.dma_start(row12[:, 1:2], ssm_a_log.rearrange("l h -> h l")).then_inc(S("params_landed").sem, 16)

            raw_free(3)
            load(3, rows(cross_wkv)[:, :, 3 * P:4 * P], (KD, P))
            for g in range(4):
                raw_free(N_XV + g)
                load(N_XV + g, rows(cross_wkv)[:, 4 * g:4 * g + 4, 512:1024], (4, 512))

            def load_columns(first, count, w, col):
                v = rows(w)
                with sp.Fori(0, count // RING) as i:
                    for s in range(RING):
                        n = first + s
                        sp.wait_ge(S("lo_ready").sem, i * RING + (n - RING + 1))
                        load(n, v[:, :, bass.ds(i * (RING * P) + (col + s * P), P)], (KD, P))
                for s in range(count // RING * RING, count):
                    raw_free(first + s)
                    load(first + s, v[:, :, col + s * P:col + (s + 1) * P], (KD, P))

            load_columns(N_CQ, 6, w_in, 0)
            raw_free(N_KRDT)
            slot = raw[:, N_KRDT % RING, :].rearrange("p (k c) -> p k c", c=P)
            for lo_, hi_, col in ((0, ROPE, COL_KR), (ROPE, ROPE + SSM_H, COL_DT)):
                sp.dma_start(slot[:, :, lo_:hi_], rows(w_in)[:, :, col:col + hi_ - lo_]).then_inc(
                    S(f"raw_landed{N_KRDT % RING}").sem, 16)
            load_columns(N_XBC, 10, w_in, COL_XBC)
            load_columns(N_QKV, 6, w_in, COL_Q)
            uq = mla_w_uq[0].rearrange("(k p) (h e) -> p k h e", p=P, e=NOPE + ROPE)
            ukv = mla_w_ukv[0].rearrange("(k p) (h e) -> p k h e", p=P, e=NOPE + VD)

            def load4(n, parts):
                raw_free(n)
                off = 0
                for src, k, h, e in parts:
                    dst = raw[:, n % RING, off:off + k * h * e].rearrange("p (k h e) -> p k h e", h=h, e=e)
                    for kt in range(k):
                        sp.dma_start(dst[:, kt], src[:, kt]).then_inc(S(f"raw_landed{n % RING}").sem, 16)
                    off += k * h * e

            load4(N_U, [(uq[:, :, 0:4, 0:NOPE], 4, 4, NOPE)])
            load4(N_U + 1, [(uq[:, :, 4:6, 0:NOPE], 4, 2, NOPE), (uq[:, :, 0:4, NOPE:], 4, 4, ROPE)])
            load4(N_U + 2, [(uq[:, :, 4:6, NOPE:], 4, 2, ROPE), (ukv[:, :, :, 0:NOPE], 2, 6, NOPE)])
            load4(N_U + 3, [(ukv[:, :, :, NOPE:], 2, 6, VD)])
            load_columns(N_Z, 6, w_in, COL_Z)
            n = N_OUT
            for g in OUT_ORDER:
                for cb in range(4):
                    raw_free(n)
                    load(n, rows(w_out)[:, 4 * g:4 * g + 4, cb * 512:(cb + 1) * 512], (4, 512))
                    n += 1
            sp.wait_ge(S("probsT_done").sem, A_X)
            sp.wait_ge(S("out_done").sem, A_X)
            for t in range(TT):
                sp.dma_start(hres[:, t, :], x[0, t * P:(t + 1) * P, :]).then_inc(S("residual_landed").sem, 16)
            for h in range(X_H):
                raw_free(N_WQ + h)
                load(N_WQ + h, rows(cross_wq)[:, :, h * P:(h + 1) * P], (KD, P))
            for cb in range(4):
                raw_free(N_WO + cb)
                load(N_WO + cb, rows(cross_wo)[:, :, cb * 512:(cb + 1) * 512], (4, 512))
            sp.wait_ge(S("mix_added").sem, 8)
            sp.dma_start(gfin[:, :], norm_final.partition_broadcast(P)).then_inc(S("gfin_landed").sem, 16)
            with sp.Fori(0, GROUPS) as i:
                for c in range(GROUP):
                    n = N_FFN + c
                    sp.wait_ge(S("lo_ready").sem, i * GROUP + (n - RING + 1))
                    if c < 8:
                        col = (c % 2) * FF + (c // 2) * P
                        load(n, rows(ffn_w_up)[:, :, bass.ds(i * (4 * P) + col, P)], (KD, P))
                    else:
                        cb = c - 8
                        load(n, rows(ffn_w_down)[:, bass.ds(i * 4, 4), cb * 512:(cb + 1) * 512], (4, 512))
            for t in range(TT):
                sp.wait_ge(S("out_ready").sem, t + 1)
                sp.dma_start(out[0, t * P:(t + 1) * P, :], hwork[:, t, :]).then_inc(S("out_stored").sem, 16)
            sp.wait_ge(S("out_stored").sem, 16 * TT)

        def landed_at(n, i, per):
            return landed(n) if i is None else i * (16 * per // RING) + landed(n)

        @block.scalar
        def _(act):
            a = Engine(act)

            def split(n, i=None, per=GROUP):
                act.wait_ge(S(f"raw_landed{n % RING}").sem, landed_at(n, i, per))
                if i is not None or n >= RING:
                    before = products(n - RING)
                    act.wait_ge(S("products_done").sem, before if i is None else i * per + before)
                a.mark(act.copy(hi[:, n % RING, :], raw[:, n % RING, :]), S("hi_ready"))

            def token_norm(name, src, dst, g_col, ready, groups=True):
                ready()
                for t in range(TT):
                    a.mark(act.activation(dst, src[:, t, :], ACT.Square, accum_out=small[:, s_ss + t:s_ss + t + 1]),
                           S(f"{name}_ss"))
                    a.settle()
                act.wait_ge(S(f"{name}_var").sem, 1)
                a.mark(act.activation(small[:, s_std:s_std + 2], small[:, s_var:s_var + 2], ACT.Sqrt), S(f"{name}_std"))

            def token_hi(name, g, g_col, b):
                act.wait_ge(S(f"{name}_turned").sem, g + 1)
                for k in (2 * g, 2 * g + 1):
                    a.mark(act.activation(uh[:, k, :], bank[b][:, (k % 2) * T:(k % 2 + 1) * T], ACT.Copy,
                                          scale=vecs[:, g_col + k:g_col + k + 1]), S(f"{name}_hi"))

            def feature_norm(name, src, n, dst_h, g_col, sq, free=None):
                a.mark(act.activation(sq[:, 0:n * T], src, ACT.Square), S(f"{name}_sq"))
                act.wait_ge(S(f"{name}_var").sem, 1)
                a.mark(act.activation(rtmp[:, 1, :], rtmp[:, 0, :], ACT.Sqrt), S(f"{name}_std"))

            def feature_hi(name, src, n, dst_h, g_col):
                act.wait_ge(S(f"{name}_scaled").sem, 1)
                for k in range(n):
                    a.mark(act.activation(dst_h[:, k, :], src[:, k, :], ACT.Copy,
                                          scale=vecs[:, g_col + k:g_col + k + 1]), S(f"{name}_hi"))

            def take(b_index, dst, func=ACT.Copy, done=None, rows_=(0, P), cols=T, i=None, per=0):
                r0, r1 = rows_
                return act.activation(dst, bank[b_index % 3][r0:r1, 0:cols], func)

            def attend_exp(j):
                act.wait_ge(S("negmax_ready").sem, j + 1)
                s = stat[:, j % 2, :]
                for t in range(TT):
                    if j < A_MLA:
                        act.activation(s[:, 4 + t:5 + t], small[:, s_sink + j:s_sink + j + 1], ACT.Exp, bias=s[:, t:t + 1])
                for t in range(TT):
                    c0, c1 = span(j, t)
                    ins = act.activation(ssb[:, j % 2, c0:c1], ssb[:, j % 2, c0:c1], ACT.Exp,
                                         bias=s[:, t:t + 1], accum_out=s[:, 2 + t:3 + t])
                a.mark(ins, S("exp_done"))

            def attend_turn(j):
                act.wait_ge(S("probsT_done").sem, j + 1)
                if j >= 2:
                    act.wait_ge(S("out_done").sem, j - 1)
                w = 512 if j >= A_X else 384
                a.mark(act.copy(pts[:, j % 2, 0:w], bank[5 + j % 2][:, 0:w]), S("probsT_copied"))

            def attend_out(j):
                act.wait_ge(S("out_done").sem, j + 1)
                if j < A_MLA:
                    r = 64 * (j % 2)
                    ins = act.copy(o_swa[r:r + 64, j // 2, :], bank[7][r:r + 64, 0:T])
                elif j < A_X:
                    ins = act.copy(o_mla[:, j - A_MLA, :], bank[7][:, 0:T])
                else:
                    ins = act.copy(ch[:, j - A_X, :], bank[7][:, 0:T])
                a.mark(ins, S("out_copied"))

            def attend(steps):
                for j in steps:
                    attend_exp(j)
                    if j - 1 >= steps_first(j):
                        attend_turn(j - 1)
                        attend_out(j - 1)

            def attend_flush(j):
                attend_turn(j)
                attend_out(j)

            def wait_product(n, i=None, per=0):
                v = products(n)
                act.wait_ge(S("products_done").sem, v if i is None else i * per + v)

            split(0)
            token_norm("mem", mems, junk, V_MEM, lambda: act.wait_ge(S("mem_landed").sem, 32))
            split(1)
            act.wait_ge(S("vecs_turned").sem, 1)
            a.mark(act.copy(vecs[:, :], bank[7][:, 0:V_ALL]), S("vecs_ready"))
            a.settle()
            for g in range(8):
                token_hi("mem", g, V_MEM, MEM_BANKS[g])
            token_norm("x", xs, junk, V_MIX, lambda: act.wait_ge(S("x_landed").sem, 32))
            for f in range(2):
                act.wait_ge(S("angles_ready").sem, f + 1)
                a.mark(act.activation((sinT, cosT)[f], (kk, kl)[f], ACT.Sin), S("sincos"))
            for n in range(N_XK, N_XK + 4):
                split(n + 2)
                wait_product(n)
                a.mark(act.copy(kxT[:, n, :], bank[n % 3][:, 0:T]), S("tile_taken"))
            for n in range(N_XV, N_XV + 4):
                if n > N_XV:
                    for g in (2 * (n - N_XV) - 2, 2 * (n - N_XV) - 1):
                        act.wait_ge(S("products_done").sem, products(n - 1))
                        token_hi("x", g, V_MIX, X_BANKS[g])
                split(n + 2)
            act.wait_ge(S("products_done").sem, products(N_XV + 3))
            for g in (6, 7):
                token_hi("x", g, V_MIX, X_BANKS[g])

            def in_loop(signals_, per, turns, body):
                start = {s: s.n for s in signals_}
                with act.Fori(0, turns) as i:
                    for s in signals_:
                        s.n = i * signals_[s] + start[s]
                    body(i)
                for s in signals_:
                    s.n = start[s] + signals_[s] * turns

            for n in range(N_CQ, N_CQ + 6):
                split(n + 2)
                wait_product(n)
                a.mark(act.copy(cq_raw[:, n - N_CQ, :], bank[n % 3][:, 0:T]), S("tile_taken"))
            split(N_KRDT + 2)
            wait_product(N_KRDT)
            b = bank[N_KRDT % 3]
            a.mark(act.copy(krT[0:64, :], b[0:64, 0:T]), S("kr_parts"))
            a.mark(act.copy(krT[64:128, :], b[0:64, 0:T]), S("kr_parts"))
            a.mark(act.copy(dt_rows[0:SSM_H, 0, :], b[64:64 + SSM_H, 0:T]), S("tile_taken"))

            def conv_first(n, i=None):
                c = n - N_XBC
                wait_product(n, i, 3)
                s = n % RING
                col = (V_CW + 30 + c, V_CB + c) if i is None else (i * 3 + (V_CW + 30 + c), i * 3 + (V_CB + c))
                a.mark(act.activation(convacc[:, s, :], bank[n % 3][:, 0:T], ACT.Identity,
                                      scale=vecs[:, bass.ds(col[0], 1)], bias=vecs[:, bass.ds(col[1], 1)]), S("conv_first"))
                a.mark(act.copy(convraw[:, s, :], bank[n % 3][:, 0:T]), S("tile_taken"))

            def conv_silu(n, i=None):
                c = n - N_XBC
                act.wait_ge(S("conv_done").sem, c + 1 if i is None else i * 3 + c + 1)
                dst = xbcT[:, c, :].unsqueeze(1) if i is None else xbcT[:, bass.ds(i * 3 + c, 1), :]
                a.mark(act.activation(dst, convacc[:, n % RING, :].unsqueeze(1), ACT.Silu), S("xbc_ready"))

            def body(i):
                for s in range(3):
                    split(N_XBC + s + 2, i, 3)
                    conv_first(N_XBC + s, i)
                    conv_silu(N_XBC + s, i)
            in_loop({S("hi_ready"): 3, S("tile_taken"): 3, S("conv_first"): 3, S("xbc_ready"): 3}, 3, 3, body)
            split(N_XBC + 9 + 2)
            feature_norm("cq", cq_raw[:, 0:4, :].rearrange("p a b -> p (a b)"), 4, ch, V_CQ, sq1)
            feature_hi("cq", cq_raw, 4, ch, V_CQ)
            a.settle()
            act.wait_ge(S("cq_ss").sem, 1)
            feature_norm("ckv", cq_raw[:, 4:6, :].rearrange("p a b -> p (a b)"), 2, ch, V_CKV, sq1)
            feature_hi("ckv", cq_raw[:, 4:6, :], 2, ch[:, 4:6, :], V_CKV)
            conv_first(N_XBC + 9)
            conv_silu(N_XBC + 9)

            def take_qkv(n):
                wait_product(n)
                src = bank[n % 3]
                k = n - N_QKV
                if k < 4:
                    a.mark(act.copy(swa_q[:, k, :], src[:, 0:T]), S("tile_taken"))
                elif k == 4:
                    a.mark(act.copy(swa_kswap[0:64, :], src[64:128, 0:T]), S("kr_parts"))
                    a.mark(act.copy(swa_kswap[64:128, :], src[0:64, 0:T]), S("kr_parts"))
                    a.mark(act.copy(swa_k[:, :], src[:, 0:T]), S("tile_taken"))
                else:
                    a.mark(act.copy(swa_v[:, :], src[:, 0:T]), S("tile_taken"))

            split(N_QKV + 2)
            act.wait_ge(S("dt_abs").sem, 1)
            a.mark(act.activation(dt_rows[0:SSM_H, 2, :], dt_rows[0:SSM_H, 2, :], ACT.Exp), S("dt_exp"))
            a.mark(act.activation(row12[:, 2:3], row12[:, 1:2], ACT.Exp), S("a_exp"))
            act.wait_ge(S("dt_w").sem, 1)
            a.mark(act.activation(dt_rows[0:SSM_H, 3, :], dt_rows[0:SSM_H, 3, :], ACT.Ln), S("dt_ln"))
            for b in range(3):
                act.wait_ge(S("xbc_turned").sem, b + 1)
                for k in range(2):
                    a.mark(act.copy(x_tok[:, :, (2 * b + k) * P:(2 * b + k + 1) * P],
                                    bank[3 + b][:, k * T:(k + 1) * T].rearrange("p (t c) -> p t c", c=P)), S("x_tok_ready"))
            take_qkv(N_QKV)
            split(N_QKV + 3)
            take_qkv(N_QKV + 1)
            for n in range(N_QKV + 2, N_QKV + 6):
                split(n + 2)
                for h in range(3 * (n - N_QKV - 2), 3 * (n - N_QKV - 2) + 3):
                    act.wait_ge(S("seg_ready").sem, h + 1)
                    a.mark(act.activation(dec[:, h % 2, :], dec[:, h % 2, :], ACT.Exp), S("decay_ready"))
                take_qkv(n)

            def take_u(n):
                first = products(n - 1)
                k = n - N_U
                dsts = {0: [qn[:, h, :] for h in range(4)], 1: [qn[:, 4, :], qn[:, 5, :], qr[:, 0, :], qr[:, 1, :]],
                        2: [qr[:, 2, :]] + [kn[:, h, :] for h in range(6)]}[k]
                act.wait_ge(S("y_taken").sem, 6)
                for m, dst in enumerate(dsts):
                    act.wait_ge(S("products_done").sem, first + m + 1)
                    a.mark(act.copy(dst, bank[(first + m) % 3][:, 0:T]), S("tile_taken"))

            for n in range(N_U, N_U + 4):
                split(n + 2)
                attend([2 * (n - N_U), 2 * (n - N_U) + 1])
                if n == N_U + 3:
                    attend_flush(A_MLA - 1)
                if n < N_U + 3:
                    take_u(n)
            for n in range(N_Z, N_Z + 6):
                split(n + 2)
                attend([A_MLA + n - N_Z])
                wait_product(n)
                a.mark(act.activation(zT[:, n - N_Z, :], bank[z_bank(n)][:, 0:T], ACT.Silu), S("tile_taken"))
            attend_flush(A_X - 1)
            for name, src, n_, g_col, k0 in MIX_NORMS(o_swa, yT, o_mla):
                if name == "ssm":
                    act.wait_ge(S("y_gated").sem, 6)
                else:
                    a.settle()
                feature_norm(name, src.rearrange("p a b -> p (a b)"), n_, None, g_col, sq2)
                act.wait_ge(S("products_done").sem, products(N_Z + 5))
                feature_hi(name, src, n_, uh[:, k0:k0 + n_, :], g_col)
                act.wait_ge(S(f"{name}_ss").sem, 1)
            for n in range(N_OUT, N_OUT + 16):
                split(n + 2)
            token_norm("hx", hres, hjunk, V_CROSS, lambda: act.wait_ge(S("mix_added").sem, 8))
            for g in range(8):
                token_hi("hx", g, V_CROSS, g)
            for n in range(N_WQ, N_WQ + 4):
                split(n + 2)
                wait_product(n)
                a.mark(act.copy(q_x[:, n - N_WQ, :], bank[n % 3][:, 0:T]), S("tile_taken"))
            attend(range(A_X, A_X + 4))
            attend_flush(A_X + 3)
            for n in range(N_WO, N_WO + 4):
                split(n + 2)
            token_norm("hf", hres, hjunk, V_FFN, lambda: act.wait_ge(S("cross_added").sem, 8))
            for g in range(8):
                token_hi("hf", g, V_FFN, g)

            def ffn_group(i, last=False):
                def at_turn(v, per):
                    return i * per + v
                for c in range(GROUP):
                    n = N_FFN + c
                    if not (last and c >= GROUP - 2):
                        split(n + 2, i, GROUP)
                    if c < 8:
                        s, v, k = c % 4, c % 2, c // 2
                        act.wait_ge(S("products_done").sem, at_turn(products(n), GROUP))
                        act.wait_ge(S("prod_ready").sem, at_turn(k + 3, 4))
                        tile = at_turn(v * FT + k, 4)
                        a.mark(act.activation(cacc[:, s, :], bank[c % 2][:, 0:T], ACT.Identity,
                                              scale=vecs[:, bass.ds(tile + (V_FW + 2 * 2 * FT), 1)],
                                              bias=vecs[:, bass.ds(tile + V_FB, 1)]), S("fconv_first"))
                        a.mark(act.copy(craw[:, s, :], bank[c % 2][:, 0:T]), S("fconv_raw"))
                        if v == 1:
                            act.wait_ge(S("fconv_done").sem, at_turn(2 * k + 1, 8))
                            a.mark(act.activation(sil[:, :], cacc[:, s - 1, :], ACT.Silu), S("silu_ready"))
                    if c in (2, 4, 6, 8):
                        k = c // 2 - 1
                        act.wait_ge(S("prod_ready").sem, at_turn(k + 1 + 4, 4))
                        a.mark(act.copy(ch[:, k, :], prod[:, :]), S("gated_hi"))
            act.sem_inc(S("fconv_raw").sem, 2)
            with act.Fori(0, GROUPS - 1) as i:
                ffn_group(i)
            ffn_group(GROUPS - 1, True)
            for t in range(TT):
                act.wait_ge(S("ffn_added").sem, 8 * GROUPS)
                a.mark(act.activation(hjunk, hres[:, t, :], ACT.Square, accum_out=small[:, s_ss + t:s_ss + t + 1]), S("final_ss"))
                act.wait_ge(S("final_ss").sem, t + 1)
            act.wait_ge(S("final_var").sem, 1)
            a.mark(act.activation(small[:, s_std:s_std + 2], small[:, s_var:s_var + 2], ACT.Sqrt), S("final_std"))

        @block.vector
        def _(dve):
            d = Engine(dve)
            step = S("vector_step")

            def go(ins, signal=None):
                d.mark(ins, signal or step)
                d.settle()

            def split(n, i=None, per=GROUP):
                v = n + 1
                dve.wait_ge(S("hi_ready").sem, v if i is None else i * per + v)
                if i is not None or n >= RING:
                    before = products(n - RING)
                    dve.wait_ge(S("products_done").sem, before if i is None else i * per + before)
                d.mark(dve.tensor_tensor(lo[:, n % RING, :], raw[:, n % RING, :], hi[:, n % RING, :].bitcast(F32), ALU.subtract),
                       S("lo_ready"))

            def newton(r, v, t):
                go(dve.tensor_tensor(t, r, r, ALU.mult))
                go(dve.tensor_tensor(t, t, v, ALU.mult))
                go(dve.tensor_scalar(t, t, -0.5, 1.5, ALU.mult, ALU.add))
                go(dve.tensor_tensor(r, r, t, ALU.mult))

            def token_scale(name, src, dst):
                v, sd = small[:, s_var:s_var + 2], small[:, s_std:s_std + 2]
                r, t_ = small[:, s_r:s_r + 2], small[:, s_t:s_t + 2]
                dve.wait_ge(S(f"{name}_ss").sem, TT)
                go(dve.tensor_scalar(v, small[:, s_ss:s_ss + 2], 1.0 / D, EPS, ALU.mult, ALU.add), S(f"{name}_var"))
                dve.wait_ge(S(f"{name}_std").sem, 1)
                go(dve.reciprocal(r, sd))
                newton(r, v, t_)
                if dst is not None:
                    for t in range(TT):
                        d.mark(dve.tensor_scalar(dst[:, t, :], src[:, t, :], small[:, s_r + t:s_r + t + 1], None, ALU.mult),
                               S(f"{name}_scaled"))

            def token_lo(name, g, g_col, b):
                dve.wait_ge(S(f"{name}_hi").sem, 2 * g + 2)
                for k in (2 * g, 2 * g + 1):
                    d.mark(dve.scalar_tensor_tensor(out=ul[:, k, :], in0=bank[b][:, (k % 2) * T:(k % 2 + 1) * T],
                                                    scalar=vecs[:, g_col + k:g_col + k + 1], in1=uh[:, k, :].bitcast(F32),
                                                    op0=ALU.mult, op1=ALU.subtract), S(f"{name}_lo"))

            def feature_scale(name, src, n, dim):
                dve.wait_ge(S(f"{name}_ss").sem, 1)
                go(dve.tensor_scalar(rtmp[:, 0, :], bank[7][:, 0:T], 1.0 / dim, EPS, ALU.mult, ALU.add), S(f"{name}_var"))
                dve.wait_ge(S(f"{name}_std").sem, 1)
                go(dve.reciprocal(rtmp[:, 1, :], rtmp[:, 1, :]))
                newton(rtmp[:, 1, :], rtmp[:, 0, :], rtmp[:, 2, :])
                go(dve.tensor_tensor(src, src, rtmp[:, 1, :].unsqueeze(1).to_broadcast([P, n, T]), ALU.mult), S(f"{name}_scaled"))

            def feature_lo(name, src, n, dst_h, dst_l, g_col):
                dve.wait_ge(S(f"{name}_hi").sem, n)
                for k in range(n):
                    d.mark(dve.scalar_tensor_tensor(out=dst_l[:, k, :], in0=src[:, k, :], scalar=vecs[:, g_col + k:g_col + k + 1],
                                                    in1=dst_h[:, k, :].bitcast(F32), op0=ALU.mult, op1=ALU.subtract), S(f"{name}_lo"))

            def attend(j):
                b, s, st = bank[3 + j % 2], ssb[:, j % 2, :], stat[:, j % 2, :]
                w = 512 if j >= A_X else 384
                dve.wait_ge(S("scores_done").sem, j + 1)
                if j >= 2:
                    dve.wait_ge(S("probsT_done").sem, j - 1)
                if j < A_X:
                    col, scale = (C_SWA, SWA_D ** -0.5) if j < A_MLA else (C_MLA, (NOPE + ROPE) ** -0.5)
                    go(dve.scalar_tensor_tensor(out=s[:, 0:w], in0=b[:, 0:w], scalar=scale, in1=tab[:, col:col + w],
                                                op0=ALU.mult, op1=ALU.add), S("scores_taken"))
                else:
                    go(dve.tensor_scalar(s[:, 0:w], b[:, 0:w], X_D ** -0.5, None, ALU.mult), S("scores_taken"))
                for t in range(TT):
                    c0, c1 = span(j, t)
                    ins = dve.tensor_reduce(st[:, t:t + 1], s[:, c0:c1], AX.X, ALU.max, negate=True)
                    if j >= A_MLA and t == 1:
                        go(ins, S("negmax_ready"))
                    else:
                        go(ins)
                if j < A_MLA:
                    go(dve.tensor_scalar(st[:, 0:2], st[:, 0:2], small[:, s_nsink + j:s_nsink + j + 1], None, ALU.min), S("negmax_ready"))
                dve.wait_ge(S("exp_done").sem, j + 1)
                if j < A_MLA:
                    go(dve.tensor_tensor(st[:, 2:4], st[:, 2:4], st[:, 4:6], ALU.add))
                go(dve.reciprocal(st[:, 6:8], st[:, 2:4]))
                for t in range(TT):
                    c0, c1 = span(j, t)
                    ins = dve.tensor_scalar(s[:, c0:c1], s[:, c0:c1], st[:, 6 + t:7 + t], None, ALU.mult)
                    go(ins, S("probs_ready") if t == 1 else None)

            token_scale("mem", mems, mems)
            split(0)
            split(1)
            dve.wait_ge(S("vecs_ready").sem, 1)
            for g in range(8):
                token_lo("mem", g, V_MEM, MEM_BANKS[g])
            token_scale("x", xs, xs)
            dve.wait_ge(S("pos_landed").sem, 16)
            dve.wait_ge(S("consts_landed").sem, N_CONSTS)
            go(dve.tensor_copy(ang, posi.bitcast(I32)))
            go(dve.tensor_scalar(ang, ang, tab[:, C_INV:C_INV + 1], None, ALU.mult))
            magic = 1.5 * 2.0 ** 23
            go(dve.tensor_scalar(kk, ang, float(1 / (2 * np.pi)), magic, ALU.mult, ALU.add))
            go(dve.tensor_scalar(kk, kk, -magic, None, ALU.add))
            go(dve.tensor_scalar(kl, kk, magic * 2.0 ** 12, None, ALU.add))
            go(dve.tensor_scalar(kl, kl, -magic * 2.0 ** 12, None, ALU.add))
            go(dve.tensor_tensor(kk, kk, kl, ALU.subtract))
            rest = 2 * np.pi
            for _ in range(4):
                e = 2.0 ** (np.floor(np.log2(rest)) - 10)
                part = float(np.floor(rest / e) * e)
                rest -= part
                go(dve.scalar_tensor_tensor(out=ang, in0=kl, scalar=-part, in1=ang, op0=ALU.mult, op1=ALU.add))
                go(dve.scalar_tensor_tensor(out=ang, in0=kk, scalar=-part, in1=ang, op0=ALU.mult, op1=ALU.add))
            lim = 3.1415925
            go(dve.tensor_scalar(kk, ang, lim, -lim, ALU.min, ALU.max), S("angles_ready"))
            go(dve.tensor_scalar(tmp4, ang, float(np.pi / 2), float(-2 * np.pi), ALU.is_gt, ALU.mult))
            go(dve.scalar_tensor_tensor(out=kl, in0=ang, scalar=float(np.pi / 2), in1=tmp4, op0=ALU.add, op1=ALU.add))
            go(dve.tensor_scalar(kl, kl, lim, -lim, ALU.min, ALU.max), S("angles_ready"))
            for n in range(N_XK, N_XK + 4):
                split(n + 2)
            dve.wait_ge(S("sincos").sem, 1)
            go(dve.tensor_scalar(sinT, sinT, tab[:, C_SGN:C_SGN + 1], None, ALU.mult))
            for n in range(N_XV, N_XV + 4):
                if n > N_XV:
                    for g in (2 * (n - N_XV) - 2, 2 * (n - N_XV) - 1):
                        dve.wait_ge(S("products_done").sem, products(n - 1))
                        token_lo("x", g, V_MIX, X_BANKS[g])
                split(n + 2)
            dve.wait_ge(S("products_done").sem, products(N_XV + 3))
            for g in (6, 7):
                token_lo("x", g, V_MIX, X_BANKS[g])
            for t in range(TT):
                d.mark(dve.tensor_copy(vx[:, t, :], bank[4 + t][:, :]), S("vx_ready"))
            dve.wait_ge(S("params_landed").sem, 16 * 4)
            for half in range(2):
                rows_ = slice(64 * half, 64 * half + 64)
                go(dve.tensor_copy(small[rows_, s_dcol:s_dcol + 6],
                                   small[rows_, s_dall:s_dall + SSM_H].rearrange("p (t s) -> p t s", s=2)[:, :, half]))
            go(dve.tensor_scalar(small[:, s_nsink:s_nsink + SWA_H], small[:, s_sink:s_sink + SWA_H], -1.0, None, ALU.mult))

            def in_loop(signals_, turns, body):
                start = {s: s.n for s in signals_}
                with dve.Fori(0, turns) as i:
                    for s in signals_:
                        s.n = i * signals_[s] + start[s]
                    body(i)
                for s in signals_:
                    s.n = start[s] + signals_[s] * turns

            for n in range(N_CQ, N_CQ + 6):
                split(n + 2)
            split(N_KRDT + 2)

            def conv_rest(n, i=None):
                c = n - N_XBC
                dve.wait_ge(S("tile_taken").sem, TAKEN_XBC + c + 1 if i is None else i * 3 + (TAKEN_XBC + c + 1))
                s = n % RING
                for k in (1, 2, 3):
                    col = V_CW + 10 * (3 - k) + c if i is None else i * 3 + (V_CW + 10 * (3 - k) + c)
                    go(dve.scalar_tensor_tensor(out=convacc[:, s, k:T], in0=convraw[:, s, 0:T - k], scalar=vecs[:, bass.ds(col, 1)],
                                                in1=convacc[:, s, k:T], op0=ALU.mult, op1=ALU.add),
                       S("conv_done") if k == 3 else None)

            def body(i):
                for s in range(3):
                    split(N_XBC + s + 2, i, 3)
                    conv_rest(N_XBC + s, i)
            in_loop({S("lo_ready"): 3, S("conv_done"): 3, step: 6}, 3, body)
            split(N_XBC + 11)
            feature_scale("cq", cq_raw[:, 0:4, :], 4, 512)
            feature_lo("cq", cq_raw, 4, ch, cl, V_CQ)
            feature_scale("ckv", cq_raw[:, 4:6, :], 2, 256)
            feature_lo("ckv", cq_raw[:, 4:6, :], 2, ch[:, 4:6, :], cl[:, 4:6, :], V_CKV)
            conv_rest(N_XBC + 9)
            split(N_QKV + 2)
            H = slice(0, SSM_H)
            r0, r1, r2, r3 = (dt_rows[H, k, :] for k in range(4))
            dve.wait_ge(S("tile_taken").sem, TAKEN_XBC)
            go(dve.tensor_scalar(r0, r0, row12[:, 0:1], None, ALU.add))
            go(dve.tensor_scalar(r2, r0, -1.0, None, ALU.mult))
            go(dve.tensor_tensor(r2, r2, r0, ALU.min), S("dt_abs"))
            go(dve.tensor_scalar(r0, r0, 0.0, None, ALU.max))
            dve.wait_ge(S("dt_exp").sem, 1)
            go(dve.tensor_scalar(r3, r2, 1.0, None, ALU.add))
            go(dve.tensor_scalar(r1, r3, -1.0, None, ALU.add), S("dt_w"))
            go(dve.tensor_scalar(acum[H, :], r1, 0.0, None, ALU.is_equal))
            go(dve.tensor_tensor(r1, r1, acum[H, :], ALU.add))
            go(dve.reciprocal(r1, r1))
            dve.wait_ge(S("dt_ln").sem, 1)
            go(dve.tensor_tensor(r3, r3, acum[H, :], ALU.add))
            go(dve.tensor_tensor(r3, r3, r1, ALU.mult))
            go(dve.tensor_tensor(r3, r3, r2, ALU.mult))
            go(dve.tensor_tensor(r0, r0, r3, ALU.add))
            dve.wait_ge(S("a_exp").sem, 1)
            go(dve.tensor_scalar(r1, r0, row12[:, 2:3], -1.0, ALU.mult, ALU.mult))
            for t in range(TT):
                go(dve.tensor_tensor_scan(acum[H, t * P:(t + 1) * P], tab[H, C_ONE:C_ONE + P], r1[:, t * P:(t + 1) * P], 0.0,
                                          ALU.mult, ALU.add))
            go(dve.tensor_scalar(r2, acum[H, :], -1.0, None, ALU.mult))
            go(dve.tensor_scalar(r3[:, 0:P], r2[:, 0:P], acum[H, P - 1:P], None, ALU.add), S("dt_rows_ready"))
            split(N_QKV + 3)
            dve.wait_ge(S("dt_turned").sem, 1)
            go(dve.tensor_copy(small[:, s_cols:s_cols + 60], bank[6][:, 0:60]), S("dt_cols_ready"))
            for g in range(2):
                dve.wait_ge(S("cb_done").sem, g + 1)
                go(dve.tensor_tensor(cbm[:, g, :], bank[3 + g][:, 0:384], tab[:, C_CAUSAL:C_CAUSAL + 384], ALU.mult), S("cb_masked"))

            def ssd_head(h):
                dt0, dt1, na0, na1, ea0 = (small[:, s_cols + 12 * k + h:s_cols + 12 * k + h + 1] for k in range(5))
                b, e = bank[3 + h % 2], dec[:, h % 2, :]
                dve.wait_ge(S("acum_spread").sem, h + 1)
                if h >= 2:
                    dve.wait_ge(S("ssd_used").sem, h - 1)
                d.mark(dve.tensor_scalar(e[:, 0:P], b[:, 0:P], na0, 0.0, ALU.add, ALU.min), step)
                d.mark(dve.tensor_scalar(e[:, P:T], b[:, P:T], ea0, 0.0, ALU.add, ALU.min), step)
                d.mark(dve.tensor_scalar(e[:, T:T + P], b[:, P:T], na1, 0.0, ALU.add, ALU.min), S("seg_ready"))
                dve.wait_ge(S("decay_ready").sem, h + 1)
                g = h // 6
                d.mark(dve.scalar_tensor_tensor(out=e[:, 0:T], in0=e[:, 0:T], scalar=dt0, in1=cbm[:, g, 0:T],
                                                op0=ALU.mult, op1=ALU.mult), step)
                d.mark(dve.scalar_tensor_tensor(out=e[:, T:T + P], in0=e[:, T:T + P], scalar=dt1, in1=cbm[:, g, T:T + P],
                                                op0=ALU.mult, op1=ALU.mult), S("ssd_weights"))

            def take_y(pair):
                dve.wait_ge(S("ssd_used").sem, 2 * pair + 2)
                go(dve.scalar_tensor_tensor(out=yT[:, pair, :], in0=xbcT[:, pair, :], scalar=small[:, s_dcol + pair:s_dcol + pair + 1],
                                            in1=bank[5 + pair % 2][:, 0:T], op0=ALU.mult, op1=ALU.add), S("y_taken"))

            for n in range(N_QKV + 2, N_QKV + 6):
                split(n + 2)
                for h in range(3 * (n - N_QKV - 2), 3 * (n - N_QKV - 2) + 3):
                    ssd_head(h)
                    if h % 2 == 0 and h >= 2:
                        take_y(h // 2 - 1)
            take_y(5)
            for n in range(N_U, N_U + 4):
                split(n + 2)
                if n == N_U:
                    dve.wait_ge(S("v_turned").sem, 1)
                    go(dve.tensor_copy(v_tok[:, :, :], bank[7][:, 0:T].rearrange("p (t c) -> p t c", c=P)), S("v_tok_ready"))
                attend(2 * (n - N_U))
                attend(2 * (n - N_U) + 1)
                if n == N_U + 3:
                    for t in range(TT):
                        dve.wait_ge(S("products_done").sem, products(n - 1) + t + 1)
                        d.mark(dve.tensor_copy(vm[:, t, 0:512], bank[3 + 2 * t][:, :]), S("vm_ready"))
                        d.mark(dve.tensor_copy(vm[:, t, 512:768], bank[4 + 2 * t][:, 0:256]), S("vm_ready"))

            def rotate(tile):
                for q in range(4):
                    d.mark(dve.tensor_copy(rot[32 * q:32 * q + 32, :], tile[32 * (q ^ 1):32 * (q ^ 1) + 32, :]), step)
                d.settle()
                go(dve.tensor_tensor(rot, rot, sinT, ALU.mult))
                go(dve.tensor_tensor(tile, tile, cosT, ALU.mult))
                go(dve.tensor_tensor(tile, tile, rot, ALU.add), S("rotated"))

            for n in range(N_Z, N_Z + 6):
                split(n + 2)
                if n == N_Z:
                    dve.wait_ge(S("sincos").sem, 2)
                    dve.wait_ge(S("tile_taken").sem, TAKEN_U)
                    rotate(krT)
                    for k in range(3):
                        rotate(qr[:, k, :])
                attend(A_MLA + n - N_Z)
            for k in range(6):
                dve.wait_ge(S("tile_taken").sem, TAKEN_U + k + 1)
                go(dve.tensor_tensor(yT[:, k, :], yT[:, k, :], zT[:, k, :], ALU.mult), S("y_gated"))
            for name, src, n_, g_col, k0 in MIX_NORMS(o_swa, yT, o_mla):
                feature_scale(name, src, n_, n_ * P)
                dve.wait_ge(S("products_done").sem, products(N_Z + 5))
                feature_lo(name, src, n_, uh[:, k0:k0 + n_, :], ul[:, k0:k0 + n_, :], g_col)
            for n in range(N_OUT, N_OUT + 16):
                split(n + 2)

            def add_bank(b, t, cb, signal):
                d.mark(dve.tensor_tensor(hres[:, t, cb * 512:(cb + 1) * 512], hres[:, t, cb * 512:(cb + 1) * 512], bank[b][:, :],
                                         ALU.add), signal)

            dve.wait_ge(S("residual_landed").sem, 32)
            for cb in range(4):
                dve.wait_ge(S("products_done").sem, products(N_OUT + 12 + cb))
                for t in range(TT):
                    add_bank(2 * cb + t, t, cb, S("mix_added"))
            d.settle()
            token_scale("hx", hres, hwork)
            for g in range(8):
                token_lo("hx", g, V_CROSS, g)
            for n in range(N_WQ, N_WQ + 4):
                split(n + 2)
            for j in range(A_X, A_X + 4):
                attend(j)
                if j > A_X:
                    cross_lo(dve, d, S, j - 1, cl, ch, bank)
            cross_lo(dve, d, S, A_X + 3, cl, ch, bank)
            for n in range(N_WO, N_WO + 4):
                split(n + 2)
                dve.wait_ge(S("products_done").sem, products(n))
                for t in range(TT):
                    add_bank(2 * (n - N_WO) + t, t, n - N_WO, S("cross_added"))
            d.settle()
            token_scale("hf", hres, hwork)
            for g in range(8):
                token_lo("hf", g, V_FFN, g)
            dve.sem_inc(S("prod_ready").sem, 4)

            def ffn_group(i, last=False):
                def at_turn(v, per):
                    return i * per + v
                for c in range(GROUP):
                    n = N_FFN + c
                    if not (last and c >= GROUP - 2):
                        split(n + 2, i, GROUP)
                    if c < 8:
                        s, v, k = c % 4, c % 2, c // 2
                        dve.wait_ge(S("fconv_raw").sem, at_turn(c + 3, 8))
                        for tap in (1, 2):
                            col = at_turn(v * FT + k + (V_FW + (2 - tap) * 2 * FT), 4)
                            go(dve.scalar_tensor_tensor(out=cacc[:, s, tap:T], in0=craw[:, s, 0:T - tap], scalar=vecs[:, bass.ds(col, 1)],
                                                        in1=cacc[:, s, tap:T], op0=ALU.mult, op1=ALU.add),
                               S("fconv_done") if tap == 2 else None)
                        if v == 1:
                            if k > 0:
                                gated_lo(k - 1, at_turn)
                                d.settle()
                            dve.wait_ge(S("silu_ready").sem, at_turn(k + 1, 4))
                            go(dve.tensor_tensor(prod[:, :], sil[:, :], cacc[:, s, :], ALU.mult), S("prod_ready"))
                    if c == 8:
                        gated_lo(3, at_turn)
                    if c >= 9:
                        for cb in ((c - 9,) if c < 11 else (2, 3)):
                            dve.wait_ge(S("products_done").sem, at_turn(products(N_FFN + 8 + cb), GROUP))
                            for t in range(TT):
                                add_bank(FFN_BANKS[cb] + t, t, cb, S("ffn_added"))

            def gated_lo(k, at_turn):
                dve.wait_ge(S("gated_hi").sem, at_turn(k + 1, 4))
                d.mark(dve.tensor_tensor(cl[:, k, :], prod[:, :], ch[:, k, :].bitcast(F32), ALU.subtract), S("gated_lo"))

            per = {S("lo_ready"): GROUP, S("fconv_done"): 8, S("prod_ready"): 4, S("gated_lo"): 4, S("ffn_added"): 8, step: 8}
            start = {s: s.n for s in per}
            start[S("prod_ready")] = 4
            with dve.Fori(0, GROUPS - 1) as i:
                for s in per:
                    s.n = i * per[s] + start[s]
                ffn_group(i)
            for s in per:
                s.n = start[s] + per[s] * (GROUPS - 1)
            ffn_group(GROUPS - 1, True)
            token_scale("final", hres, None)
            dve.wait_ge(S("gfin_landed").sem, 16)
            for t in range(TT):
                go(dve.scalar_tensor_tensor(out=hwork[:, t, :], in0=hres[:, t, :], scalar=small[:, s_r + t:s_r + t + 1],
                                            in1=gfin[:, :], op0=ALU.mult, op1=ALU.mult), S("out_ready"))

        @block.tensor
        def _(pe):
            done = S("products_done").sem

            def ready(n, i=None, per=0):
                pe.wait_ge(S("lo_ready").sem, n + 1 if i is None else i * per + n + 1)

            def three(dst, wh, wl, xh, xl, start, stop, stationary_x=False):
                if stationary_x:
                    pe.matmul(dst, xh, wh, start=start, stop=False)
                    pe.matmul(dst, xh, wl, start=False, stop=False)
                    return pe.matmul(dst, xl, wh, start=False, stop=stop)
                pe.matmul(dst, wh, xh, start=start, stop=False)
                pe.matmul(dst, wh, xl, start=False, stop=False)
                return pe.matmul(dst, wl, xh, start=False, stop=stop)

            def tile_product(n, b, cols=P):
                s = n % RING
                for k in range(KD):
                    last = three(bank[b][0:cols, 0:T], hi[:, s, k * P:k * P + cols], lo[:, s, k * P:k * P + cols],
                                 uh[:, k, :], ul[:, k, :], k == 0, k == KD - 1)
                last.then_inc(done, 1)

            def row_product(n, xh, xl, k0, b0, start, stop, signal=True, ks=range(4), b_start=None):
                s = n % RING
                for t in range(TT):
                    for k in ks:
                        last = three(bank[b0 + t][:, :], hi[:, s, k * 512:(k + 1) * 512], lo[:, s, k * 512:(k + 1) * 512],
                                     xh[:, k0 + k, t * P:(t + 1) * P], xl[:, k0 + k, t * P:(t + 1) * P],
                                     start and k == ks[0], stop and k == ks[-1], stationary_x=True)
                if signal:
                    last.then_inc(done, 1)

            def turn_group(name, src, g, b):
                for k in (2 * g, 2 * g + 1):
                    for t in range(TT):
                        o = (k % 2) * T + t * P
                        last = pe.transpose(bank[b][:, o:o + P], src[:, t, k * P:(k + 1) * P], ident)
                last.then_inc(S(f"{name}_turned").sem, 1)

            def square_sum(name, sq, n):
                pe.wait_ge(S(f"{name}_sq").sem, 1)
                for k in range(n):
                    last = pe.matmul(bank[7][:, 0:T], ones, sq[:, k * T:(k + 1) * T], start=(k == 0), stop=(k == n - 1))
                last.then_inc(S(f"{name}_ss").sem, 1)

            def scores(j):
                b = bank[3 + j % 2]
                if j >= 2:
                    pe.wait_ge(S("scores_taken").sem, j - 1)
                if j < A_MLA:
                    r = 64 * (j % 2)
                    key = swa_k if (j // 4) == (j % 2) else swa_kswap
                    pairs = [(swa_q[r:r + 64, j // 2, :], key[r:r + 64, :])]
                elif j < A_X:
                    h = j - A_MLA
                    r = 64 * (h % 2)
                    pairs = [(qn[:, h, :], kn[:, h, :]), (qr[r:r + 64, h // 2, :], krT[r:r + 64, :])]
                else:
                    h = j - A_X
                    pairs = [(q_x[:, h, :], kxT[:, h, :])]
                for t in range(TT):
                    c0, c1 = span(j, t)
                    for m, (q, k) in enumerate(pairs):
                        last = pe.matmul(b[:, c0:c1], q[:, t * P:(t + 1) * P], k[:, 0:c1 - c0], start=(m == 0), stop=(m == len(pairs) - 1))
                last.then_inc(S("scores_done").sem, 1)

            def attend_pv(j):
                pe.wait_ge(S("probs_ready").sem, j + 1)
                if j >= 2:
                    pe.wait_ge(S("probsT_copied").sem, j - 1)
                b = bank[5 + j % 2]
                s = ssb[:, j % 2, :]
                if j < A_X:
                    blocks = [(0, 0), (P, P), (2 * P, 2 * P)]
                    parts = [(0, 0, P, 0, True, True), (0, P, T, P, True, False), (1, P, T, 2 * P, False, True)]
                else:
                    blocks = [(0, 0), (T, P), (P, T), (T + P, T + P)]
                    parts = [(0, 0, T, 0, True, False), (1, 0, T, T, False, True)]
                for src, dst in blocks:
                    last = pe.transpose(b[:, dst:dst + P], s[:, src:src + P], ident)
                last.then_inc(S("probsT_done").sem, 1)
                pe.wait_ge(S("probsT_copied").sem, j + 1)
                if j >= 1:
                    pe.wait_ge(S("out_copied").sem, j)
                if j > A_X:
                    pe.wait_ge(S("cross_lo").sem, j - A_X)
                for kt, q0, q1, c, start, stop in parts:
                    if j < A_MLA:
                        r, g = 64 * (j % 2), j // 4
                        v, o = v_tok[:, kt, 64 * g:64 * g + 64], bank[7][r:r + 64, q0:q1]
                    elif j < A_X:
                        h = j - A_MLA
                        v, o = vm[:, kt, h * VD:(h + 1) * VD], bank[7][:, q0:q1]
                    else:
                        h = j - A_X
                        v, o = vx[:, kt, h * X_D:(h + 1) * X_D], bank[7][:, q0:q1]
                    last = pe.matmul(o, v, pts[:, j % 2, c:c + q1 - q0], start=start, stop=stop)
                last.then_inc(S("out_done").sem, 1)

            def attend(steps):
                for j in steps:
                    scores(j)
                    if j - 1 >= steps_first(j):
                        attend_pv(j - 1)

            pe.wait_ge(S("consts_landed").sem, N_CONSTS)
            for k, (r, col) in enumerate(((96, 0), (40, V_CW), (88, V_FW), (88, V_FW + 88), (88, V_FW + 176), (88, V_FB))):
                last = pe.transpose(bank[7][:, col:col + r], vrows[0:r, k, :], tab[0:r, C_ID:C_ID + r])
            last.then_inc(S("vecs_turned").sem, 1)
            pe.wait_ge(S("mem_scaled").sem, TT)
            for g in range(8):
                if g == 7:
                    pe.wait_ge(S("mem_lo").sem, 2)
                turn_group("mem", mems, g, MEM_BANKS[g])
            pe.wait_ge(S("mem_lo").sem, 16)
            for n in range(N_XK, N_XK + 4):
                ready(n)
                if n >= 3:
                    pe.wait_ge(S("tile_taken").sem, n - 2)
                tile_product(n, n % 3)
            for n in range(N_XV, N_XV + 4):
                ready(n)
                g = n - N_XV
                row_product(n, uh, ul, 4 * g, 4, g == 0, g == 3)
                if g == 0:
                    pe.wait_ge(S("x_scaled").sem, TT)
                    pe.wait_ge(S("tile_taken").sem, 4)
                if g == 3:
                    pe.wait_ge(S("x_lo").sem, 4)
                for gg in (2 * g, 2 * g + 1):
                    turn_group("x", xs, gg, X_BANKS[gg])
            pe.wait_ge(S("x_lo").sem, 16)
            with pe.Fori(0, 2) as i:
                for s in range(3):
                    ready(N_CQ + s, i, 3)
                    pe.wait_ge(S("tile_taken").sem, i * 3 + (4 + s - 2))
                    tile_product(N_CQ + s, (N_CQ + s) % 3)
            ready(N_KRDT)
            pe.wait_ge(S("tile_taken").sem, 8)
            tile_product(N_KRDT, N_KRDT % 3, ROPE + SSM_H)
            with pe.Fori(0, 3) as i:
                for s in range(3):
                    n = N_XBC + s
                    ready(n, i, 3)
                    pe.wait_ge(S("tile_taken").sem, i * 3 + (TAKEN_XBC + s - 2))
                    tile_product(n, n % 3)

            def w_in_tile(n):
                ready(n)
                pe.wait_ge(S("tile_taken").sem, TAKEN_XBC + n - N_XBC - 2)
                tile_product(n, n % 3)

            pe.wait_ge(S("vx_ready").sem, 2)
            pe.wait_ge(S("tile_taken").sem, TAKEN_XBC - 1)
            square_sum("cq", sq1, 4)
            pe.wait_ge(S("cq_var").sem, 1)
            square_sum("ckv", sq1, 2)
            w_in_tile(N_XBC + 9)
            for b in range(3):
                pe.wait_ge(S("xbc_ready").sem, 2 * b + 2)
                for k in (2 * b, 2 * b + 1):
                    for t in range(TT):
                        o = (k % 2) * T + t * P
                        last = pe.transpose(bank[3 + b][:, o:o + P], xbcT[:, k, t * P:(t + 1) * P], ident)
                last.then_inc(S("xbc_turned").sem, 1)
            w_in_tile(N_QKV)
            pe.wait_ge(S("dt_rows_ready").sem, 1)
            for k, (row, t) in enumerate(((0, 0), (0, 1), (2, 0), (2, 1), (3, 0))):
                last = pe.transpose(bank[6][:, 12 * k:12 * k + 12], dt_rows[0:SSM_H, row, t * P:(t + 1) * P], tab[0:SSM_H, C_ID:C_ID + SSM_H])
            last.then_inc(S("dt_turned").sem, 1)
            pe.wait_ge(S("x_tok_ready").sem, 6)
            pe.wait_ge(S("xbc_ready").sem, 10)
            for g in range(2):
                pe.matmul(bank[3 + g][:, 0:T], xbcT[:, 6 + g, 0:P], xbcT[:, 8 + g, :], start=True, stop=True)
                pe.matmul(bank[3 + g][:, T:T + P], xbcT[:, 6 + g, P:T], xbcT[:, 8 + g, P:T], start=True, stop=True).then_inc(S("cb_done").sem, 1)
            w_in_tile(N_QKV + 1)

            def spread(h):
                if h < 2:
                    pe.wait_ge(S("cb_masked").sem, h + 1)
                else:
                    pe.wait_ge(S("seg_ready").sem, h - 1)
                pe.matmul(bank[3 + h % 2][:, 0:T], tab[0:SSM_H, C_ID + h:C_ID + h + 1].to_broadcast([SSM_H, P]), acum[0:SSM_H, :],
                          start=True, stop=True).then_inc(S("acum_spread").sem, 1)

            def ssd_y(h):
                pair, r = h // 2, 64 * (h % 2)
                b = bank[5 + pair % 2]
                if h % 2 == 0:
                    if pair < 2:
                        pe.wait_ge(S("dt_cols_ready").sem, 1)
                    else:
                        pe.wait_ge(S("y_taken").sem, pair - 1)
                pe.wait_ge(S("ssd_weights").sem, h + 1)
                e = dec[:, h % 2, :]
                pe.matmul(b[r:r + 64, 0:P], x_tok[:, 0, h * 64:(h + 1) * 64], e[:, 0:P], start=True, stop=True)
                pe.matmul(b[r:r + 64, P:T], x_tok[:, 0, h * 64:(h + 1) * 64], e[:, P:T], start=True, stop=False)
                pe.matmul(b[r:r + 64, P:T], x_tok[:, 1, h * 64:(h + 1) * 64], e[:, T:T + P], start=False, stop=True).then_inc(S("ssd_used").sem, 1)

            spread(0)
            for n in range(N_QKV + 2, N_QKV + 6):
                for h in range(3 * (n - N_QKV - 2), 3 * (n - N_QKV - 2) + 3):
                    if h + 1 < SSM_H:
                        spread(h + 1)
                    ssd_y(h)
                w_in_tile(n)
            pe.wait_ge(S("tile_taken").sem, TAKEN_XBC + 16)
            pe.wait_ge(S("y_taken").sem, 6)
            for t in range(TT):
                last = pe.transpose(bank[7][:, t * P:(t + 1) * P], swa_v[:, t * P:(t + 1) * P], ident)
            last.then_inc(S("v_turned").sem, 1)
            pe.wait_ge(S("v_tok_ready").sem, 1)

            def latent_tile(index, w0, wcols, k0, kn_, s):
                pe.wait_ge(S("tile_taken").sem, TAKEN_XBC + 16 + index - 2)
                b = bank[(products(N_U - 1) + index) % 3]
                for k in range(kn_):
                    o = w0 + k * wcols
                    last = three(b[:, 0:T], hi[:, s, o:o + P], lo[:, s, o:o + P], ch[:, k0 + k, :], cl[:, k0 + k, :], k == 0, k == kn_ - 1)
                last.then_inc(done, 1)

            pe.wait_ge(S("ckv_lo").sem, 2)
            for n in range(N_U, N_U + 4):
                attend([2 * (n - N_U), 2 * (n - N_U) + 1])
                if n == N_U + 3:
                    attend_pv(A_MLA - 1)
                ready(n)
                s = n % RING
                if n == N_U:
                    for h in range(4):
                        latent_tile(h, h * NOPE, 4 * NOPE, 0, 4, s)
                elif n == N_U + 1:
                    for h in range(2):
                        latent_tile(4 + h, h * NOPE, 2 * NOPE, 0, 4, s)
                    for h in range(2):
                        latent_tile(6 + h, 1024 + h * P, 4 * ROPE, 0, 4, s)
                elif n == N_U + 2:
                    latent_tile(8, 0, P, 0, 4, s)
                    for h in range(6):
                        latent_tile(9 + h, 512 + h * NOPE, 6 * NOPE, 4, 2, s)
                else:
                    pe.wait_ge(S("probsT_copied").sem, A_MLA)
                    for t in range(TT):
                        for b, c0, c1 in ((3 + 2 * t, 0, 512), (4 + 2 * t, 512, 768)):
                            for k in range(2):
                                o = k * MLA_H * VD
                                last = three(bank[b][:, 0:c1 - c0], hi[:, s, o + c0:o + c1], lo[:, s, o + c0:o + c1],
                                             ch[:, 4 + k, t * P:(t + 1) * P], cl[:, 4 + k, t * P:(t + 1) * P], k == 0, k == 1,
                                             stationary_x=True)
                        last.then_inc(done, 1)
            pe.wait_ge(S("vm_ready").sem, 4)
            pe.wait_ge(S("rotated").sem, 4)
            for n in range(N_Z, N_Z + 6):
                attend([A_MLA + n - N_Z])
                ready(n)
                pe.wait_ge(S("tile_taken").sem, TAKEN_U + (n - N_Z) - 2)
                tile_product(n, z_bank(n))
            attend_pv(A_X - 1)
            pe.wait_ge(S("out_copied").sem, A_X)
            for name, n_ in (("swa", 4), ("mla", 6), ("ssm", 6)):
                square_sum(name, sq2, n_)
                pe.wait_ge(S(f"{name}_var").sem, 1)
            pe.wait_ge(S("tile_taken").sem, TAKEN_U + 6)
            n = N_OUT
            waits = {3: ("swa_lo", 4), 0: ("mla_lo", 6), 1: ("ssm_lo", 6), 2: ("ssm_lo", 6)}
            for m, g in enumerate(OUT_ORDER):
                pe.wait_ge(S(waits[g][0]).sem, waits[g][1])
                for cb in range(4):
                    ready(n)
                    row_product(n, uh, ul, 4 * g, 2 * cb, m == 0, m == 3)
                    n += 1
            pe.wait_ge(S("hx_scaled").sem, TT)
            for g in range(8):
                turn_group("hx", hwork, g, g)
            pe.wait_ge(S("hx_lo").sem, 16)
            for n in range(N_WQ, N_WQ + 4):
                ready(n)
                if n - N_WQ == 3:
                    pe.wait_ge(S("tile_taken").sem, TAKEN_U + 6 + 1)
                tile_product(n, n % 3)
            pe.wait_ge(S("tile_taken").sem, TAKEN_U + 10)
            attend(range(A_X, A_X + 4))
            attend_pv(A_X + 3)
            pe.wait_ge(S("cross_lo").sem, 4)
            for cb in range(4):
                ready(N_WO + cb)
                row_product(N_WO + cb, ch, cl, 0, 2 * cb, True, True)
            pe.wait_ge(S("hf_scaled").sem, TT)
            for g in range(8):
                turn_group("hf", hwork, g, g)
            pe.wait_ge(S("hf_lo").sem, 16)

            with pe.Fori(0, GROUPS) as i:
                for c in range(8):
                    n = N_FFN + c
                    ready(n, i, GROUP)
                    pe.wait_ge(S("fconv_raw").sem, i * 8 + (c + 1))
                    tile_product(n, c % 2)
                for c in (8, 9):
                    pe.wait_ge(S("gated_lo").sem, i * 4 + 3)
                    ready(N_FFN + c, i, GROUP)
                    row_product(N_FFN + c, ch, cl, 0, FFN_BANKS[c - 8], True, False, signal=False, ks=range(3))
                pe.wait_ge(S("gated_lo").sem, i * 4 + 4)
                for c in (8, 9):
                    row_product(N_FFN + c, ch, cl, 0, FFN_BANKS[c - 8], False, True, ks=range(3, 4))
                for c in (10, 11):
                    ready(N_FFN + c, i, GROUP)
                    if c == 11:
                        pe.wait_ge(S("ffn_added").sem, i * 8 + 2)
                    row_product(N_FFN + c, ch, cl, 0, FFN_BANKS[c - 8], True, True)


MEM_BANKS = (0, 1, 2, 3, 4, 5, 6, 0)
X_BANKS = (0, 1, 2, 3, 6, 7, 0, 1)
FFN_BANKS = (2, 4, 6, 2)
OUT_ORDER = (3, 0, 1, 2)
N_CONSTS = 16 * (1 + 10 + 1 + 3 + 1)
TAKEN_XBC = 11
TAKEN_U = TAKEN_XBC + 16 + 15


def MIX_NORMS(o_swa, y, o_mla):
    return (("swa", o_swa, 4, V_SWA, 12), ("mla", o_mla, 6, V_MLA, 0), ("ssm", y, 6, V_SSM, 6))


def z_bank(n):
    return (n - N_Z + 1) % 3


def steps_first(j):
    return A_SWA if j < A_MLA else A_MLA if j < A_X else A_X


def span(j, t):
    if j >= A_X:
        return t * 256, (t + 1) * 256
    return (0, 128) if t == 0 else (128, 384)


def cross_lo(dve, d, S, j, cl, ch, bank):
    dve.wait_ge(S("out_copied").sem, j + 1)
    d.mark(dve.tensor_tensor(cl[:, j - A_X, :], bank[7][:, 0:T], ch[:, j - A_X, :].bitcast(F32), ALU.subtract), S("cross_lo"))


_INS = ['x', 'mem', 'positions', 'norm_mix', 'w_in', 'mla_q_norm', 'mla_w_uq', 'mla_kv_norm', 'mla_w_ukv',
        'mla_out_norm', 'ssm_conv_w', 'ssm_conv_b', 'ssm_dt_bias', 'ssm_a_log', 'ssm_d', 'ssm_norm', 'swa_sinks',
        'swa_out_norm', 'w_out', 'norm_cross', 'norm_mem', 'cross_wq', 'cross_wkv', 'cross_wo', 'norm_ffn',
        'ffn_w_up', 'ffn_conv_w', 'ffn_conv_b', 'ffn_w_down', 'norm_final']


def kernel(**inputs):
    import numpy as _np
    import concourse.bacc as _bacc
    from concourse import mybir as _mybir
    from concourse.bass_utils import run_bass_kernel_spmd as _run

    nc = _bacc.Bacc("TRN2", target_bir_lowering=False, num_devices=1)
    arrays, args = {}, []
    for name in _INS:
        arr = _np.ascontiguousarray(inputs[name])
        arrays[f"in_{name}_dram"] = arr
        args.append(nc.dram_tensor(f"in_{name}_dram", arr.shape, _mybir.dt.from_np(arr.dtype), kind="ExternalInput").ap())
    arrays["table_dram"] = constant_table()
    args.append(nc.dram_tensor("table_dram", (P, C_ALL), F32, kind="ExternalInput").ap())
    args.append(nc.dram_tensor("out_0_dram", (1, T, D), F32, kind="ExternalOutput").ap())
    encoder(nc, *args)
    r = _run(nc, [arrays], core_ids=[0])
    return r.results[0]["out_0_dram"]
```

```python
from contextlib import ExitStack

import numpy as np
import concourse.bass as bass
from concourse import mybir

F32, F32R, I32 = mybir.dt.float32, mybir.dt.float32r, mybir.dt.int32
ALU, ACT, AX = mybir.AluOpType, mybir.ActivationFunctionType, mybir.AxisListType

P = 128
T = 256
TT = T // P
D = 2048
KD = D // P
M = 256
EPS = 1e-6
NEG = -1e30
FF = 5632
FT = FF // P
RING = 3
CH = 2048

MLA_H, NOPE, ROPE, VD = 6, 128, 64, 128
SSM_H, SSM_P = 12, 64
SWA_H, SWA_D = 8, 64
X_H, X_D = 4, 128

COL_KR, COL_Z, COL_XBC, COL_DT, COL_Q = 768, 832, 1600, 2880, 2892

N_XK, N_XV, N_CQ, N_KRDT, N_XBC, N_QKV, N_ZA, N_U, N_ZB, N_OUT, N_WQ, N_WO, N_FFN = 0, 4, 8, 14, 15, 25, 31, 34, 38, 41, 57, 61, 65
GROUP = 12
GROUPS = FT // 4
LAST = N_FFN + GROUP * GROUPS

V_MIX, V_CROSS, V_MEM, V_FFN, V_CQ, V_CKV, V_MLA, V_SSM, V_SWA, V_CB = 0, 16, 32, 48, 64, 68, 70, 76, 82, 86
V_ROWS_A = 96
V_CW = V_ROWS_A
V_FW = V_CW + 40
V_FB = V_FW + 3 * 2 * FT
V_ALL = V_FB + 2 * FT

C_ID, C_ONE, C_MLA, C_SWA, C_CAUSAL, C_INV, C_SGN = 0, 128, 256, 640, 1024, 1408, 1409
C_ALL = 1410

A_SWA, A_MLA, A_X = 0, SWA_H, SWA_H + MLA_H


def constant_table():
    c = np.zeros((P, C_ALL), np.float32)
    c[:, C_ID:C_ID + P] = np.eye(P)
    c[:, C_ONE:C_ONE + P] = 1.0
    q = np.arange(P)
    for base, window in ((C_MLA, 99), (C_SWA, 2)):
        for t, (lo, nk) in enumerate(((0, P), (P, T))):
            qc, kc = (t * P + q)[:, None] // 64, np.arange(nk)[None, :] // 64
            c[:, base + lo:base + lo + nk] = np.where((kc <= qc) & (kc > qc - window), 0.0, NEG)
    j, i = q[:, None], np.arange(T)[None, :]
    c[:, C_CAUSAL:C_CAUSAL + T] = i >= j
    c[:, C_CAUSAL + T:C_CAUSAL + T + P] = i[:, :P] >= j
    freq = (np.float32(10000.0) ** (-np.arange(0, ROPE, 2, dtype=np.float32) / np.float32(ROPE))).astype(np.float32)
    c[:, C_INV] = np.tile(freq, 4)
    c[:, C_SGN] = np.where(q % 64 < 32, -1.0, 1.0)
    return c


def dmas_of(n):
    return {N_KRDT: 2, N_U: 4, N_U + 1: 8, N_U + 2: 6, N_U + 3: 2}.get(n, 1)


def landed(n):
    return 16 * sum(dmas_of(m) for m in range(n % RING, n + 1, RING))


def products(n):
    extra = {N_U: 3, N_U + 1: 3, N_U + 2: 6, N_U + 3: 1}
    return n + 1 + sum(v for m, v in extra.items() if m <= n)


class Signal:

    def __init__(self, sem):
        self.sem, self.n = sem, 0


class Engine:

    def __init__(self, eng):
        self.eng, self.last = eng, None

    def mark(self, ins, signal):
        ins.then_inc(signal.sem, 1)
        signal.n = signal.n + 1
        self.last = signal

    def settle(self):
        self.eng.wait_ge(self.last.sem, self.last.n)


def encoder(nc, x, mem, positions, norm_mix, w_in, mla_q_norm, mla_w_uq, mla_kv_norm, mla_w_ukv, mla_out_norm,
            ssm_conv_w, ssm_conv_b, ssm_dt_bias, ssm_a_log, ssm_d, ssm_norm, swa_sinks, swa_out_norm, w_out,
            norm_cross, norm_mem, cross_wq, cross_wkv, cross_wo, norm_ffn, ffn_w_up, ffn_conv_w, ffn_conv_b,
            ffn_w_down, norm_final, table, out):
    ctx = ExitStack()
    with ctx:
        def sb(name, shape, dt=F32):
            return ctx.enter_context(nc.sbuf_tensor(name, shape, dt))

        signals = {}

        def S(name):
            if name not in signals:
                signals[name] = Signal(ctx.enter_context(nc.semaphore(name)))
            return signals[name]

        raw = sb("raw", [P, RING, CH])
        hi = sb("hi", [P, RING, CH], F32R)
        lo = sb("lo", [P, RING, CH], F32R)
        uh = sb("uh", [P, KD, T], F32R)
        ul = sb("ul", [P, KD, T], F32R)
        ch = sb("ch", [P, 6, T], F32R)
        cl = sb("cl", [P, 6, T], F32R)
        tab = sb("tab", [P, C_ALL])
        vecs = sb("vecs", [P, V_ALL])
        small = sb("small", [P, 112])
        arena = sb("arena", [P, 20400])
        bank = [ctx.enter_context(nc.psum_tensor(f"bank{i}", [P, 512], F32)) for i in range(8)]

        ident, ones = tab[:, C_ID:C_ID + P], tab[:, C_ONE:C_ONE + P]

        def at(off, *shape):
            size = int(np.prod(shape))
            v = arena[:, off:off + size]
            if len(shape) == 2:
                v = v.rearrange("p (a b) -> p a b", b=shape[1])
            if len(shape) == 3:
                v = v.rearrange("p (a b c) -> p a b c", b=shape[1], c=shape[2])
            return v

        kxT = at(0, X_H, M)
        vx = at(1024, TT, 512)
        cosT, sinT = at(2048, T), at(2304, T)
        o_swa = at(2560, 4, T)
        dt_rows = at(2560, 4, T)
        acum = at(3584, T)
        krT = at(3840, T)
        convraw, convacc = at(4096, RING, T), at(4864, RING, T)
        o_mla = at(5632, MLA_H, T)
        sq_cq, sq_ckv = at(5632, 4 * T), at(6656, 2 * T)
        cq_raw = at(7168, 6, T)
        yT = at(7168, 6, T)
        swa_q, swa_k, swa_v, swa_kswap = at(8704, 4, T), at(9728, T), at(9984, T), at(10240, T)
        sq_swa, sq_ssm = at(8704, 4 * T), at(8704, 6 * T)
        zT = at(4096, 6, T)
        v_tok = at(10496, TT, P)
        ssb = at(10752, 2, 512)
        pts = at(11776, 2, 512)
        rtmp_a, rtmp_b = at(12800, 3, T), at(10752, 3, T)
        xbcT = at(13568, 10, T)
        x_tok = at(16128, TT, 768)
        cbm = at(17664, 2, 384)
        dec = at(18432, 4, 384)
        qn = at(13568, MLA_H, T)
        kn = at(15104, MLA_H, T)
        vm = at(16640, TT, MLA_H * VD)
        qr = at(18176, 3, T)
        rot = at(18944, T)
        sq_mla = at(13568, 6 * T)
        mems, xs, junk = at(2560, TT, D), at(6656, TT, D), at(10752, D)
        vrows = at(12800, 6, P)
        posi = at(13568, T)
        ang, kk, kl, tmp4 = at(13824, T), at(14080, T), at(14336, T), at(14592, T)
        junk_v = at(15104, D)
        hres = at(2048 + 14000, TT, D)
        hwork = at(6144, TT, D)
        hjunk = at(2048, 4, 512)
        q_x = at(4096, X_H, T)
        craw, cacc = at(10240, 4, T), at(11264, 4, T)
        sil, prod = at(12288, T), at(12544, T)
        gfin = at(13568, D)

        s_ss, s_var, s_std, s_r, s_t = 0, 2, 4, 6, 8
        s_dcol, s_sink, s_nsink = 10, 16, 24
        s_cols = 32
        s_dall = 96
        stat = sb("stat", [P, 2, 8])
        parts = sb("parts", [P, TT, 4])
        row12 = sb("row12", [SSM_H, 4])
        assert arena.shape[1] >= 18176 + 768 + 256

        block = ctx.enter_context(nc.Block())

        def tail(t):
            return {0: (0, P), 1: (P, T)}[t]

        @block.sync
        def _(sp):
            def raw_free(n):
                sp.wait_ge(S("lo_ready").sem, n - RING + 1)

            def load(n, src, shape, slot=None, off=0):
                slot = n % RING if slot is None else slot
                size = int(np.prod(shape))
                dst = raw[:, slot, off:off + size]
                if len(shape) == 2:
                    dst = dst.rearrange("p (a b) -> p a b", b=shape[1])
                    sp.dma_start(dst, src).then_inc(S(f"raw_landed{slot}").sem, 16)
                else:
                    dst = dst.rearrange("p (a b c) -> p a b c", b=shape[1], c=shape[2])
                    sp.dma_start(dst, src).then_inc(S(f"raw_landed{slot}").sem, 16)

            def rows(w):
                return w[0].rearrange("(k p) c -> p k c", p=P)

            for t in range(TT):
                sp.dma_start(mems[:, t, :], mem[0, t * P:(t + 1) * P, :]).then_inc(S("mem_landed").sem, 16)
            load(0, rows(cross_wkv)[:, :, 0:P], (KD, P))
            load(1, rows(cross_wkv)[:, :, P:2 * P], (KD, P))
            load(2, rows(cross_wkv)[:, :, 2 * P:3 * P], (KD, P))
            for t in range(TT):
                sp.dma_start(xs[:, t, :], x[0, t * P:(t + 1) * P, :]).then_inc(S("x_landed").sem, 16)
            sp.dma_start(posi.bitcast(I32), positions[0].partition_broadcast(P)).then_inc(S("pos_landed").sem, 16)
            sp.dma_start(small[:, s_dall:s_dall + SSM_H], ssm_d[0].partition_broadcast(P)).then_inc(S("params_landed").sem, 16)
            sp.dma_start(small[:, s_sink:s_sink + SWA_H], swa_sinks[0].partition_broadcast(P)).then_inc(S("params_landed").sem, 16)
            sp.dma_start(row12[:, 0:1], ssm_dt_bias.rearrange("l h -> h l")).then_inc(S("params_landed").sem, 16)
            sp.dma_start(row12[:, 1:2], ssm_a_log.rearrange("l h -> h l")).then_inc(S("params_landed").sem, 16)

            raw_free(3)
            load(3, rows(cross_wkv)[:, :, 3 * P:4 * P], (KD, P))
            for g in range(4):
                raw_free(N_XV + g)
                load(N_XV + g, rows(cross_wkv)[:, 4 * g:4 * g + 4, 512:1024], (4, 512))

            def load_columns(first, count, w, col):
                v = rows(w)
                with sp.Fori(0, count // RING) as i:
                    for s in range(RING):
                        n = first + s
                        sp.wait_ge(S("lo_ready").sem, i * RING + (n - RING + 1))
                        load(n, v[:, :, bass.ds(i * (RING * P) + (col + s * P), P)], (KD, P))
                for s in range(count // RING * RING, count):
                    raw_free(first + s)
                    load(first + s, v[:, :, col + s * P:col + (s + 1) * P], (KD, P))

            load_columns(N_CQ, 6, w_in, 0)
            raw_free(N_KRDT)
            slot = raw[:, N_KRDT % RING, :].rearrange("p (k c) -> p k c", c=P)
            for lo_, hi_, col in ((0, ROPE, COL_KR), (ROPE, ROPE + SSM_H, COL_DT)):
                sp.dma_start(slot[:, :, lo_:hi_], rows(w_in)[:, :, col:col + hi_ - lo_]).then_inc(
                    S(f"raw_landed{N_KRDT % RING}").sem, 16)
            load_columns(N_XBC, 10, w_in, COL_XBC)
            load_columns(N_QKV, 6, w_in, COL_Q)
            load_columns(N_ZA, 3, w_in, COL_Z)
            uq = mla_w_uq[0].rearrange("(k p) (h e) -> p k h e", p=P, e=NOPE + ROPE)
            ukv = mla_w_ukv[0].rearrange("(k p) (h e) -> p k h e", p=P, e=NOPE + VD)

            def load4(n, parts):
                raw_free(n)
                off = 0
                for src, k, h, e in parts:
                    dst = raw[:, n % RING, off:off + k * h * e].rearrange("p (k h e) -> p k h e", h=h, e=e)
                    for kt in range(k):
                        sp.dma_start(dst[:, kt], src[:, kt]).then_inc(S(f"raw_landed{n % RING}").sem, 16)
                    off += k * h * e

            load4(N_U, [(uq[:, :, 0:4, 0:NOPE], 4, 4, NOPE)])
            load4(N_U + 1, [(uq[:, :, 4:6, 0:NOPE], 4, 2, NOPE), (uq[:, :, 0:4, NOPE:], 4, 4, ROPE)])
            load4(N_U + 2, [(uq[:, :, 4:6, NOPE:], 4, 2, ROPE), (ukv[:, :, :, 0:NOPE], 2, 6, NOPE)])
            load4(N_U + 3, [(ukv[:, :, :, NOPE:], 2, 6, VD)])
            load_columns(N_ZB, 3, w_in, COL_Z + 3 * P)
            n = N_OUT
            for g in OUT_ORDER:
                for cb in range(4):
                    raw_free(n)
                    load(n, rows(w_out)[:, 4 * g:4 * g + 4, cb * 512:(cb + 1) * 512], (4, 512))
                    n += 1
            sp.wait_ge(S("out_done").sem, A_X)
            for t in range(TT):
                sp.dma_start(hres[:, t, :], x[0, t * P:(t + 1) * P, :]).then_inc(S("residual_landed").sem, 16)
            for h in range(X_H):
                raw_free(N_WQ + h)
                load(N_WQ + h, rows(cross_wq)[:, :, h * P:(h + 1) * P], (KD, P))
            for cb in range(4):
                raw_free(N_WO + cb)
                load(N_WO + cb, rows(cross_wo)[:, :, cb * 512:(cb + 1) * 512], (4, 512))
            sp.wait_ge(S("mix_added").sem, 8)
            sp.dma_start(gfin[:, :], norm_final.partition_broadcast(P)).then_inc(S("gfin_landed").sem, 16)
            with sp.Fori(0, GROUPS) as i:
                for c in range(GROUP):
                    n = N_FFN + c
                    sp.wait_ge(S("lo_ready").sem, i * GROUP + (n - RING + 1))
                    if c < 8:
                        col = (c % 2) * FF + (c // 2) * P
                        load(n, rows(ffn_w_up)[:, :, bass.ds(i * (4 * P) + col, P)], (KD, P))
                    else:
                        cb = c - 8
                        load(n, rows(ffn_w_down)[:, bass.ds(i * 4, 4), cb * 512:(cb + 1) * 512], (4, 512))
            for cb in range(4):
                for t in range(TT):
                    sp.wait_ge(S(f"out_ready{t}").sem, cb + 1)
                    sp.dma_start(out[0, t * P:(t + 1) * P, cb * 512:(cb + 1) * 512],
                                 hwork[:, t, cb * 512:(cb + 1) * 512]).then_inc(S("out_stored").sem, 16)
            sp.wait_ge(S("out_stored").sem, 16 * TT * 4)

        def landed_at(n, i, per):
            return landed(n) if i is None else i * (16 * per // RING) + landed(n)

        @block.scalar
        def _(act):
            a = Engine(act)

            def split(n, i=None, per=GROUP):
                act.wait_ge(S(f"raw_landed{n % RING}").sem, landed_at(n, i, per))
                if i is not None or n >= RING:
                    before = products(n - RING)
                    act.wait_ge(S("products_done").sem, before if i is None else i * per + before)
                a.mark(act.copy(hi[:, n % RING, :], raw[:, n % RING, :]), S("hi_ready"))

            def token_root(name):
                act.wait_ge(S(f"{name}_var").sem, 1)
                a.mark(act.activation(small[:, s_std:s_std + 2], small[:, s_var:s_var + 2], ACT.Sqrt), S(f"{name}_std"))

            def block_squares(name, added, base):
                for cb in range(4):
                    for t in range(TT):
                        act.wait_ge(S(added).sem, base + TT * cb + t + 1)
                        if cb >= 2:
                            a.settle()
                        a.mark(act.activation(hjunk[:, (TT * cb + t) % 4, :], hres[:, t, cb * 512:(cb + 1) * 512], ACT.Square,
                                              accum_out=parts[:, t, cb:cb + 1]), S(f"{name}_parts"))
                token_root(name)

            def token_hi(name, g, g_col, b):
                act.wait_ge(S(f"{name}_turned").sem, g + 1)
                for k in (2 * g, 2 * g + 1):
                    a.mark(act.activation(uh[:, k, :], bank[b][:, (k % 2) * T:(k % 2 + 1) * T], ACT.Copy,
                                          scale=vecs[:, g_col + k:g_col + k + 1]), S(f"{name}_hi"))

            def squares(name, src, sq, n):
                a.settle()
                a.mark(act.activation(sq[:, 0:n * T], src.rearrange("p a b -> p (a b)"), ACT.Square), S(f"{name}_sq"))

            def root(name, tmp):
                act.wait_ge(S(f"{name}_var").sem, 1)
                a.mark(act.activation(tmp[:, 1, :], tmp[:, 0, :], ACT.Sqrt), S(f"{name}_std"))

            def feature_hi(name, src, n, dst_h, g_col):
                act.wait_ge(S(f"{name}_scaled").sem, 1)
                for k in range(n):
                    a.mark(act.activation(dst_h[:, k, :], src[:, k, :], ACT.Copy,
                                          scale=vecs[:, g_col + k:g_col + k + 1]), S(f"{name}_hi"))

            def attend_exp(j):
                act.wait_ge(S("negmax_ready").sem, j + 1)
                st = stat[:, j % 2, :]
                if j < A_MLA:
                    for t in range(TT):
                        act.activation(st[:, 4 + t:5 + t], small[:, s_sink + j:s_sink + j + 1], ACT.Exp, bias=st[:, t:t + 1])
                for t in range(TT):
                    c0, c1 = span(j, t)
                    ins = act.activation(ssb[:, j % 2, c0:c1], ssb[:, j % 2, c0:c1], ACT.Exp,
                                         bias=st[:, t:t + 1], accum_out=st[:, 2 + t:3 + t])
                a.mark(ins, S("exp_done"))

            def attend_turned(j):
                act.wait_ge(S("probsT_done").sem, j + 1)
                if j >= 2:
                    act.wait_ge(S("out_done").sem, j - 1)
                w = 512 if j >= A_X else 384
                a.mark(act.copy(pts[:, j % 2, 0:w], bank[5 + j % 2][:, 0:w]), S("probsT_copied"))

            def attend_out(pair):
                act.wait_ge(S("out_done").sem, 2 * pair + 2)
                if pair < A_MLA // 2:
                    ins = act.copy(o_swa[:, pair, :], bank[7][:, 0:T])
                elif pair < A_X // 2:
                    k = 2 * pair - A_MLA
                    ins = act.copy(o_mla[:, k:k + 2, :], bank[7][:, :].rearrange("p (a b) -> p a b", b=T))
                else:
                    k = 2 * pair - A_X
                    ins = act.copy(ch[:, k:k + 2, :], bank[7][:, :].rearrange("p (a b) -> p a b", b=T))
                a.mark(ins, S("out_copied"))

            def wait_product(n):
                act.wait_ge(S("products_done").sem, products(n))

            def take(n, b, dst):
                wait_product(n)
                a.mark(act.copy(dst, bank[b][:, 0:T]), S("tile_taken"))

            consts = S("consts_landed").sem
            act.dma_start(tab[:, :], table[:, :]).then_inc(consts, 16)
            at_row = 0
            for v, n in ((norm_mix, 16), (norm_cross, 16), (norm_mem, 16), (norm_ffn, 16), (mla_q_norm, 4),
                         (mla_kv_norm, 2), (mla_out_norm, 6), (ssm_norm, 6), (swa_out_norm, 4), (ssm_conv_b, 10)):
                act.dma_start(vrows[at_row:at_row + n, 0, :], v.rearrange("l (r c) -> (l r) c", c=P)).then_inc(consts, 16)
                at_row += n
            act.dma_start(vrows[0:40, 1, :], ssm_conv_w[0].rearrange("k (r c) -> (k r) c", c=P)).then_inc(consts, 16)
            for k in range(3):
                act.dma_start(vrows[0:2 * FT, 2 + k, :], ffn_conv_w[0, k].rearrange("(r c) -> r c", c=P)).then_inc(consts, 16)
            act.dma_start(vrows[0:2 * FT, 5, :], ffn_conv_b[0].rearrange("(r c) -> r c", c=P)).then_inc(consts, 16)

            act.wait_ge(S("mem_landed").sem, 32)
            a.mark(act.activation(junk, mems[:, 0, :], ACT.Square, accum_out=small[:, s_ss:s_ss + 1]), S("mem_ss"))
            token_root("mem")
            split(0)
            act.wait_ge(S("vecs_turned").sem, 1)
            a.mark(act.copy(vecs[:, :], bank[7][:, 0:V_ALL]), S("vecs_ready"))
            a.settle()
            for g in range(8):
                token_hi("mem", g, V_MEM, MEM_BANKS[g])
                if g == 3:
                    split(1)
            act.wait_ge(S("x_landed").sem, 32)
            a.mark(act.activation(junk, xs[:, 0, :], ACT.Square, accum_out=small[:, s_ss:s_ss + 1]), S("x_ss"))
            for n in range(N_XK, N_XK + 4):
                split(n + 2)
                take(n, n % 3, kxT[:, n, :])
                if n == N_XK:
                    token_root("x")
                if n == N_XK + 2:
                    for f in range(2):
                        act.wait_ge(S("angles_ready").sem, f + 1)
                        a.mark(act.activation((sinT, cosT)[f], (kk, kl)[f], ACT.Sin), S("sincos"))
            for n in range(N_XV, N_XV + 4):
                if n > N_XV:
                    for g in (2 * (n - N_XV) - 2, 2 * (n - N_XV) - 1):
                        act.wait_ge(S("products_done").sem, products(n - 1))
                        token_hi("x", g, V_MIX, X_BANKS[g])
                split(n + 2)
            wait_product(N_XV + 3)
            for g in (6, 7):
                token_hi("x", g, V_MIX, X_BANKS[g])
            for n in range(N_CQ, N_CQ + 6):
                split(n + 2)
                take(n, n % 3, cq_raw[:, n - N_CQ, :])
            split(N_KRDT + 2)
            wait_product(N_KRDT)
            b = bank[N_KRDT % 3]
            a.mark(act.copy(krT[0:64, :], b[0:64, 0:T]), S("kr_parts"))
            a.mark(act.copy(krT[64:128, :], b[0:64, 0:T]), S("kr_parts"))
            a.mark(act.copy(dt_rows[0:SSM_H, 0, :], b[64:64 + SSM_H, 0:T]), S("tile_taken"))
            squares("cq", cq_raw[:, 0:4, :], sq_cq, 4)
            squares("ckv", cq_raw[:, 4:6, :], sq_ckv, 2)

            def conv_first(n):
                c = n - N_XBC
                wait_product(n)
                if c >= RING:
                    act.wait_ge(S("xbc_ready").sem, c - RING + 1)
                a.mark(act.activation(convacc[:, n % RING, :], bank[n % 3][:, 0:T], ACT.Identity,
                                      scale=vecs[:, V_CW + 30 + c:V_CW + 31 + c], bias=vecs[:, V_CB + c:V_CB + c + 1]), S("conv_first"))
                a.mark(act.copy(convraw[:, n % RING, :], bank[n % 3][:, 0:T]), S("tile_taken"))

            def conv_silu(n):
                c = n - N_XBC
                act.wait_ge(S("conv_done").sem, c + 1)
                a.mark(act.activation(xbcT[:, c, :], convacc[:, n % RING, :], ACT.Silu), S("xbc_ready"))

            def take_x_tok(b):
                act.wait_ge(S("xbc_turned").sem, b + 1)
                for k in range(2):
                    a.mark(act.copy(x_tok[:, :, (2 * b + k) * P:(2 * b + k + 1) * P],
                                    bank[3 + b][:, k * T:(k + 1) * T].rearrange("p (t c) -> p t c", c=P)), S("x_tok_ready"))

            for n in range(N_XBC, N_XBC + 10):
                split(n + 2)
                if n == 16:
                    act.wait_ge(S("dt_abs").sem, 1)
                    a.mark(act.activation(dt_rows[0:SSM_H, 2, :], dt_rows[0:SSM_H, 2, :], ACT.Exp), S("dt_exp"))
                    a.mark(act.activation(row12[:, 2:3], row12[:, 1:2], ACT.Exp), S("a_exp"))
                if n == 18:
                    act.wait_ge(S("dt_w").sem, 1)
                    a.mark(act.activation(dt_rows[0:SSM_H, 3, :], dt_rows[0:SSM_H, 3, :], ACT.Ln), S("dt_ln"))
                if n == 22:
                    root("cq", rtmp_a)
                    root("ckv", rtmp_b)
                if n == 24:
                    feature_hi("cq", cq_raw, 4, ch, V_CQ)
                if n in (22, 23, 24):
                    take_x_tok(n - 22)
                conv_first(n)
                if n > N_XBC:
                    conv_silu(n - 1)
            for n in range(N_QKV, N_QKV + 6):
                split(n + 2)
                if n == N_QKV:
                    conv_silu(n - 1)
                    feature_hi("ckv", cq_raw[:, 4:6, :], 2, ch[:, 4:6, :], V_CKV)
                if n >= N_SSD:
                    for h in (2 * (n - N_SSD), 2 * (n - N_SSD) + 1):
                        ssd_exp(h, act, a, S, dec)
                k = n - N_QKV
                if k == 4:
                    wait_product(n)
                    a.mark(act.copy(swa_kswap[0:64, :], bank[n % 3][64:128, 0:T]), S("kr_parts"))
                    a.mark(act.copy(swa_kswap[64:128, :], bank[n % 3][0:64, 0:T]), S("kr_parts"))
                take(n, n % 3, swa_q[:, k, :] if k < 4 else (swa_k, swa_v)[k - 4])

            def pair_step(n):
                old, new = pair_of(n - 1), pair_of(n)
                if old is not None:
                    attend_turned(2 * old)
                    attend_turned(2 * old + 1)
                split(n + 2)
                if new is not None:
                    attend_exp(2 * new)
                    attend_exp(2 * new + 1)
                if old is not None:
                    attend_out(old)

            def take_u(n):
                first = products(n - 1)
                dsts = {0: [qn[:, h, :] for h in range(4)], 1: [qn[:, 4, :], qn[:, 5, :], qr[:, 0, :], qr[:, 1, :]],
                        2: [qr[:, 2, :]] + [kn[:, h, :] for h in range(6)]}[n - N_U]
                act.wait_ge(S("y_taken").sem, 6)
                for m, dst in enumerate(dsts):
                    act.wait_ge(S("products_done").sem, first + m + 1)
                    a.mark(act.copy(dst, bank[(first + m) % 3][:, 0:T]), S("tile_taken"))

            for n in range(N_ZA, N_OUT + 1):
                if n >= N_PAIR:
                    pair_step(n)
                else:
                    split(n + 2)
                if n < N_SSD + 6:
                    for h in (2 * (n - N_SSD), 2 * (n - N_SSD) + 1):
                        ssd_exp(h, act, a, S, dec)
                if n == 38:
                    squares("swa", o_swa, sq_swa, 4)
                if n == 40:
                    root("swa", rtmp_a)
                if n < N_U:
                    take(n, z_bank(n), zT[:, n - N_ZA, :])
                elif n < N_U + 3:
                    take_u(n)
                elif N_ZB <= n < N_OUT:
                    take(n, z_bank(n), zT[:, 3 + n - N_ZB, :])
                if n == 40:
                    a.settle()
                    a.mark(act.activation(zT[:, :, :], zT[:, :, :], ACT.Silu), S("gate_ready"))
                    feature_hi("swa", o_swa, 4, ch, V_SWA)
                if n == 41:
                    act.wait_ge(S("y_gated").sem, 1)
                    squares("ssm", yT, sq_ssm, 6)
                    squares("mla", o_mla, sq_mla, 6)
            split(44)
            root("ssm", rtmp_a)
            root("mla", rtmp_b)
            feature_hi("mla", o_mla, 6, uh, V_MLA)
            split(45)
            feature_hi("ssm", yT, 6, uh[:, 6:12, :], V_SSM)
            for n in range(44, N_OUT + 16):
                split(n + 2)
            block_squares("hx", "mix_added", 0)
            for g in range(8):
                token_hi("hx", g, V_CROSS, g)
            for n in range(N_WQ, N_WQ + 4):
                split(n + 2)
                if n == N_WQ + 3:
                    attend_turned(A_X)
                    attend_turned(A_X + 1)
                take(n, n % 3, q_x[:, n - N_WQ, :])
                if n == N_WQ + 2:
                    attend_exp(A_X)
                    attend_exp(A_X + 1)
            attend_out(A_X // 2)
            attend_exp(A_X + 2)
            attend_exp(A_X + 3)
            attend_turned(A_X + 2)
            attend_turned(A_X + 3)
            attend_out(A_X // 2 + 1)
            for n in range(N_WO, N_WO + 4):
                split(n + 2)
            block_squares("hf", "cross_added", 0)
            for g in range(8):
                token_hi("hf", g, V_FFN, g)

            def ffn_group(i, last=False):
                def at_turn(v, per):
                    return i * per + v

                def gated_hi(k):
                    act.wait_ge(S("prod_ready").sem, at_turn(k + 1 + 4, 4))
                    a.mark(act.copy(ch[:, k, :], prod[:, :]), S("gated_hi"))

                for c in range(GROUP):
                    n = N_FFN + c
                    if c == 8:
                        gated_hi(3)
                    if not (last and c >= GROUP - 2):
                        split(n + 2, i, GROUP)
                    if c < 8:
                        s, v, k = c % 4, c % 2, c // 2
                        act.wait_ge(S("products_done").sem, at_turn(products(n), GROUP))
                        act.wait_ge(S("prod_ready").sem, at_turn(k + 3, 4))
                        tile = at_turn(v * FT + k, 4)
                        a.mark(act.activation(cacc[:, s, :], bank[c % 2][:, 0:T], ACT.Identity,
                                              scale=vecs[:, bass.ds(tile + (V_FW + 2 * 2 * FT), 1)],
                                              bias=vecs[:, bass.ds(tile + V_FB, 1)]), S("fconv_first"))
                        a.mark(act.copy(craw[:, s, :], bank[c % 2][:, 0:T]), S("fconv_raw"))
                        if v == 1:
                            act.wait_ge(S("fconv_done").sem, at_turn(2 * k + 1, 8))
                            a.mark(act.activation(sil[:, :], cacc[:, s - 1, :], ACT.Silu), S("silu_ready"))
                        elif k > 0:
                            gated_hi(k - 1)
            act.sem_inc(S("fconv_raw").sem, 2)
            with act.Fori(0, GROUPS - 1) as i:
                ffn_group(i)
            ffn_group(GROUPS - 1, True)
            block_squares("final", "ffn_added", 8 * (GROUPS - 1))
            act.wait_ge(S("final_r").sem, 1)
            for cb in range(4):
                c = slice(cb * 512, (cb + 1) * 512)
                a.mark(act.activation(hwork[:, 0, c], hwork[:, 0, c], ACT.Copy, scale=small[:, s_r:s_r + 1]), S("out_ready0"))

        @block.vector
        def _(dve):
            d = Engine(dve)
            step = S("vector_step")

            def go(ins, signal=None):
                d.mark(ins, signal or step)
                d.settle()

            def split(n, i=None, per=GROUP):
                v = n + 1
                dve.wait_ge(S("hi_ready").sem, v if i is None else i * per + v)
                if i is not None or n >= RING:
                    before = products(n - RING)
                    dve.wait_ge(S("products_done").sem, before if i is None else i * per + before)
                d.mark(dve.tensor_tensor(lo[:, n % RING, :], raw[:, n % RING, :], hi[:, n % RING, :].bitcast(F32), ALU.subtract),
                       S("lo_ready"))

            def newton(r, v, t, last=None):
                go(dve.tensor_tensor(t, r, r, ALU.mult))
                go(dve.tensor_tensor(t, t, v, ALU.mult))
                go(dve.tensor_scalar(t, t, -0.5, 1.5, ALU.mult, ALU.add))
                go(dve.tensor_tensor(r, r, t, ALU.mult), last)

            def token_rsqrt(name, last=None):
                v, sd = small[:, s_var:s_var + 2], small[:, s_std:s_std + 2]
                r, t_ = small[:, s_r:s_r + 2], small[:, s_t:s_t + 2]
                go(dve.tensor_scalar(v, small[:, s_ss:s_ss + 2], 1.0 / D, EPS, ALU.mult, ALU.add), S(f"{name}_var"))
                dve.wait_ge(S(f"{name}_std").sem, 1)
                go(dve.reciprocal(r, sd))
                newton(r, v, t_, last)

            def token_scale(name, src, dst):
                for q in range(4):
                    for t in range(TT):
                        c = slice(q * 512, (q + 1) * 512)
                        d.mark(dve.tensor_scalar(dst[:, t, c], src[:, t, c], small[:, s_r + t:s_r + t + 1], None, ALU.mult),
                               S(f"{name}_scaled"))

            def tile_squares(name, src):
                go(dve.tensor_tensor_reduce(junk_v, src[:, 1, :], src[:, 1, :], 1.0, 0.0, ALU.mult, ALU.add,
                                            small[:, s_ss + 1:s_ss + 2]))
                dve.wait_ge(S(f"{name}_ss").sem, 1)

            def sum_parts(name):
                dve.wait_ge(S(f"{name}_parts").sem, 8)
                go(dve.tensor_reduce(small[:, s_ss:s_ss + 2], parts[:, :, :], AX.X, ALU.add))

            def token_lo(name, g, g_col, b):
                dve.wait_ge(S(f"{name}_hi").sem, 2 * g + 2)
                for k in (2 * g, 2 * g + 1):
                    d.mark(dve.scalar_tensor_tensor(out=ul[:, k, :], in0=bank[b][:, (k % 2) * T:(k % 2 + 1) * T],
                                                    scalar=vecs[:, g_col + k:g_col + k + 1], in1=uh[:, k, :].bitcast(F32),
                                                    op0=ALU.mult, op1=ALU.subtract), S(f"{name}_lo"))

            def feature_var(name, b, tmp, dim):
                dve.wait_ge(S(f"{name}_ss").sem, 1)
                go(dve.tensor_scalar(tmp[:, 0, :], bank[b][:, 0:T], 1.0 / dim, EPS, ALU.mult, ALU.add), S(f"{name}_var"))

            def feature_scale(name, src, n, tmp):
                dve.wait_ge(S(f"{name}_std").sem, 1)
                go(dve.reciprocal(tmp[:, 1, :], tmp[:, 1, :]))
                newton(tmp[:, 1, :], tmp[:, 0, :], tmp[:, 2, :])
                go(dve.tensor_tensor(src, src, tmp[:, 1, :].unsqueeze(1).to_broadcast([P, n, T]), ALU.mult), S(f"{name}_scaled"))

            def feature_lo(name, src, n, dst_h, dst_l, g_col):
                dve.wait_ge(S(f"{name}_hi").sem, n)
                for k in range(n):
                    d.mark(dve.scalar_tensor_tensor(out=dst_l[:, k, :], in0=src[:, k, :], scalar=vecs[:, g_col + k:g_col + k + 1],
                                                    in1=dst_h[:, k, :].bitcast(F32), op0=ALU.mult, op1=ALU.subtract), S(f"{name}_lo"))

            def attend_mask(j):
                b, s, st = bank[3 + j % 2], ssb[:, j % 2, :], stat[:, j % 2, :]
                w = 512 if j >= A_X else 384
                dve.wait_ge(S("scores_done").sem, j + 1)
                if j >= 2:
                    dve.wait_ge(S("probsT_done").sem, j - 1)
                if j < A_X:
                    col, scale = (C_SWA, SWA_D ** -0.5) if j < A_MLA else (C_MLA, (NOPE + ROPE) ** -0.5)
                    go(dve.scalar_tensor_tensor(out=s[:, 0:w], in0=b[:, 0:w], scalar=scale, in1=tab[:, col:col + w],
                                                op0=ALU.mult, op1=ALU.add), S("scores_taken"))
                else:
                    go(dve.tensor_scalar(s[:, 0:w], b[:, 0:w], X_D ** -0.5, None, ALU.mult), S("scores_taken"))
                for t in range(TT):
                    c0, c1 = span(j, t)
                    ins = dve.tensor_reduce(st[:, t:t + 1], s[:, c0:c1], AX.X, ALU.max, negate=True)
                    d.mark(ins, S("negmax_ready") if j >= A_MLA and t == 1 else step)
                if j < A_MLA:
                    d.settle()
                    d.mark(dve.tensor_scalar(st[:, 0:2], st[:, 0:2], small[:, s_nsink + j:s_nsink + j + 1], None, ALU.min), S("negmax_ready"))

            def attend_norm(j):
                s, st = ssb[:, j % 2, :], stat[:, j % 2, :]
                dve.wait_ge(S("exp_done").sem, j + 1)
                if j < A_MLA:
                    go(dve.tensor_tensor(st[:, 2:4], st[:, 2:4], st[:, 4:6], ALU.add))
                go(dve.reciprocal(st[:, 6:8], st[:, 2:4]))
                for t in range(TT):
                    c0, c1 = span(j, t)
                    ins = dve.tensor_scalar(s[:, c0:c1], s[:, c0:c1], st[:, 6 + t:7 + t], None, ALU.mult)
                    d.mark(ins, S("probs_ready") if t == 1 else step)

            dve.wait_ge(S("mem_landed").sem, 32)
            tile_squares("mem", mems)
            token_rsqrt("mem")
            token_scale("mem", mems, mems)
            split(0)
            dve.wait_ge(S("vecs_ready").sem, 1)
            for g in range(8):
                token_lo("mem", g, V_MEM, MEM_BANKS[g])
            split(1)
            dve.wait_ge(S("x_landed").sem, 32)
            tile_squares("x", xs)
            split(2)
            token_rsqrt("x")
            token_scale("x", xs, xs)
            dve.wait_ge(S("pos_landed").sem, 16)
            dve.wait_ge(S("consts_landed").sem, N_CONSTS)
            go(dve.tensor_copy(ang, posi.bitcast(I32)))
            go(dve.tensor_scalar(ang, ang, tab[:, C_INV:C_INV + 1], None, ALU.mult))
            magic = 1.5 * 2.0 ** 23
            go(dve.tensor_scalar(kk, ang, float(1 / (2 * np.pi)), magic, ALU.mult, ALU.add))
            go(dve.tensor_scalar(kk, kk, -magic, None, ALU.add))
            go(dve.tensor_scalar(kl, kk, magic * 2.0 ** 12, None, ALU.add))
            go(dve.tensor_scalar(kl, kl, -magic * 2.0 ** 12, None, ALU.add))
            go(dve.tensor_tensor(kk, kk, kl, ALU.subtract))
            rest = 2 * np.pi
            for _ in range(4):
                e = 2.0 ** (np.floor(np.log2(rest)) - 10)
                part = float(np.floor(rest / e) * e)
                rest -= part
                go(dve.scalar_tensor_tensor(out=ang, in0=kl, scalar=-part, in1=ang, op0=ALU.mult, op1=ALU.add))
                go(dve.scalar_tensor_tensor(out=ang, in0=kk, scalar=-part, in1=ang, op0=ALU.mult, op1=ALU.add))
            lim = 3.1415925
            go(dve.tensor_scalar(kk, ang, lim, -lim, ALU.min, ALU.max), S("angles_ready"))
            go(dve.tensor_scalar(tmp4, ang, float(np.pi / 2), float(-2 * np.pi), ALU.is_gt, ALU.mult))
            go(dve.scalar_tensor_tensor(out=kl, in0=ang, scalar=float(np.pi / 2), in1=tmp4, op0=ALU.add, op1=ALU.add))
            go(dve.tensor_scalar(kl, kl, lim, -lim, ALU.min, ALU.max), S("angles_ready"))
            for n in range(N_XK + 1, N_XK + 4):
                split(n + 2)
            dve.wait_ge(S("sincos").sem, 1)
            go(dve.tensor_scalar(sinT, sinT, tab[:, C_SGN:C_SGN + 1], None, ALU.mult))
            for n in range(N_XV, N_XV + 4):
                if n > N_XV:
                    for g in (2 * (n - N_XV) - 2, 2 * (n - N_XV) - 1):
                        dve.wait_ge(S("products_done").sem, products(n - 1))
                        token_lo("x", g, V_MIX, X_BANKS[g])
                split(n + 2)
            dve.wait_ge(S("products_done").sem, products(N_XV + 3))
            for g in (6, 7):
                token_lo("x", g, V_MIX, X_BANKS[g])
            for t in range(TT):
                d.mark(dve.tensor_copy(vx[:, t, :], bank[4 + t][:, :]), S("vx_ready"))
            dve.wait_ge(S("params_landed").sem, 16 * 4)
            for half in range(2):
                rows_ = slice(64 * half, 64 * half + 64)
                go(dve.tensor_copy(small[rows_, s_dcol:s_dcol + 6],
                                   small[rows_, s_dall:s_dall + SSM_H].rearrange("p (t s) -> p t s", s=2)[:, :, half]))
            go(dve.tensor_scalar(small[:, s_nsink:s_nsink + SWA_H], small[:, s_sink:s_sink + SWA_H], -1.0, None, ALU.mult))

            for n in range(N_CQ, N_CQ + 6):
                split(n + 2)
            split(N_KRDT + 2)

            def conv_rest(n):
                c = n - N_XBC
                dve.wait_ge(S("tile_taken").sem, TAKEN_XBC + c + 1)
                s = n % RING
                for k in (1, 2, 3):
                    col = V_CW + 10 * (3 - k) + c
                    go(dve.scalar_tensor_tensor(out=convacc[:, s, k:T], in0=convraw[:, s, 0:T - k], scalar=vecs[:, col:col + 1],
                                                in1=convacc[:, s, k:T], op0=ALU.mult, op1=ALU.add),
                       S("conv_done") if k == 3 else None)

            H = slice(0, SSM_H)
            r0, r1, r2, r3 = (dt_rows[H, k, :] for k in range(4))
            for n in range(N_XBC, N_XBC + 10):
                split(n + 2)
                if n == 15:
                    dve.wait_ge(S("tile_taken").sem, TAKEN_XBC)
                    go(dve.tensor_scalar(r0, r0, row12[:, 0:1], None, ALU.add))
                    go(dve.tensor_scalar(r2, r0, -1.0, None, ALU.mult))
                    go(dve.tensor_tensor(r2, r2, r0, ALU.min), S("dt_abs"))
                    go(dve.tensor_scalar(r0, r0, 0.0, None, ALU.max))
                if n == 17:
                    dve.wait_ge(S("dt_exp").sem, 1)
                    go(dve.tensor_scalar(r3, r2, 1.0, None, ALU.add))
                    go(dve.tensor_scalar(r1, r3, -1.0, None, ALU.add), S("dt_w"))
                    go(dve.tensor_scalar(acum[H, :], r1, 0.0, None, ALU.is_equal))
                    go(dve.tensor_tensor(r1, r1, acum[H, :], ALU.add))
                    go(dve.reciprocal(r1, r1))
                if n == 19:
                    dve.wait_ge(S("dt_ln").sem, 1)
                    go(dve.tensor_tensor(r3, r3, acum[H, :], ALU.add))
                    go(dve.tensor_tensor(r3, r3, r1, ALU.mult))
                    go(dve.tensor_tensor(r3, r3, r2, ALU.mult))
                    go(dve.tensor_tensor(r0, r0, r3, ALU.add))
                if n == 20:
                    dve.wait_ge(S("a_exp").sem, 1)
                    go(dve.tensor_scalar(r1, r0, row12[:, 2:3], -1.0, ALU.mult, ALU.mult))
                    for t in range(TT):
                        go(dve.tensor_tensor_scan(acum[H, t * P:(t + 1) * P], tab[H, C_ONE:C_ONE + P], r1[:, t * P:(t + 1) * P], 0.0,
                                                  ALU.mult, ALU.add))
                    go(dve.tensor_scalar(r2, acum[H, :], -1.0, None, ALU.mult))
                    go(dve.tensor_scalar(r3[:, 0:P], r2[:, 0:P], acum[H, P - 1:P], None, ALU.add), S("dt_rows_ready"))
                if n == 21:
                    feature_var("cq", 7, rtmp_a, 512)
                    feature_var("ckv", 6, rtmp_b, 256)
                if n == 22:
                    dve.wait_ge(S("dt_turned").sem, 1)
                    go(dve.tensor_copy(small[:, s_cols:s_cols + 60], bank[6][:, 0:60]), S("dt_cols_ready"))
                if n == 23:
                    feature_scale("cq", cq_raw[:, 0:4, :], 4, rtmp_a)
                if n == 24:
                    feature_scale("ckv", cq_raw[:, 4:6, :], 2, rtmp_b)
                conv_rest(n)
            split(N_QKV + 2)
            feature_lo("cq", cq_raw, 4, ch, cl, V_CQ)
            split(N_QKV + 3)
            for g in range(2):
                dve.wait_ge(S("cb_done").sem, g + 1)
                go(dve.tensor_tensor(cbm[:, g, :], bank[3 + g][:, 0:384], tab[:, C_CAUSAL:C_CAUSAL + 384], ALU.mult), S("cb_masked"))
            feature_lo("ckv", cq_raw[:, 4:6, :], 2, ch[:, 4:6, :], cl[:, 4:6, :], V_CKV)

            def ssd_seg(h):
                na0, na1, ea0 = (small[:, s_cols + 12 * k + h:s_cols + 12 * k + h + 1] for k in (2, 3, 4))
                b, e = bank[3 + h % 2], dec[:, h % 4, :]
                dve.wait_ge(S("acum_spread").sem, h + 1)
                if h >= 4:
                    dve.wait_ge(S("ssd_used").sem, h - 3)
                d.mark(dve.tensor_scalar(e[:, 0:P], b[:, 0:P], na0, 0.0, ALU.add, ALU.min), step)
                d.mark(dve.tensor_scalar(e[:, P:T], b[:, P:T], ea0, 0.0, ALU.add, ALU.min), step)
                d.mark(dve.tensor_scalar(e[:, T:T + P], b[:, P:T], na1, 0.0, ALU.add, ALU.min), S("seg_ready"))

            def ssd_weigh(h):
                dt0, dt1 = (small[:, s_cols + 12 * k + h:s_cols + 12 * k + h + 1] for k in (0, 1))
                e, g = dec[:, h % 4, :], h // 6
                dve.wait_ge(S("decay_ready").sem, h + 1)
                d.mark(dve.scalar_tensor_tensor(out=e[:, 0:T], in0=e[:, 0:T], scalar=dt0, in1=cbm[:, g, 0:T],
                                                op0=ALU.mult, op1=ALU.mult), step)
                d.mark(dve.scalar_tensor_tensor(out=e[:, T:T + P], in0=e[:, T:T + P], scalar=dt1, in1=cbm[:, g, T:T + P],
                                                op0=ALU.mult, op1=ALU.mult), S("ssd_weights"))

            def take_y(pair):
                dve.wait_ge(S("ssd_used").sem, 2 * pair + 2)
                d.mark(dve.scalar_tensor_tensor(out=yT[:, pair, :], in0=xbcT[:, pair, :], scalar=small[:, s_dcol + pair:s_dcol + pair + 1],
                                                in1=bank[5 + pair % 2][:, 0:T], op0=ALU.mult, op1=ALU.add), S("y_taken"))

            def rotate(tile):
                for q in range(4):
                    d.mark(dve.tensor_copy(rot[32 * q:32 * q + 32, :], tile[32 * (q ^ 1):32 * (q ^ 1) + 32, :]), step)
                d.settle()
                go(dve.tensor_tensor(rot, rot, sinT, ALU.mult))
                go(dve.tensor_tensor(tile, tile, cosT, ALU.mult))
                go(dve.tensor_tensor(tile, tile, rot, ALU.add), S("rotated"))

            def take_vm(t):
                dve.wait_ge(S("products_done").sem, products(N_U + 2) + t + 1)
                d.mark(dve.tensor_copy(vm[:, t, 0:512], bank[3][:, :]), S("vm_ready"))
                d.mark(dve.tensor_copy(vm[:, t, 512:768], bank[4][:, 0:256]), S("vm_ready"))

            for n in range(N_SSD, N_OUT + 1):
                if n < N_SSD + 6:
                    for h in (2 * (n - N_SSD), 2 * (n - N_SSD) + 1):
                        ssd_seg(h)
                if N_SSD < n <= N_SSD + 6:
                    take_y(n - N_SSD - 1)
                if n == N_PAIR:
                    dve.wait_ge(S("v_turned").sem, 1)
                    d.mark(dve.tensor_copy(v_tok[:, :, :], bank[7][:, 0:T].rearrange("p (t c) -> p t c", c=P)), S("v_tok_ready"))
                if n == N_U + 2:
                    rotate(krT)
                    for k in range(2):
                        dve.wait_ge(S("tile_taken").sem, TAKEN_U + 7 + k)
                        rotate(qr[:, k, :])
                if n == N_U + 3:
                    dve.wait_ge(S("tile_taken").sem, TAKEN_U + 9)
                    rotate(qr[:, 2, :])
                    take_vm(0)
                pair = pair_of(n)
                if pair is not None:
                    for j in (2 * pair, 2 * pair + 1):
                        attend_mask(j)
                split(n + 2)
                if n == N_U + 3:
                    take_vm(1)
                if n < N_SSD + 6:
                    for h in (2 * (n - N_SSD), 2 * (n - N_SSD) + 1):
                        ssd_weigh(h)
                if pair is not None:
                    for j in (2 * pair, 2 * pair + 1):
                        attend_norm(j)
                if n == 39:
                    feature_var("swa", 7, rtmp_a, 512)
                if n == 40:
                    feature_scale("swa", o_swa, 4, rtmp_a)
                    feature_lo("swa", o_swa, 4, ch, cl, V_SWA)
                if n == 41:
                    dve.wait_ge(S("gate_ready").sem, 1)
                    go(dve.tensor_tensor(yT[:, :, :], yT[:, :, :], zT[:, :, :], ALU.mult), S("y_gated"))
            feature_var("ssm", 7, rtmp_a, 768)
            split(44)
            feature_var("mla", 6, rtmp_b, 768)
            feature_scale("mla", o_mla, 6, rtmp_b)
            feature_lo("mla", o_mla, 6, uh, ul, V_MLA)
            split(45)
            feature_scale("ssm", yT, 6, rtmp_a)
            feature_lo("ssm", yT, 6, uh[:, 6:12, :], ul[:, 6:12, :], V_SSM)
            for n in range(44, N_OUT + 16):
                split(n + 2)

            def add_bank(b, t, cb, signal):
                d.mark(dve.tensor_tensor(hres[:, t, cb * 512:(cb + 1) * 512], hres[:, t, cb * 512:(cb + 1) * 512], bank[b][:, :],
                                         ALU.add), signal)

            dve.wait_ge(S("residual_landed").sem, 32)
            for cb in range(4):
                dve.wait_ge(S("products_done").sem, products(N_OUT + 12 + cb))
                for t in range(TT):
                    add_bank(2 * cb + t, t, cb, S("mix_added"))
            d.settle()
            sum_parts("hx")
            token_rsqrt("hx")
            token_scale("hx", hres, hwork)
            for g in range(8):
                token_lo("hx", g, V_CROSS, g)
            for n in range(N_WQ, N_WQ + 4):
                split(n + 2)
                if n == N_WQ + 2:
                    attend_mask(A_X)
                    attend_mask(A_X + 1)
                    attend_norm(A_X)
                    attend_norm(A_X + 1)

            def cross_lo(k):
                dve.wait_ge(S("out_copied").sem, A_X // 2 + k + 1)
                d.mark(dve.tensor_tensor(cl[:, 2 * k:2 * k + 2, :], bank[7][:, :].rearrange("p (a b) -> p a b", b=T),
                                         ch[:, 2 * k:2 * k + 2, :].bitcast(F32), ALU.subtract), S("cross_lo"))

            cross_lo(0)
            attend_mask(A_X + 2)
            attend_mask(A_X + 3)
            attend_norm(A_X + 2)
            attend_norm(A_X + 3)
            cross_lo(1)
            for n in range(N_WO, N_WO + 4):
                split(n + 2)
                dve.wait_ge(S("products_done").sem, products(n))
                for t in range(TT):
                    add_bank(2 * (n - N_WO) + t, t, n - N_WO, S("cross_added"))
            d.settle()
            sum_parts("hf")
            token_rsqrt("hf")
            token_scale("hf", hres, hwork)
            for g in range(8):
                token_lo("hf", g, V_FFN, g)
            dve.sem_inc(S("prod_ready").sem, 4)

            def ffn_group(i, last=False):
                def at_turn(v, per):
                    return i * per + v
                for c in range(GROUP):
                    n = N_FFN + c
                    if c == 8:
                        gated_lo(3, at_turn)
                    if not (last and c >= GROUP - 2):
                        split(n + 2, i, GROUP)
                    if c < 8:
                        s, v, k = c % 4, c % 2, c // 2
                        dve.wait_ge(S("fconv_raw").sem, at_turn(c + 3, 8))
                        for tap in (1, 2):
                            col = at_turn(v * FT + k + (V_FW + (2 - tap) * 2 * FT), 4)
                            go(dve.scalar_tensor_tensor(out=cacc[:, s, tap:T], in0=craw[:, s, 0:T - tap], scalar=vecs[:, bass.ds(col, 1)],
                                                        in1=cacc[:, s, tap:T], op0=ALU.mult, op1=ALU.add),
                               S("fconv_done") if tap == 2 else None)
                        if v == 0 and k > 0:
                            gated_lo(k - 1, at_turn)
                        if v == 1:
                            dve.wait_ge(S("silu_ready").sem, at_turn(k + 1, 4))
                            go(dve.tensor_tensor(prod[:, :], sil[:, :], cacc[:, s, :], ALU.mult), S("prod_ready"))
                    if c >= 9:
                        for cb in ((c - 9,) if c < 11 else (2, 3)):
                            dve.wait_ge(S("products_done").sem, at_turn(products(N_FFN + 8 + cb), GROUP))
                            for t in range(TT):
                                add_bank(FFN_BANKS[cb] + t, t, cb, S("ffn_added"))
                            if last:
                                d.settle()
                                for t in range(TT):
                                    cols = slice(cb * 512, (cb + 1) * 512)
                                    d.mark(dve.tensor_tensor(hwork[:, t, cols], hres[:, t, cols], gfin[:, cols], ALU.mult), step)

            def gated_lo(k, at_turn):
                dve.wait_ge(S("gated_hi").sem, at_turn(k + 1, 4))
                d.mark(dve.tensor_tensor(cl[:, k, :], prod[:, :], ch[:, k, :].bitcast(F32), ALU.subtract), S("gated_lo"))

            per = {S("lo_ready"): GROUP, S("fconv_done"): 8, S("prod_ready"): 4, S("gated_lo"): 4, S("ffn_added"): 8, step: 8}
            start = {s: s.n for s in per}
            start[S("prod_ready")] = 4
            with dve.Fori(0, GROUPS - 1) as i:
                for s in per:
                    s.n = i * per[s] + start[s]
                ffn_group(i)
            for s in per:
                s.n = start[s] + per[s] * (GROUPS - 1)
            dve.wait_ge(S("gfin_landed").sem, 16)
            ffn_group(GROUPS - 1, True)
            sum_parts("final")
            token_rsqrt("final", S("final_r"))
            for cb in range(4):
                c = slice(cb * 512, (cb + 1) * 512)
                d.mark(dve.tensor_scalar(hwork[:, 1, c], hwork[:, 1, c], small[:, s_r + 1:s_r + 2], None, ALU.mult), S("out_ready1"))

        @block.tensor
        def _(pe):
            done = S("products_done").sem

            def ready(n, i=None, per=0):
                pe.wait_ge(S("lo_ready").sem, n + 1 if i is None else i * per + n + 1)

            def three(dst, wh, wl, xh, xl, start, stop, stationary_x=False):
                if stationary_x:
                    pe.matmul(dst, xh, wh, start=start, stop=False)
                    pe.matmul(dst, xh, wl, start=False, stop=False)
                    return pe.matmul(dst, xl, wh, start=False, stop=stop)
                pe.matmul(dst, wh, xh, start=start, stop=False)
                pe.matmul(dst, wh, xl, start=False, stop=False)
                return pe.matmul(dst, wl, xh, start=False, stop=stop)

            def tile_product(n, b, cols=P, mid=None, lo_signal=None):
                s = n % RING
                for k in range(KD):
                    if k == KD // 2 and mid:
                        mid()
                    if lo_signal and k % 2 == 0:
                        pe.wait_ge(S(lo_signal).sem, k + 2)
                    last = three(bank[b][0:cols, 0:T], hi[:, s, k * P:k * P + cols], lo[:, s, k * P:k * P + cols],
                                 uh[:, k, :], ul[:, k, :], k == 0, k == KD - 1)
                last.then_inc(done, 1)

            def row_product(n, xh, xl, k0, b0, start, stop, signal=True, ks=range(4), mid=None):
                s = n % RING
                for t in range(TT):
                    if t == 1 and mid:
                        mid()
                    for k in ks:
                        last = three(bank[b0 + t][:, :], hi[:, s, k * 512:(k + 1) * 512], lo[:, s, k * 512:(k + 1) * 512],
                                     xh[:, k0 + k, t * P:(t + 1) * P], xl[:, k0 + k, t * P:(t + 1) * P],
                                     start and k == ks[0], stop and k == ks[-1], stationary_x=True)
                if signal:
                    last.then_inc(done, 1)

            def turn_group(name, src, g, b):
                pe.wait_ge(S(f"{name}_scaled").sem, TT * (g // 2) + TT)
                for k in (2 * g, 2 * g + 1):
                    for t in range(TT):
                        o = (k % 2) * T + t * P
                        last = pe.transpose(bank[b][:, o:o + P], src[:, t, k * P:(k + 1) * P], ident)
                last.then_inc(S(f"{name}_turned").sem, 1)

            def square_sum(name, sq, n, b):
                pe.wait_ge(S(f"{name}_sq").sem, 1)
                for k in range(n):
                    last = pe.matmul(bank[b][:, 0:T], ones, sq[:, k * T:(k + 1) * T], start=(k == 0), stop=(k == n - 1))
                last.then_inc(S(f"{name}_ss").sem, 1)

            def scores(j):
                b = bank[3 + j % 2]
                if j >= 2:
                    pe.wait_ge(S("scores_taken").sem, j - 1)
                if j < A_MLA:
                    r = 64 * (j % 2)
                    key = swa_k if (j // 4) == (j % 2) else swa_kswap
                    pairs = [(swa_q[r:r + 64, j // 2, :], key[r:r + 64, :])]
                elif j < A_X:
                    h = j - A_MLA
                    r = 64 * (h % 2)
                    pairs = [(qn[:, h, :], kn[:, h, :]), (qr[r:r + 64, h // 2, :], krT[r:r + 64, :])]
                else:
                    h = j - A_X
                    pairs = [(q_x[:, h, :], kxT[:, h, :])]
                for t in range(TT):
                    c0, c1 = span(j, t)
                    for m, (q, k) in enumerate(pairs):
                        last = pe.matmul(b[:, c0:c1], q[:, t * P:(t + 1) * P], k[:, 0:c1 - c0], start=(m == 0), stop=(m == len(pairs) - 1))
                last.then_inc(S("scores_done").sem, 1)

            def turn_probs(j):
                pe.wait_ge(S("probs_ready").sem, j + 1)
                if j >= 2:
                    pe.wait_ge(S("probsT_copied").sem, j - 1)
                blocks = [(0, 0), (P, P), (2 * P, 2 * P)] if j < A_X else [(0, 0), (T, P), (P, T), (T + P, T + P)]
                for src, dst in blocks:
                    last = pe.transpose(bank[5 + j % 2][:, dst:dst + P], ssb[:, j % 2, src:src + P], ident)
                last.then_inc(S("probsT_done").sem, 1)

            def head_out(j):
                pe.wait_ge(S("probsT_copied").sem, j + 1)
                if j >= 2 and j % 2 == 0:
                    pe.wait_ge(S("out_copied").sem, j // 2)
                if j == A_X + 2:
                    pe.wait_ge(S("cross_lo").sem, 1)
                if j < A_X:
                    parts_ = [(0, 0, P, 0, True, True), (0, P, T, P, True, False), (1, P, T, 2 * P, False, True)]
                else:
                    parts_ = [(0, 0, T, 0, True, False), (1, 0, T, T, False, True)]
                for kt, q0, q1, c, start, stop in parts_:
                    if j < A_MLA:
                        r, g = 64 * (j % 2), j // 4
                        v, o = v_tok[:, kt, 64 * g:64 * g + 64], bank[7][r:r + 64, q0:q1]
                    else:
                        h = j - A_MLA if j < A_X else j - A_X
                        v, o = (vm if j < A_X else vx)[:, kt, h * P:(h + 1) * P], bank[7][:, T * (j % 2) + q0:T * (j % 2) + q1]
                    last = pe.matmul(o, v, pts[:, j % 2, c:c + q1 - q0], start=start, stop=stop)
                last.then_inc(S("out_done").sem, 1)

            def both(f, pair):
                f(2 * pair)
                f(2 * pair + 1)

            pe.wait_ge(S("consts_landed").sem, N_CONSTS)
            for k, (r, col) in enumerate(((96, 0), (40, V_CW), (88, V_FW), (88, V_FW + 88), (88, V_FW + 176), (88, V_FB))):
                last = pe.transpose(bank[7][:, col:col + r], vrows[0:r, k, :], tab[0:r, C_ID:C_ID + r])
            last.then_inc(S("vecs_turned").sem, 1)
            for g in range(8):
                if g == 7:
                    pe.wait_ge(S("mem_lo").sem, 2)
                turn_group("mem", mems, g, MEM_BANKS[g])
            pe.wait_ge(S("mem_lo").sem, 16)
            for n in range(N_XK, N_XK + 4):
                ready(n)
                if n >= 3:
                    pe.wait_ge(S("tile_taken").sem, n - 2)
                tile_product(n, n % 3)
            for n in range(N_XV, N_XV + 4):
                ready(n)
                g = n - N_XV
                row_product(n, uh, ul, 4 * g, 4, g == 0, g == 3)
                if g == 0:
                    pe.wait_ge(S("tile_taken").sem, 4)
                if g == 3:
                    pe.wait_ge(S("x_lo").sem, 4)
                for gg in (2 * g, 2 * g + 1):
                    turn_group("x", xs, gg, X_BANKS[gg])
            with_lo = "x_lo"
            for n in range(N_CQ, N_CQ + 6):
                ready(n)
                pe.wait_ge(S("tile_taken").sem, n - N_CQ + 2)
                tile_product(n, n % 3, lo_signal=with_lo)
                with_lo = None
            ready(N_KRDT)
            pe.wait_ge(S("tile_taken").sem, 8)
            tile_product(N_KRDT, N_KRDT % 3, ROPE + SSM_H)

            def w_in_tile(n, mid=None):
                ready(n)
                pe.wait_ge(S("tile_taken").sem, TAKEN_XBC + n - N_XBC - 2)
                tile_product(n, n % 3, mid=mid)

            def turn_x(b):
                pe.wait_ge(S("xbc_ready").sem, 2 * b + 2)
                for k in (2 * b, 2 * b + 1):
                    for t in range(TT):
                        o = (k % 2) * T + t * P
                        last = pe.transpose(bank[3 + b][:, o:o + P], xbcT[:, k, t * P:(t + 1) * P], ident)
                last.then_inc(S("xbc_turned").sem, 1)

            for n in range(N_XBC, N_QKV + 2):
                if n == 21:
                    square_sum("cq", sq_cq, 4, 7)
                    square_sum("ckv", sq_ckv, 2, 6)
                if n == 22:
                    pe.wait_ge(S("dt_rows_ready").sem, 1)
                    pe.wait_ge(S("ckv_var").sem, 1)
                    for k, (row, t) in enumerate(((0, 0), (0, 1), (2, 0), (2, 1), (3, 0))):
                        last = pe.transpose(bank[6][:, 12 * k:12 * k + 12], dt_rows[0:SSM_H, row, t * P:(t + 1) * P],
                                            tab[0:SSM_H, C_ID:C_ID + SSM_H])
                    last.then_inc(S("dt_turned").sem, 1)
                if n in (22, 23, 24):
                    pe.wait_ge(S("vx_ready").sem, 2)
                    turn_x(n - 22)
                if n == 26:
                    pe.wait_ge(S("x_tok_ready").sem, 6)
                    pe.wait_ge(S("xbc_ready").sem, 10)
                    for g in range(2):
                        b = bank[3 + g]
                        pe.matmul(b[:, 0:T], xbcT[:, 6 + g, 0:P], xbcT[:, 8 + g, :], start=True, stop=True)
                        pe.matmul(b[:, T:T + P], xbcT[:, 6 + g, P:T], xbcT[:, 8 + g, P:T], start=True, stop=True).then_inc(S("cb_done").sem, 1)
                w_in_tile(n)

            def spread(h):
                if h < 2:
                    pe.wait_ge(S("cb_masked").sem, h + 1)
                else:
                    pe.wait_ge(S("seg_ready").sem, h - 1)
                pe.matmul(bank[3 + h % 2][:, 0:T], tab[0:SSM_H, C_ID + h:C_ID + h + 1].to_broadcast([SSM_H, P]), acum[0:SSM_H, :],
                          start=True, stop=True).then_inc(S("acum_spread").sem, 1)

            def ssd_y(h):
                pair, r = h // 2, 64 * (h % 2)
                b = bank[5 + pair % 2]
                if h % 2 == 0:
                    if pair < 2:
                        pe.wait_ge(S("dt_cols_ready").sem, 1)
                    else:
                        pe.wait_ge(S("y_taken").sem, pair - 1)
                pe.wait_ge(S("ssd_weights").sem, h + 1)
                e = dec[:, h % 4, :]
                pe.matmul(b[r:r + 64, 0:P], x_tok[:, 0, h * 64:(h + 1) * 64], e[:, 0:P], start=True, stop=True)
                pe.matmul(b[r:r + 64, P:T], x_tok[:, 0, h * 64:(h + 1) * 64], e[:, P:T], start=True, stop=False)
                pe.matmul(b[r:r + 64, P:T], x_tok[:, 1, h * 64:(h + 1) * 64], e[:, T:T + P], start=False, stop=True).then_inc(S("ssd_used").sem, 1)

            def latent_tile(index, w0, wcols, k0, kn_, s):
                pe.wait_ge(S("tile_taken").sem, TAKEN_U + index - 2)
                b = bank[(products(N_U - 1) + index) % 3]
                for k in range(kn_):
                    o = w0 + k * wcols
                    last = three(b[:, 0:T], hi[:, s, o:o + P], lo[:, s, o:o + P], ch[:, k0 + k, :], cl[:, k0 + k, :], k == 0, k == kn_ - 1)
                last.then_inc(done, 1)

            def latent_values(t, s):
                for b, c0, c1 in ((3, 0, 512), (4, 512, 768)):
                    for k in range(2):
                        o = k * MLA_H * VD
                        last = three(bank[b][:, 0:c1 - c0], hi[:, s, o + c0:o + c1], lo[:, s, o + c0:o + c1],
                                     ch[:, 4 + k, t * P:(t + 1) * P], cl[:, 4 + k, t * P:(t + 1) * P], k == 0, k == 1,
                                     stationary_x=True)
                last.then_inc(done, 1)

            for n in range(N_SSD, N_OUT):
                s = n % RING
                if n < N_SSD + 6:
                    both(spread, n - N_SSD)
                if N_SSD < n <= N_SSD + 6:
                    both(ssd_y, n - N_SSD - 1)
                turn, new = pair_of(n - 1), pair_of(n)
                if n == N_PAIR:
                    pe.wait_ge(S("tile_taken").sem, TAKEN_XBC + 16)
                    for t in range(TT):
                        last = pe.transpose(bank[7][:, t * P:(t + 1) * P], swa_v[:, t * P:(t + 1) * P], ident)
                    last.then_inc(S("v_turned").sem, 1)
                    pe.wait_ge(S("seg_ready").sem, SSM_H)
                if n == N_PAIR + 1:
                    pe.wait_ge(S("y_taken").sem, 6)
                    pe.wait_ge(S("v_tok_ready").sem, 1)
                if turn is not None:
                    both(turn_probs, turn)
                if n == N_ZB:
                    pe.wait_ge(S("vm_ready").sem, 4)
                    pe.wait_ge(S("rotated").sem, 4)
                if n == 39:
                    pe.wait_ge(S("out_copied").sem, A_MLA // 2)
                    square_sum("swa", sq_swa, 4, 7)
                if new is not None:
                    both(scores, new)
                if n == 39:
                    pe.wait_ge(S("swa_var").sem, 1)

                def mid():
                    if turn is not None:
                        both(head_out, turn)

                ready(n)
                if n < N_ZA:
                    w_in_tile(n, mid)
                elif n < N_U:
                    pe.wait_ge(S("tile_taken").sem, TAKEN_XBC + n - N_XBC - 2)
                    tile_product(n, z_bank(n), mid=mid)
                elif n == N_U:
                    pe.wait_ge(S("ckv_lo").sem, 2)
                    for h in range(4):
                        if h == 2:
                            mid()
                        latent_tile(h, h * NOPE, 4 * NOPE, 0, 4, s)
                elif n == N_U + 1:
                    for h in range(2):
                        latent_tile(4 + h, h * NOPE, 2 * NOPE, 0, 4, s)
                    mid()
                    for h in range(2):
                        latent_tile(6 + h, 1024 + h * P, 4 * ROPE, 0, 4, s)
                elif n == N_U + 2:
                    latent_tile(8, 0, P, 0, 4, s)
                    for h in range(6):
                        if h == 2:
                            mid()
                        latent_tile(9 + h, 512 + h * NOPE, 6 * NOPE, 4, 2, s)
                elif n == N_U + 3:
                    pe.wait_ge(S("scores_taken").sem, A_MLA)
                    latent_values(0, s)
                    mid()
                    pe.wait_ge(S("vm_ready").sem, 2)
                    latent_values(1, s)
                else:
                    pe.wait_ge(S("tile_taken").sem, TAKEN_U + 15 + (n - N_ZB) - 2)
                    tile_product(n, z_bank(n), mid=mid)

            both(turn_probs, A_X // 2 - 1)

            def last_heads():
                both(head_out, A_X // 2 - 1)

            def ssm_squares():
                pe.wait_ge(S("out_copied").sem, A_X // 2)
                square_sum("ssm", sq_ssm, 6, 7)

            def mla_squares():
                pe.wait_ge(S("probsT_copied").sem, A_X)
                square_sum("mla", sq_mla, 6, 6)

            mids = {N_OUT: last_heads, N_OUT + 1: ssm_squares, N_OUT + 2: mla_squares}
            n = N_OUT
            for m, g in enumerate(OUT_ORDER):
                xh, xl, k0 = (ch, cl, 0) if g == 3 else (uh, ul, 4 * g)
                name, count = {3: ("swa_lo", 4), 0: ("mla_lo", 4), 1: ("ssm_lo", 2), 2: ("ssm_lo", 6)}[g]
                pe.wait_ge(S(name).sem, count)
                for cb in range(4):
                    ready(n)
                    if n == N_OUT + 1:
                        pe.wait_ge(S("tile_taken").sem, TAKEN_U + 18)
                    if n == N_OUT + 3:
                        pe.wait_ge(S("ssm_var").sem, 1)
                        pe.wait_ge(S("mla_var").sem, 1)
                    row_product(n, xh, xl, k0, 2 * cb, m == 0, m == 3, mid=mids.get(n))
                    n += 1
            for g in range(8):
                turn_group("hx", hwork, g, g)
            for n in range(N_WQ, N_WQ + 4):
                ready(n)
                if n == N_WQ:
                    pe.wait_ge(S("hx_lo").sem, 16)
                if n == N_WQ + 3:
                    pe.wait_ge(S("tile_taken").sem, TAKEN_U + 19)
                    both(turn_probs, A_X // 2)

                def mid():
                    if n == N_WQ + 2:
                        pe.wait_ge(S("tile_taken").sem, TAKEN_U + 20)
                        both(scores, A_X // 2)
                    if n == N_WQ + 3:
                        both(head_out, A_X // 2)
                tile_product(n, n % 3, mid=mid)
            pe.wait_ge(S("tile_taken").sem, TAKEN_U + 22)
            both(scores, A_X // 2 + 1)
            pe.wait_ge(S("cross_lo").sem, 1)
            ready(N_WO)
            row_product(N_WO, ch, cl, 0, 0, True, False, signal=False, ks=range(2))
            both(turn_probs, A_X // 2 + 1)
            ready(N_WO + 1)
            row_product(N_WO + 1, ch, cl, 0, 2, True, False, signal=False, ks=range(2))
            both(head_out, A_X // 2 + 1)
            pe.wait_ge(S("cross_lo").sem, 2)
            for cb in (0, 1):
                row_product(N_WO + cb, ch, cl, 0, 2 * cb, False, True, ks=range(2, 4))
            for cb in (2, 3):
                ready(N_WO + cb)
                row_product(N_WO + cb, ch, cl, 0, 2 * cb, True, True)
            for g in range(8):
                turn_group("hf", hwork, g, g)
            pe.wait_ge(S("hf_lo").sem, 16)

            with pe.Fori(0, GROUPS) as i:
                for c in range(8):
                    n = N_FFN + c
                    ready(n, i, GROUP)
                    pe.wait_ge(S("fconv_raw").sem, i * 8 + (c + 1))
                    tile_product(n, c % 2)
                for c in (8, 9):
                    pe.wait_ge(S("gated_lo").sem, i * 4 + 3)
                    ready(N_FFN + c, i, GROUP)
                    row_product(N_FFN + c, ch, cl, 0, FFN_BANKS[c - 8], True, False, signal=False, ks=range(3))
                pe.wait_ge(S("gated_lo").sem, i * 4 + 4)
                for c in (8, 9):
                    row_product(N_FFN + c, ch, cl, 0, FFN_BANKS[c - 8], False, True, ks=range(3, 4))
                for c in (10, 11):
                    ready(N_FFN + c, i, GROUP)
                    if c == 11:
                        pe.wait_ge(S("ffn_added").sem, i * 8 + 2)
                    row_product(N_FFN + c, ch, cl, 0, FFN_BANKS[c - 8], True, True)


MEM_BANKS = (0, 1, 2, 3, 4, 5, 6, 0)
X_BANKS = (0, 1, 2, 3, 6, 7, 0, 1)
FFN_BANKS = (2, 4, 6, 2)
OUT_ORDER = (3, 0, 1, 2)
N_CONSTS = 16 * (1 + 10 + 1 + 3 + 1)
TAKEN_XBC = 11
TAKEN_U = TAKEN_XBC + 16 + 3
N_SSD = 27
N_PAIR = 33


def z_bank(n):
    return n % 3 if n < N_U else (n - N_ZB + 1) % 3


def pair_of(n):
    if N_PAIR <= n < N_PAIR + A_MLA // 2:
        return n - N_PAIR
    if N_ZB <= n < N_OUT:
        return n - N_ZB + A_MLA // 2
    return None


def span(j, t):
    if j >= A_X:
        return t * 256, (t + 1) * 256
    return (0, 128) if t == 0 else (128, 384)


def ssd_exp(h, act, a, S, dec):
    act.wait_ge(S("seg_ready").sem, h + 1)
    a.mark(act.activation(dec[:, h % 4, :], dec[:, h % 4, :], ACT.Exp), S("decay_ready"))


_INS = ['x', 'mem', 'positions', 'norm_mix', 'w_in', 'mla_q_norm', 'mla_w_uq', 'mla_kv_norm', 'mla_w_ukv',
        'mla_out_norm', 'ssm_conv_w', 'ssm_conv_b', 'ssm_dt_bias', 'ssm_a_log', 'ssm_d', 'ssm_norm', 'swa_sinks',
        'swa_out_norm', 'w_out', 'norm_cross', 'norm_mem', 'cross_wq', 'cross_wkv', 'cross_wo', 'norm_ffn',
        'ffn_w_up', 'ffn_conv_w', 'ffn_conv_b', 'ffn_w_down', 'norm_final']


def kernel(**inputs):
    import numpy as _np
    import concourse.bacc as _bacc
    from concourse import mybir as _mybir
    from concourse.bass_utils import run_bass_kernel_spmd as _run

    nc = _bacc.Bacc("TRN2", target_bir_lowering=False, num_devices=1)
    arrays, args = {}, []
    for name in _INS:
        arr = _np.ascontiguousarray(inputs[name])
        arrays[f"in_{name}_dram"] = arr
        args.append(nc.dram_tensor(f"in_{name}_dram", arr.shape, _mybir.dt.from_np(arr.dtype), kind="ExternalInput").ap())
    arrays["table_dram"] = constant_table()
    args.append(nc.dram_tensor("table_dram", (P, C_ALL), F32, kind="ExternalInput").ap())
    args.append(nc.dram_tensor("out_0_dram", (1, T, D), F32, kind="ExternalOutput").ap())
    encoder(nc, *args)
    r = _run(nc, [arrays], core_ids=[0])
    return r.results[0]["out_0_dram"]
```

```python
from contextlib import ExitStack

import numpy as np
import concourse.bass as bass
from concourse import mybir

F32, F32R, I32 = mybir.dt.float32, mybir.dt.float32r, mybir.dt.int32
ALU, ACT, AX = mybir.AluOpType, mybir.ActivationFunctionType, mybir.AxisListType

P = 128
T = 256
TT = T // P
D = 2048
KD = D // P
M = 256
EPS = 1e-6
NEG = -1e30
FF = 5632
FT = FF // P
RING = 3
CH = 2048

MLA_H, NOPE, ROPE, VD = 6, 128, 64, 128
SSM_H = 12
SWA_H, SWA_D = 8, 64
X_H, X_D = 4, 128

COL_KR, COL_Z, COL_XBC, COL_DT, COL_Q = 768, 832, 1600, 2880, 2892

N_XK, N_XV, N_CQ, N_KRDT, N_XBC, N_QKV, N_ZA, N_U, N_ZB, N_OUT, N_WQ, N_WO, N_FFN = 0, 4, 8, 14, 15, 25, 31, 34, 38, 41, 57, 61, 65
GROUP = 12
GROUPS = FT // 4

V_MIX, V_CROSS, V_FFN, V_CQ, V_CKV, V_MLA, V_SSM, V_SWA, V_CB = 0, 16, 32, 48, 52, 54, 60, 66, 70
V_ROWS_A = 80
V_CW = V_ROWS_A
V_FW = V_CW + 40
V_FB = V_FW + 3 * 2 * FT
V_MEM = V_FB + 2 * FT
V_ALL = V_MEM + 16

C_ID, C_ONE, C_MLA, C_SWA, C_CAUSAL, C_INV, C_SGN = 0, 128, 256, 640, 1024, 1408, 1409
C_ALL = 1410

A_MLA, A_X = SWA_H, SWA_H + MLA_H


def constant_table():
    c = np.zeros((P, C_ALL), np.float32)
    c[:, C_ID:C_ID + P] = np.eye(P)
    c[:, C_ONE:C_ONE + P] = 1.0
    q = np.arange(P)
    for base, window in ((C_MLA, 99), (C_SWA, 2)):
        for t, (lo, nk) in enumerate(((0, P), (P, T))):
            qc, kc = (t * P + q)[:, None] // 64, np.arange(nk)[None, :] // 64
            c[:, base + lo:base + lo + nk] = np.where((kc <= qc) & (kc > qc - window), 0.0, NEG)
    j, i = q[:, None], np.arange(T)[None, :]
    c[:, C_CAUSAL:C_CAUSAL + T] = i >= j
    c[:, C_CAUSAL + T:C_CAUSAL + T + P] = i[:, :P] >= j
    freq = (np.float32(10000.0) ** (-np.arange(0, ROPE, 2, dtype=np.float32) / np.float32(ROPE))).astype(np.float32)
    c[:, C_INV] = np.tile(freq, 4)
    c[:, C_SGN] = np.where(q % 64 < 32, -1.0, 1.0)
    return c


def dmas_of(n):
    return {N_KRDT: 2, N_U: 4, N_U + 1: 8, N_U + 2: 6, N_U + 3: 2}.get(n, 1)


def landed(n):
    return 16 * sum(dmas_of(m) for m in range(n % RING, n + 1, RING))


def products(n):
    extra = {N_U: 3, N_U + 1: 3, N_U + 2: 6, N_U + 3: 1}
    return n + 1 + sum(v for m, v in extra.items() if m <= n)


class Signal:

    def __init__(self, sem):
        self.sem, self.n = sem, 0


class Engine:

    def __init__(self, eng):
        self.eng, self.last = eng, None

    def mark(self, ins, signal):
        ins.then_inc(signal.sem, 1)
        signal.n = signal.n + 1
        self.last = signal

    def settle(self):
        self.eng.wait_ge(self.last.sem, self.last.n)


def encoder(nc, x, mem, positions, norm_mix, w_in, mla_q_norm, mla_w_uq, mla_kv_norm, mla_w_ukv, mla_out_norm,
            ssm_conv_w, ssm_conv_b, ssm_dt_bias, ssm_a_log, ssm_d, ssm_norm, swa_sinks, swa_out_norm, w_out,
            norm_cross, norm_mem, cross_wq, cross_wkv, cross_wo, norm_ffn, ffn_w_up, ffn_conv_w, ffn_conv_b,
            ffn_w_down, norm_final, table, out):
    ctx = ExitStack()
    with ctx:
        def sb(name, shape, dt=F32):
            return ctx.enter_context(nc.sbuf_tensor(name, shape, dt))

        signals = {}

        def S(name):
            if name not in signals:
                signals[name] = Signal(ctx.enter_context(nc.semaphore(name)))
            return signals[name]

        raw = sb("raw", [P, RING, CH])
        hi = sb("hi", [P, RING, CH], F32R)
        lo = sb("lo", [P, RING, CH], F32R)
        uh = sb("uh", [P, KD, T], F32R)
        ul = sb("ul", [P, KD, T], F32R)
        ch = sb("ch", [P, 6, T], F32R)
        cl = sb("cl", [P, 6, T], F32R)
        tab = sb("tab", [P, C_ALL])
        vecs = sb("vecs", [P, V_ALL])
        small = sb("small", [P, 112])
        arena = sb("arena", [P, 20400])
        bank = [ctx.enter_context(nc.psum_tensor(f"bank{i}", [P, 512], F32)) for i in range(8)]

        ident, ones = tab[:, C_ID:C_ID + P], tab[:, C_ONE:C_ONE + P]

        def at(off, *shape):
            size = int(np.prod(shape))
            v = arena[:, off:off + size]
            if len(shape) == 2:
                v = v.rearrange("p (a b) -> p a b", b=shape[1])
            if len(shape) == 3:
                v = v.rearrange("p (a b c) -> p a b c", b=shape[1], c=shape[2])
            return v

        kxT = at(0, X_H, M)
        vx = at(1024, TT, 512)
        cosT, sinT = at(2048, T), at(2304, T)
        o_swa = at(2560, 4, T)
        dt_rows = at(2560, 4, T)
        acum = at(3584, T)
        krT = at(3840, T)
        convraw, convacc = at(4096, RING, T), at(4864, RING, T)
        o_mla = at(5632, MLA_H, T)
        sq_cq, sq_ckv = at(5632, 4 * T), at(6656, 2 * T)
        cq_raw = at(7168, 6, T)
        yT = at(7168, 6, T)
        swa_q, swa_k, swa_v, swa_kswap = at(8704, 4, T), at(9728, T), at(9984, T), at(10240, T)
        sq_swa = at(8704, 4 * T)
        zT = at(4096, 6, T)
        v_tok = at(10496, TT, P)
        ssb = at(10752, 2, 512)
        pts = at(11776, 2, 512)
        rtmp_a, rtmp_b = at(12800, 3, T), at(10752, 3, T)
        xbcT = at(13568, 10, T)
        x_tok = at(16128, TT, 768)
        cbm = at(17664, 2, 384)
        dec = at(18432, 4, 384)
        qn = at(13568, MLA_H, T)
        kn = at(15104, MLA_H, T)
        vm = at(16640, TT, MLA_H * VD)
        qr = at(18176, 3, T)
        rot = at(18944, T)
        sq_mla, sq_ssm = at(13568, 6 * T), at(11776, 6 * T)
        mems, xs, junk = at(2560, TT, D), at(6656, TT, D), at(10752, D)
        vrows = at(12800, 6, P)
        posi = at(13568, T)
        ang, kk, kl, tmp4 = at(13824, T), at(14080, T), at(14336, T), at(14592, T)
        mem_rows = at(14848, P)
        junk_v = at(15104, D)
        mem_diag, x_diag = at(17152, TT, P), at(17408, TT, P)
        mem_scale = at(17664, T)
        hres = at(2048 + 14000, TT, D)
        hwork = at(6144, TT, D)
        hjunk = at(2048, 4, 512)
        q_x = at(4096, X_H, T)
        craw, cacc = at(10240, 4, T), at(11264, 4, T)
        sil, prod = at(12288, T), at(12544, T)
        gfin = at(13568, D)
        hf_diag, hf_scale = at(12800, TT, P), at(15616, T)

        s_ss, s_var, s_std, s_r, s_t = 0, 2, 4, 6, 8
        s_dcol, s_sink, s_nsink = 10, 16, 24
        s_cols = 32
        s_dall = 96
        stat = sb("stat", [P, 2, 8])
        pick = sb("pick", [SSM_H, SSM_H], F32R)
        acum_h = sb("acum_h", [SSM_H, T], F32R)
        acum_l = sb("acum_l", [SSM_H, T], F32R)
        mem_r = sb("mem_r", [P, TT])
        mixed = sb("mixed", [P, 4, 6])
        parts = sb("parts", [P, TT, 4])
        row12 = sb("row12", [SSM_H, 4])
        assert arena.shape[1] >= 18176 + 768 + 256

        block = ctx.enter_context(nc.Block())

        @block.sync
        def _(sp):
            def raw_free(n):
                sp.wait_ge(S("lo_ready").sem, n - RING + 1)

            def load(n, src, shape, slot=None, off=0):
                slot = n % RING if slot is None else slot
                size = int(np.prod(shape))
                dst = raw[:, slot, off:off + size]
                if len(shape) == 2:
                    dst = dst.rearrange("p (a b) -> p a b", b=shape[1])
                    sp.dma_start(dst, src).then_inc(S(f"raw_landed{slot}").sem, 16)
                else:
                    dst = dst.rearrange("p (a b c) -> p a b c", b=shape[1], c=shape[2])
                    sp.dma_start(dst, src).then_inc(S(f"raw_landed{slot}").sem, 16)

            def rows(w):
                return w[0].rearrange("(k p) c -> p k c", p=P)

            for q in range(4):
                sp.dma_start(mems[:, :, q * 512:(q + 1) * 512],
                             mem[0].rearrange("(t p) d -> p t d", p=P)[:, :, q * 512:(q + 1) * 512]).then_inc(S(f"mem_landed{q}").sem, 16)
                if q % 2:
                    half = q // 2
                    sp.dma_start(raw[:, 0, half * CH // 2:(half + 1) * CH // 2].rearrange("p (a b) -> p a b", b=P),
                                 rows(cross_wkv)[:, half * KD // 2:(half + 1) * KD // 2, 0:P]).then_inc(
                                     S("raw_landed0" if half else "first_landed").sem, 16)
            for q in range(4):
                sp.wait_ge(S(f"mem_landed{q}").sem, 16)
            load(1, rows(cross_wkv)[:, :, P:2 * P], (KD, P))
            load(2, rows(cross_wkv)[:, :, 2 * P:3 * P], (KD, P))
            raw_free(3)
            load(3, rows(cross_wkv)[:, :, 3 * P:4 * P], (KD, P))
            vectors = S("vectors_landed").sem
            sp.dma_start(tab[:, 2 * P:], table[:, 2 * P:]).then_inc(vectors, 16)
            at_row = 0
            for v, n in ((norm_mix, 16), (norm_cross, 16), (norm_ffn, 16), (mla_q_norm, 4),
                         (mla_kv_norm, 2), (mla_out_norm, 6), (ssm_norm, 6), (swa_out_norm, 4), (ssm_conv_b, 10)):
                sp.dma_start(vrows[at_row:at_row + n, 0, :], v.rearrange("l (r c) -> (l r) c", c=P)).then_inc(vectors, 16)
                at_row += n
            sp.dma_start(vrows[0:40, 1, :], ssm_conv_w[0].rearrange("k (r c) -> (k r) c", c=P)).then_inc(vectors, 16)
            for k in range(3):
                sp.dma_start(vrows[0:2 * FT, 2 + k, :], ffn_conv_w[0, k].rearrange("(r c) -> r c", c=P)).then_inc(vectors, 16)
            sp.dma_start(vrows[0:2 * FT, 5, :], ffn_conv_b[0].rearrange("(r c) -> r c", c=P)).then_inc(vectors, 16)
            for t in range(TT):
                sp.dma_start(xs[:, t, :], x[0, t * P:(t + 1) * P, :]).then_inc(S("x_landed").sem, 16)
            sp.dma_start(posi.bitcast(I32), positions[0].partition_broadcast(P)).then_inc(S("pos_landed").sem, 16)
            sp.dma_start(small[:, s_dall:s_dall + SSM_H], ssm_d[0].partition_broadcast(P)).then_inc(S("params_landed").sem, 16)
            sp.dma_start(small[:, s_sink:s_sink + SWA_H], swa_sinks[0].partition_broadcast(P)).then_inc(S("params_landed").sem, 16)
            sp.dma_start(row12[:, 0:1], ssm_dt_bias.rearrange("l h -> h l")).then_inc(S("params_landed").sem, 16)
            sp.dma_start(row12[:, 1:2], ssm_a_log.rearrange("l h -> h l")).then_inc(S("params_landed").sem, 16)

            for g in range(4):
                raw_free(N_XV + g)
                load(N_XV + g, rows(cross_wkv)[:, 4 * g:4 * g + 4, 512:1024], (4, 512))

            def load_columns(first, count, w, col):
                v = rows(w)
                with sp.Fori(0, count // RING) as i:
                    for s in range(RING):
                        n = first + s
                        sp.wait_ge(S("lo_ready").sem, i * RING + (n - RING + 1))
                        load(n, v[:, :, bass.ds(i * (RING * P) + (col + s * P), P)], (KD, P))
                for s in range(count // RING * RING, count):
                    raw_free(first + s)
                    load(first + s, v[:, :, col + s * P:col + (s + 1) * P], (KD, P))

            load_columns(N_CQ, 6, w_in, 0)
            raw_free(N_KRDT)
            slot = raw[:, N_KRDT % RING, :].rearrange("p (k c) -> p k c", c=P)
            for lo_, hi_, col in ((0, ROPE, COL_KR), (ROPE, ROPE + SSM_H, COL_DT)):
                sp.dma_start(slot[:, :, lo_:hi_], rows(w_in)[:, :, col:col + hi_ - lo_]).then_inc(
                    S(f"raw_landed{N_KRDT % RING}").sem, 16)
            load_columns(N_XBC, 10, w_in, COL_XBC)
            load_columns(N_QKV, 6, w_in, COL_Q)
            load_columns(N_ZA, 3, w_in, COL_Z)
            uq = mla_w_uq[0].rearrange("(k p) (h e) -> p k h e", p=P, e=NOPE + ROPE)
            ukv = mla_w_ukv[0].rearrange("(k p) (h e) -> p k h e", p=P, e=NOPE + VD)

            def load4(n, parts):
                raw_free(n)
                off = 0
                for src, k, h, e in parts:
                    dst = raw[:, n % RING, off:off + k * h * e].rearrange("p (k h e) -> p k h e", h=h, e=e)
                    for kt in range(k):
                        sp.dma_start(dst[:, kt], src[:, kt]).then_inc(S(f"raw_landed{n % RING}").sem, 16)
                    off += k * h * e

            load4(N_U, [(uq[:, :, 0:4, 0:NOPE], 4, 4, NOPE)])
            load4(N_U + 1, [(uq[:, :, 4:6, 0:NOPE], 4, 2, NOPE), (uq[:, :, 0:4, NOPE:], 4, 4, ROPE)])
            load4(N_U + 2, [(uq[:, :, 4:6, NOPE:], 4, 2, ROPE), (ukv[:, :, :, 0:NOPE], 2, 6, NOPE)])
            load4(N_U + 3, [(ukv[:, :, :, NOPE:], 2, 6, VD)])
            load_columns(N_ZB, 3, w_in, COL_Z + 3 * P)
            for m, (g, cb) in enumerate(OUT_CHUNKS):
                raw_free(N_OUT + m)
                load(N_OUT + m, rows(w_out)[:, 4 * g:4 * g + 4, cb * 512:(cb + 1) * 512], (4, 512))
                if m == 2:
                    sp.wait_ge(S("out_done").sem, A_X)
                    for t in range(TT):
                        sp.dma_start(hres[:, t, :], x[0, t * P:(t + 1) * P, :]).then_inc(S("residual_landed").sem, 16)
            for h in range(X_H):
                raw_free(N_WQ + h)
                load(N_WQ + h, rows(cross_wq)[:, :, h * P:(h + 1) * P], (KD, P))
            for cb in range(4):
                raw_free(N_WO + cb)
                load(N_WO + cb, rows(cross_wo)[:, :, cb * 512:(cb + 1) * 512], (4, 512))
            sp.wait_ge(S("mix_added").sem, 24)
            sp.dma_start(gfin[:, :], norm_final.partition_broadcast(P)).then_inc(S("gfin_landed").sem, 16)
            with sp.Fori(0, GROUPS) as i:
                for c in range(GROUP):
                    n = N_FFN + c
                    sp.wait_ge(S("lo_ready").sem, i * GROUP + (n - RING + 1))
                    if c < 8:
                        col = (c % 2) * FF + (c // 2) * P
                        load(n, rows(ffn_w_up)[:, :, bass.ds(i * (4 * P) + col, P)], (KD, P))
                    else:
                        cb = c - 8
                        load(n, rows(ffn_w_down)[:, bass.ds(i * 4, 4), cb * 512:(cb + 1) * 512], (4, 512))
            for cb in range(4):
                for t in range(TT):
                    sp.wait_ge(S(f"out_ready{t}").sem, cb + 1)
                    sp.dma_start(out[0, t * P:(t + 1) * P, cb * 512:(cb + 1) * 512],
                                 hwork[:, t, cb * 512:(cb + 1) * 512]).then_inc(S("out_stored").sem, 16)
            sp.wait_ge(S("out_stored").sem, 16 * TT * 4)

        def landed_at(n, i, per):
            return landed(n) if i is None else i * (16 * per // RING) + landed(n)

        @block.scalar
        def _(act):
            a = Engine(act)

            def split(n, i=None, per=GROUP):
                act.wait_ge(S(f"raw_landed{n % RING}").sem, landed_at(n, i, per))
                if i is not None or n >= RING:
                    before = products(n - RING)
                    act.wait_ge(S("products_done").sem, before if i is None else i * per + before)
                a.mark(act.copy(hi[:, n % RING, :], raw[:, n % RING, :]), S("hi_ready"))

            def token_root(name):
                act.wait_ge(S(f"{name}_var").sem, 1)
                a.mark(act.activation(small[:, s_std:s_std + 2], small[:, s_var:s_var + 2], ACT.Sqrt), S(f"{name}_std"))

            def block_squares(name, added, cb, first):
                for t in range(TT):
                    act.wait_ge(S(added).sem, first + t)
                    if cb >= 2:
                        a.settle()
                    a.mark(act.activation(hjunk[:, (TT * cb + t) % 4, :], hres[:, t, cb * 512:(cb + 1) * 512], ACT.Square,
                                          accum_out=parts[:, t, cb:cb + 1]), S(f"{name}_parts"))

            def mixed_root(name, c0, c1):
                act.wait_ge(S(f"{name}_var").sem, 1)
                a.mark(act.activation(mixed[:, 1, c0:c1], mixed[:, 0, c0:c1], ACT.Sqrt), S(f"{name}_std"))

            def mixer_hi(name, src, n, dst_h, g_col):
                a.settle()
                for k in range(n):
                    a.mark(act.activation(dst_h[:, k, :], src[:, k, :], ACT.Copy,
                                          scale=vecs[:, g_col + k:g_col + k + 1]), S(f"{name}_hi"))

            def token_hi(name, g, g_col, b):
                act.wait_ge(S(f"{name}_turned").sem, g + 1)
                for k in (2 * g, 2 * g + 1):
                    a.mark(act.activation(uh[:, k, :], bank[b][:, (k % 2) * T:(k % 2 + 1) * T], ACT.Copy,
                                          scale=vecs[:, g_col + k:g_col + k + 1]), S(f"{name}_hi"))

            def squares(name, src, sq, n):
                a.settle()
                a.mark(act.activation(sq[:, 0:n * T], src.rearrange("p a b -> p (a b)"), ACT.Square), S(f"{name}_sq"))

            def root(name, tmp):
                act.wait_ge(S(f"{name}_var").sem, 1)
                a.mark(act.activation(tmp[:, 1, :], tmp[:, 0, :], ACT.Sqrt), S(f"{name}_std"))

            def feature_hi(name, src, n, dst_h, g_col):
                act.wait_ge(S(f"{name}_scaled").sem, 1)
                for k in range(n):
                    a.mark(act.activation(dst_h[:, k, :], src[:, k, :], ACT.Copy,
                                          scale=vecs[:, g_col + k:g_col + k + 1]), S(f"{name}_hi"))

            def attend_exp(j):
                act.wait_ge(S("negmax_ready").sem, j + 1)
                st = stat[:, j % 2, :]
                if j < A_MLA:
                    for t in range(TT):
                        act.activation(st[:, 4 + t:5 + t], small[:, s_sink + j:s_sink + j + 1], ACT.Exp, bias=st[:, t:t + 1])
                for t in range(TT):
                    c0, c1 = span(j, t)
                    ins = act.activation(ssb[:, j % 2, c0:c1], ssb[:, j % 2, c0:c1], ACT.Exp,
                                         bias=st[:, t:t + 1], accum_out=st[:, 2 + t:3 + t])
                a.mark(ins, S("exp_done"))

            def attend_turned(j):
                act.wait_ge(S("probsT_done").sem, j + 1)
                if j >= 2:
                    act.wait_ge(S("out_done").sem, j - 1)
                w = 512 if j >= A_X else 384
                a.mark(act.copy(pts[:, j % 2, 0:w], bank[5 + j % 2][:, 0:w]), S("probsT_copied"))

            def attend_out(pair):
                act.wait_ge(S("out_done").sem, 2 * pair + 2)
                if pair < A_MLA // 2:
                    ins = act.copy(o_swa[:, pair, :], bank[7][:, 0:T])
                elif pair < A_X // 2:
                    k = 2 * pair - A_MLA
                    ins = act.copy(o_mla[:, k:k + 2, :], bank[7][:, :].rearrange("p (a b) -> p a b", b=T))
                else:
                    k = 2 * pair - A_X
                    ins = act.copy(ch[:, k:k + 2, :], bank[7][:, :].rearrange("p (a b) -> p a b", b=T))
                a.mark(ins, S("out_copied"))

            def wait_product(n):
                act.wait_ge(S("products_done").sem, products(n))

            def take(n, b, dst):
                wait_product(n)
                a.mark(act.copy(dst, bank[b][:, 0:T]), S("tile_taken"))

            act.dma_start(tab[:, 0:2 * P], table[:, 0:2 * P]).then_inc(S("consts_landed").sem, 16)
            act.dma_start(mem_rows[0:16, :], norm_mem.rearrange("l (r c) -> (l r) c", c=P)).then_inc(S("consts_landed").sem, 16)
            act.wait_ge(S("vecs_turned").sem, 1)
            a.mark(act.copy(vecs[:, V_MEM:V_ALL], bank[7][:, V_MEM:V_ALL]), S("vecs_ready"))
            a.settle()
            for g in range(4):
                token_hi("mem", g, V_MEM, g)
            act.wait_ge(S("first_landed").sem, 16)
            a.mark(act.copy(hi[:, 0, 0:CH // 2], raw[:, 0, 0:CH // 2]), S("first_hi"))
            for g in (4, 5):
                token_hi("mem", g, V_MEM, g)
            act.wait_ge(S("raw_landed0").sem, 16)
            a.mark(act.copy(hi[:, 0, CH // 2:], raw[:, 0, CH // 2:]), S("hi_ready"))
            for g in (6, 7):
                token_hi("mem", g, V_MEM, g)
            split(1)
            a.mark(act.activation(junk, mems[:, 0, :], ACT.Square, accum_out=small[:, s_ss:s_ss + 1]), S("mem_ss"))
            split(2)
            token_root("mem")
            split(3)
            act.wait_ge(S("vecs_turned").sem, 2)
            a.mark(act.copy(vecs[:, 0:V_MEM], bank[3][:, 0:V_MEM]), S("vecs_ready"))
            a.settle()
            act.wait_ge(S("x_landed").sem, 32)
            a.mark(act.activation(junk, xs[:, 0, :], ACT.Square, accum_out=small[:, s_ss:s_ss + 1]), S("x_ss"))
            token_root("x")
            split(4)
            split(5)
            for n in range(N_XV, N_XV + 4):
                if n > N_XV:
                    for g in (2 * (n - N_XV) - 2, 2 * (n - N_XV) - 1):
                        act.wait_ge(S("products_done").sem, products(n - 1))
                        token_hi("x", g, V_MIX, X_BANKS[g])
                split(n + 2)
                if n == N_XV + 1:
                    for f in range(2):
                        act.wait_ge(S("angles_ready").sem, f + 1)
                        a.mark(act.activation((sinT, cosT)[f], (kk, kl)[f], ACT.Sin), S("sincos"))
            wait_product(N_XV + 3)
            for g in (6, 7):
                token_hi("x", g, V_MIX, X_BANKS[g])
            for n in range(N_CQ, N_CQ + 6):
                split(n + 2)
                take(n, n % 3, cq_raw[:, n - N_CQ, :])
            split(N_KRDT + 2)
            wait_product(N_KRDT)
            b = bank[N_KRDT % 3]
            a.mark(act.copy(krT[0:64, :], b[0:64, 0:T]), S("kr_parts"))
            a.mark(act.copy(krT[64:128, :], b[0:64, 0:T]), S("kr_parts"))
            a.mark(act.copy(dt_rows[0:SSM_H, 0, :], b[64:64 + SSM_H, 0:T]), S("tile_taken"))
            squares("cq", cq_raw[:, 0:4, :], sq_cq, 4)
            squares("ckv", cq_raw[:, 4:6, :], sq_ckv, 2)

            def conv_first(n):
                c = n - N_XBC
                wait_product(n)
                if c >= RING:
                    act.wait_ge(S("xbc_ready").sem, c - RING + 1)
                a.mark(act.activation(convacc[:, n % RING, :], bank[n % 3][:, 0:T], ACT.Identity,
                                      scale=vecs[:, V_CW + 30 + c:V_CW + 31 + c], bias=vecs[:, V_CB + c:V_CB + c + 1]), S("conv_first"))
                a.mark(act.copy(convraw[:, n % RING, :], bank[n % 3][:, 0:T]), S("tile_taken"))

            def conv_silu(n):
                c = n - N_XBC
                act.wait_ge(S("conv_done").sem, c + 1)
                a.mark(act.activation(xbcT[:, c, :], convacc[:, n % RING, :], ACT.Silu), S("xbc_ready"))

            def take_x_tok(b):
                act.wait_ge(S("xbc_turned").sem, b + 1)
                for k in range(2):
                    a.mark(act.copy(x_tok[:, :, (2 * b + k) * P:(2 * b + k + 1) * P],
                                    bank[3 + b][:, k * T:(k + 1) * T].rearrange("p (t c) -> p t c", c=P)), S("x_tok_ready"))

            for n in range(N_XBC, N_XBC + 10):
                split(n + 2)
                if n == 16:
                    act.wait_ge(S("dt_abs").sem, 1)
                    a.mark(act.activation(dt_rows[0:SSM_H, 2, :], dt_rows[0:SSM_H, 2, :], ACT.Exp), S("dt_exp"))
                    a.mark(act.activation(row12[:, 2:3], row12[:, 1:2], ACT.Exp), S("a_exp"))
                if n == 18:
                    act.wait_ge(S("dt_w").sem, 1)
                    a.mark(act.activation(dt_rows[0:SSM_H, 3, :], dt_rows[0:SSM_H, 3, :], ACT.Ln), S("dt_ln"))
                if n == 22:
                    root("cq", rtmp_a)
                    root("ckv", rtmp_b)
                if n == 24:
                    feature_hi("cq", cq_raw, 4, ch, V_CQ)
                if n in (22, 23, 24):
                    take_x_tok(n - 22)
                conv_first(n)
                if n > N_XBC:
                    conv_silu(n - 1)
            for n in range(N_QKV, N_QKV + 6):
                split(n + 2)
                if n == N_QKV:
                    conv_silu(n - 1)
                if n == N_QKV + 1:
                    feature_hi("ckv", cq_raw[:, 4:6, :], 2, ch[:, 4:6, :], V_CKV)
                if n >= N_SSD:
                    for h in (2 * (n - N_SSD), 2 * (n - N_SSD) + 1):
                        ssd_exp(h, act, a, S, dec)
                k = n - N_QKV
                if k == 4:
                    wait_product(n)
                    a.mark(act.copy(swa_kswap[0:64, :], bank[n % 3][64:128, 0:T]), S("kr_parts"))
                    a.mark(act.copy(swa_kswap[64:128, :], bank[n % 3][0:64, 0:T]), S("kr_parts"))
                take(n, n % 3, swa_q[:, k, :] if k < 4 else (swa_k, swa_v)[k - 4])

            def pair_step(n):
                old, new = pair_of(n - 1), pair_of(n)
                if old is not None:
                    attend_turned(2 * old)
                    attend_turned(2 * old + 1)
                split(n + 2)
                if new is not None:
                    attend_exp(2 * new)
                    attend_exp(2 * new + 1)
                if old is not None:
                    attend_out(old)

            def take_u(n):
                first = products(n - 1)
                dsts = {0: [qn[:, h, :] for h in range(4)], 1: [qn[:, 4, :], qn[:, 5, :], qr[:, 0, :], qr[:, 1, :]],
                        2: [qr[:, 2, :]] + [kn[:, h, :] for h in range(6)]}[n - N_U]
                act.wait_ge(S("y_taken").sem, 6)
                for m, dst in enumerate(dsts):
                    act.wait_ge(S("products_done").sem, first + m + 1)
                    a.mark(act.copy(dst, bank[(first + m) % 3][:, 0:T]), S("tile_taken"))

            for n in range(N_ZA, N_OUT + 1):
                if n >= N_PAIR:
                    pair_step(n)
                else:
                    split(n + 2)
                if n < N_SSD + 6:
                    for h in (2 * (n - N_SSD), 2 * (n - N_SSD) + 1):
                        ssd_exp(h, act, a, S, dec)
                if n == 38:
                    squares("swa", o_swa, sq_swa, 4)
                if n == 39:
                    mixer_hi("swa", o_swa, 4, ch, V_SWA)
                if n < N_U:
                    take(n, z_bank(n), zT[:, n - N_ZA, :])
                elif n < N_U + 3:
                    take_u(n)
                elif N_ZB <= n < N_OUT:
                    take(n, z_bank(n), zT[:, 3 + n - N_ZB, :])
                if n == 40:
                    a.settle()
                    a.mark(act.activation(zT[:, :, :], zT[:, :, :], ACT.Silu), S("gate_ready"))
            squares("mla", o_mla, sq_mla, 6)
            act.wait_ge(S("products_done").sem, products(N_OUT - 1))
            mixer_hi("mla", o_mla, 6, uh[:, 10:16, :], V_MLA)
            for n in range(N_OUT + 1, N_OUT + 16):
                cb, step_ = (n - N_OUT - 4) // 3, (n - N_OUT - 4) % 3
                if n == N_OUT + 4:
                    act.wait_ge(S("products_done").sem, products(n - 1))
                    mixer_hi("ssm", yT, 6, ch, V_SSM)
                if n == N_OUT + 1:
                    act.wait_ge(S("y_gated").sem, 1)
                    squares("ssm", yT, sq_ssm, 6)
                split(n + 2)
                if n == N_OUT + 1:
                    mixed_root("heads", 0, 4)
                if n == N_OUT + 2:
                    mixed_root("ssm", 4, 6)
                if cb >= 1 and step_ == 0:
                    block_squares("hx", "mix_added", cb - 1, 9 + 4 * cb - 2)
                if cb >= 1 and step_ == 1:
                    for g in (2 * cb - 2, 2 * cb - 1):
                        token_hi("hx", g, V_CROSS, hx_bank(g))
            split(N_WQ + 2)
            block_squares("hx", "mix_added", 3, 23)
            for g in (6, 7):
                token_hi("hx", g, V_CROSS, hx_bank(g))
            token_root("hx")
            for n in range(N_WQ, N_WQ + 4):
                if n > N_WQ:
                    split(n + 2)
                if n == N_WQ + 3:
                    attend_turned(A_X)
                    attend_turned(A_X + 1)
                if n == N_WQ + 2:
                    attend_exp(A_X)
                    attend_exp(A_X + 1)
                take(n, WQ_BANKS[n - N_WQ], q_x[:, n - N_WQ, :])
            attend_out(A_X // 2)
            attend_exp(A_X + 2)
            attend_exp(A_X + 3)
            attend_turned(A_X + 2)
            attend_turned(A_X + 3)
            attend_out(A_X // 2 + 1)
            for n in range(N_WO, N_WO + 4):
                cb = n - N_WO
                split(n + 2)
                if cb >= 2:
                    for g in (2 * cb - 4, 2 * cb - 3):
                        token_hi("hf", g, V_FFN, g)
                if cb >= 1:
                    block_squares("hf", "cross_added", cb - 1, TT * cb - 1)
            for g in (4, 5):
                token_hi("hf", g, V_FFN, g)
            block_squares("hf", "cross_added", 3, 7)
            for g in (6, 7):
                token_hi("hf", g, V_FFN, g)
            token_root("hf")

            def ffn_group(i, last=False):
                def at_turn(v, per):
                    return i * per + v

                def gated_hi(k):
                    act.wait_ge(S("prod_ready").sem, at_turn(k + 1 + 4, 4))
                    a.mark(act.copy(ch[:, k, :], prod[:, :]), S("gated_hi"))

                def first_tap(c):
                    s, v, k = c % 4, c % 2, c // 2
                    act.wait_ge(S("fconv_raw").sem, at_turn(c + 3, 8))
                    act.wait_ge(S("prod_ready").sem, at_turn(k + 3, 4))
                    tile = at_turn(v * FT + k, 4)
                    a.mark(act.activation(cacc[:, s, :], craw[:, s, :], ACT.Identity,
                                          scale=vecs[:, bass.ds(tile + (V_FW + 2 * 2 * FT), 1)],
                                          bias=vecs[:, bass.ds(tile + V_FB, 1)]), S("fconv_first"))
                    if v == 1:
                        act.wait_ge(S("fconv_done").sem, at_turn(2 * k + 1, 8))
                        a.mark(act.activation(sil[:, :], cacc[:, s - 1, :], ACT.Silu), S("silu_ready"))
                    elif k > 0:
                        gated_hi(k - 1)

                for c in range(GROUP):
                    if c == 8:
                        first_tap(7)
                        gated_hi(3)
                    if not (last and c >= GROUP - 2):
                        split(N_FFN + c + 2, i, GROUP)
                    if 0 < c < 8:
                        first_tap(c - 1)
            with act.Fori(0, GROUPS - 1) as i:
                ffn_group(i)
            ffn_group(GROUPS - 1, True)
            for cb in range(4):
                block_squares("final", "ffn_added", cb, 8 * (GROUPS - 1) + TT * cb + 1)
            token_root("final")
            act.wait_ge(S("final_r").sem, 1)
            for cb in range(4):
                c = slice(cb * 512, (cb + 1) * 512)
                a.mark(act.activation(hwork[:, 0, c], hwork[:, 0, c], ACT.Copy, scale=small[:, s_r:s_r + 1]), S("out_ready0"))

        @block.vector
        def _(dve):
            d = Engine(dve)
            step = S("vector_step")

            def go(ins, signal=None):
                d.mark(ins, signal or step)
                d.settle()

            def split(n, i=None, per=GROUP):
                v = n + 1
                dve.wait_ge(S("hi_ready").sem, v if i is None else i * per + v)
                if i is not None or n >= RING:
                    before = products(n - RING)
                    dve.wait_ge(S("products_done").sem, before if i is None else i * per + before)
                d.mark(dve.tensor_tensor(lo[:, n % RING, :], raw[:, n % RING, :], hi[:, n % RING, :].bitcast(F32), ALU.subtract),
                       S("lo_ready"))

            def newton(r, v, t, last=None):
                go(dve.tensor_tensor(t, r, r, ALU.mult))
                go(dve.tensor_tensor(t, t, v, ALU.mult))
                go(dve.tensor_scalar(t, t, -0.5, 1.5, ALU.mult, ALU.add))
                go(dve.tensor_tensor(r, r, t, ALU.mult), last)

            def token_rsqrt(name, last=None):
                v, sd = small[:, s_var:s_var + 2], small[:, s_std:s_std + 2]
                r, t_ = small[:, s_r:s_r + 2], small[:, s_t:s_t + 2]
                go(dve.tensor_scalar(v, small[:, s_ss:s_ss + 2], 1.0 / D, EPS, ALU.mult, ALU.add), S(f"{name}_var"))
                dve.wait_ge(S(f"{name}_std").sem, 1)
                go(dve.reciprocal(r, sd))
                newton(r, v, t_, last)

            def tile_squares(name, src):
                go(dve.tensor_tensor_reduce(junk_v, src[:, 1, :], src[:, 1, :], 1.0, 0.0, ALU.mult, ALU.add,
                                            small[:, s_ss + 1:s_ss + 2]))
                dve.wait_ge(S(f"{name}_ss").sem, 1)

            def sum_parts(name):
                dve.wait_ge(S(f"{name}_parts").sem, 8)
                go(dve.tensor_reduce(small[:, s_ss:s_ss + 2], parts[:, :, :], AX.X, ALU.add))

            def diagonal(name, diag):
                for t in range(TT):
                    d.mark(dve.tensor_scalar(diag[:, t, :], ident, small[:, s_r + t:s_r + t + 1], None, ALU.mult), S(f"{name}_diagonal"))

            def token_lo(name, g, g_col, b):
                dve.wait_ge(S(f"{name}_hi").sem, 2 * g + 2)
                for k in (2 * g, 2 * g + 1):
                    d.mark(dve.scalar_tensor_tensor(out=ul[:, k, :], in0=bank[b][:, (k % 2) * T:(k % 2 + 1) * T],
                                                    scalar=vecs[:, g_col + k:g_col + k + 1], in1=uh[:, k, :].bitcast(F32),
                                                    op0=ALU.mult, op1=ALU.subtract), S(f"{name}_lo"))

            def feature_var(name, b, tmp, dim):
                dve.wait_ge(S(f"{name}_ss").sem, 1)
                go(dve.tensor_scalar(tmp[:, 0, :], bank[b][:, 0:T], 1.0 / dim, EPS, ALU.mult, ALU.add), S(f"{name}_var"))

            def feature_scale(name, src, n, tmp):
                dve.wait_ge(S(f"{name}_std").sem, 1)
                go(dve.reciprocal(tmp[:, 1, :], tmp[:, 1, :]))
                newton(tmp[:, 1, :], tmp[:, 0, :], tmp[:, 2, :])
                go(dve.tensor_tensor(src, src, tmp[:, 1, :].unsqueeze(1).to_broadcast([P, n, T]), ALU.mult), S(f"{name}_scaled"))

            def feature_lo(name, src, n, dst_h, dst_l, g_col):
                dve.wait_ge(S(f"{name}_hi").sem, n)
                for k in range(n):
                    d.mark(dve.scalar_tensor_tensor(out=dst_l[:, k, :], in0=src[:, k, :], scalar=vecs[:, g_col + k:g_col + k + 1],
                                                    in1=dst_h[:, k, :].bitcast(F32), op0=ALU.mult, op1=ALU.subtract), S(f"{name}_lo"))

            def attend_mask(j):
                b, s, st = bank[3 + j % 2], ssb[:, j % 2, :], stat[:, j % 2, :]
                w = 512 if j >= A_X else 384
                dve.wait_ge(S("scores_done").sem, j + 1)
                if j >= 2:
                    dve.wait_ge(S("probsT_done").sem, j - 1)
                if j < A_X:
                    col, scale = (C_SWA, SWA_D ** -0.5) if j < A_MLA else (C_MLA, (NOPE + ROPE) ** -0.5)
                    go(dve.scalar_tensor_tensor(out=s[:, 0:w], in0=b[:, 0:w], scalar=scale, in1=tab[:, col:col + w],
                                                op0=ALU.mult, op1=ALU.add), S("scores_taken"))
                else:
                    for t in range(TT):
                        ins = dve.tensor_scalar(s[:, t * T:(t + 1) * T], b[:, t * T:(t + 1) * T], small[:, s_t + t:s_t + t + 1], None, ALU.mult)
                        d.mark(ins, S("scores_taken") if t == 1 else step)
                    d.settle()
                for t in range(TT):
                    c0, c1 = span(j, t)
                    ins = dve.tensor_reduce(st[:, t:t + 1], s[:, c0:c1], AX.X, ALU.max, negate=True)
                    d.mark(ins, S("negmax_ready") if j >= A_MLA and t == 1 else step)
                if j < A_MLA:
                    d.settle()
                    d.mark(dve.tensor_scalar(st[:, 0:2], st[:, 0:2], small[:, s_nsink + j:s_nsink + j + 1], None, ALU.min), S("negmax_ready"))

            def attend_norm(j):
                s, st = ssb[:, j % 2, :], stat[:, j % 2, :]
                dve.wait_ge(S("exp_done").sem, j + 1)
                if j < A_MLA:
                    go(dve.tensor_tensor(st[:, 2:4], st[:, 2:4], st[:, 4:6], ALU.add))
                go(dve.reciprocal(st[:, 6:8], st[:, 2:4]))
                for t in range(TT):
                    c0, c1 = span(j, t)
                    ins = dve.tensor_scalar(s[:, c0:c1], s[:, c0:c1], st[:, 6 + t:7 + t], None, ALU.mult)
                    d.mark(ins, S("probs_ready") if t == 1 else step)

            dve.wait_ge(S("vecs_ready").sem, 1)
            for g in range(4):
                token_lo("mem", g, V_MEM, g)
            dve.wait_ge(S("first_hi").sem, 1)
            d.mark(dve.tensor_tensor(lo[:, 0, 0:CH // 2], raw[:, 0, 0:CH // 2], hi[:, 0, 0:CH // 2].bitcast(F32), ALU.subtract),
                   S("first_lo"))
            for g in (4, 5):
                token_lo("mem", g, V_MEM, g)
            dve.wait_ge(S("hi_ready").sem, 1)
            d.mark(dve.tensor_tensor(lo[:, 0, CH // 2:], raw[:, 0, CH // 2:], hi[:, 0, CH // 2:].bitcast(F32), ALU.subtract),
                   S("lo_ready"))
            for g in (6, 7):
                token_lo("mem", g, V_MEM, g)
            split(1)
            tile_squares("mem", mems)
            split(2)
            token_rsqrt("mem")
            diagonal("mem", mem_diag)
            go(dve.tensor_copy(mem_r[:, :], small[:, s_r:s_r + 2]))
            split(3)
            dve.wait_ge(S("mem_spread").sem, 1)
            go(dve.tensor_copy(mem_scale, bank[4][:, 0:T]))

            def take_key(n):
                dve.wait_ge(S("products_done").sem, products(n))
                d.mark(dve.tensor_tensor(kxT[:, n, :], bank[KEY_BANKS[n]][:, 0:T], mem_scale, ALU.mult), S("key_taken"))

            dve.wait_ge(S("x_landed").sem, 32)
            take_key(0)
            tile_squares("x", xs)
            token_rsqrt("x")
            diagonal("x", x_diag)
            take_key(1)
            split(4)
            take_key(2)
            split(5)
            take_key(3)
            dve.wait_ge(S("pos_landed").sem, 16)
            dve.wait_ge(S("vectors_landed").sem, N_VECTORS)
            go(dve.tensor_copy(ang, posi.bitcast(I32)))
            go(dve.tensor_scalar(ang, ang, tab[:, C_INV:C_INV + 1], None, ALU.mult))
            magic = 1.5 * 2.0 ** 23
            go(dve.tensor_scalar(kk, ang, float(1 / (2 * np.pi)), magic, ALU.mult, ALU.add))
            go(dve.tensor_scalar(kk, kk, -magic, None, ALU.add))
            go(dve.tensor_scalar(kl, kk, magic * 2.0 ** 12, None, ALU.add))
            go(dve.tensor_scalar(kl, kl, -magic * 2.0 ** 12, None, ALU.add))
            go(dve.tensor_tensor(kk, kk, kl, ALU.subtract))
            rest = 2 * np.pi
            for _ in range(4):
                e = 2.0 ** (np.floor(np.log2(rest)) - 10)
                part = float(np.floor(rest / e) * e)
                rest -= part
                go(dve.scalar_tensor_tensor(out=ang, in0=kl, scalar=-part, in1=ang, op0=ALU.mult, op1=ALU.add))
                go(dve.scalar_tensor_tensor(out=ang, in0=kk, scalar=-part, in1=ang, op0=ALU.mult, op1=ALU.add))
            lim = 3.1415925
            go(dve.tensor_scalar(kk, ang, lim, -lim, ALU.min, ALU.max), S("angles_ready"))
            go(dve.tensor_scalar(tmp4, ang, float(np.pi / 2), float(-2 * np.pi), ALU.is_gt, ALU.mult))
            go(dve.scalar_tensor_tensor(out=kl, in0=ang, scalar=float(np.pi / 2), in1=tmp4, op0=ALU.add, op1=ALU.add))
            go(dve.tensor_scalar(kl, kl, lim, -lim, ALU.min, ALU.max), S("angles_ready"))
            for n in range(N_XV, N_XV + 4):
                if n > N_XV:
                    for g in (2 * (n - N_XV) - 2, 2 * (n - N_XV) - 1):
                        dve.wait_ge(S("products_done").sem, products(n - 1))
                        token_lo("x", g, V_MIX, X_BANKS[g])
                split(n + 2)
                if n == N_XV + 2:
                    dve.wait_ge(S("sincos").sem, 1)
                    go(dve.tensor_scalar(sinT, sinT, tab[:, C_SGN:C_SGN + 1], None, ALU.mult))
            dve.wait_ge(S("products_done").sem, products(N_XV + 3))
            for g in (6, 7):
                token_lo("x", g, V_MIX, X_BANKS[g])
            for t in range(TT):
                d.mark(dve.tensor_scalar(vx[:, t, :], bank[4 + t][:, :], mem_r[:, t:t + 1], None, ALU.mult), S("vx_ready"))
            dve.wait_ge(S("params_landed").sem, 16 * 4)
            for half in range(2):
                rows_ = slice(64 * half, 64 * half + 64)
                go(dve.tensor_copy(small[rows_, s_dcol:s_dcol + 6],
                                   small[rows_, s_dall:s_dall + SSM_H].rearrange("p (t s) -> p t s", s=2)[:, :, half]))
            go(dve.tensor_scalar(small[:, s_nsink:s_nsink + SWA_H], small[:, s_sink:s_sink + SWA_H], -1.0, None, ALU.mult))

            for n in range(N_CQ, N_CQ + 6):
                split(n + 2)
            split(N_KRDT + 2)

            def conv_rest(n):
                c = n - N_XBC
                dve.wait_ge(S("tile_taken").sem, TAKEN_XBC + c + 1)
                s = n % RING
                for k in (1, 2, 3):
                    col = V_CW + 10 * (3 - k) + c
                    go(dve.scalar_tensor_tensor(out=convacc[:, s, k:T], in0=convraw[:, s, 0:T - k], scalar=vecs[:, col:col + 1],
                                                in1=convacc[:, s, k:T], op0=ALU.mult, op1=ALU.add),
                       S("conv_done") if k == 3 else None)

            def rotate(tile):
                for q in range(4):
                    d.mark(dve.tensor_copy(rot[32 * q:32 * q + 32, :], tile[32 * (q ^ 1):32 * (q ^ 1) + 32, :]), step)
                d.settle()
                go(dve.tensor_tensor(rot, rot, sinT, ALU.mult))
                go(dve.tensor_tensor(tile, tile, cosT, ALU.mult))
                go(dve.tensor_tensor(tile, tile, rot, ALU.add), S("rotated"))

            H = slice(0, SSM_H)
            r0, r1, r2, r3 = (dt_rows[H, k, :] for k in range(4))
            for n in range(N_XBC, N_XBC + 10):
                split(n + 2)
                if n == 15:
                    dve.wait_ge(S("tile_taken").sem, TAKEN_XBC)
                    go(dve.tensor_scalar(r0, r0, row12[:, 0:1], None, ALU.add))
                    go(dve.tensor_scalar(r2, r0, -1.0, None, ALU.mult))
                    go(dve.tensor_tensor(r2, r2, r0, ALU.min), S("dt_abs"))
                    go(dve.tensor_scalar(r0, r0, 0.0, None, ALU.max))
                if n == 17:
                    dve.wait_ge(S("dt_exp").sem, 1)
                    go(dve.tensor_scalar(r3, r2, 1.0, None, ALU.add))
                    go(dve.tensor_scalar(r1, r3, -1.0, None, ALU.add), S("dt_w"))
                    go(dve.tensor_scalar(acum[H, :], r1, 0.0, None, ALU.is_equal))
                    go(dve.tensor_tensor(r1, r1, acum[H, :], ALU.add))
                    go(dve.reciprocal(r1, r1))
                if n == 19:
                    dve.wait_ge(S("dt_ln").sem, 1)
                    go(dve.tensor_tensor(r3, r3, acum[H, :], ALU.add))
                    go(dve.tensor_tensor(r3, r3, r1, ALU.mult))
                    go(dve.tensor_tensor(r3, r3, r2, ALU.mult))
                    go(dve.tensor_tensor(r0, r0, r3, ALU.add))
                if n == 20:
                    dve.wait_ge(S("a_exp").sem, 1)
                    go(dve.tensor_scalar(r1, r0, row12[:, 2:3], -1.0, ALU.mult, ALU.mult))
                    for t in range(TT):
                        go(dve.tensor_tensor_scan(acum[H, t * P:(t + 1) * P], tab[H, C_ONE:C_ONE + P], r1[:, t * P:(t + 1) * P], 0.0,
                                                  ALU.mult, ALU.add))
                    go(dve.tensor_scalar(r2, acum[H, :], -1.0, None, ALU.mult))
                    go(dve.tensor_scalar(r3[:, 0:P], r2[:, 0:P], acum[H, P - 1:P], None, ALU.add), S("dt_rows_ready"))
                if n == 21:
                    feature_var("cq", 7, rtmp_a, 512)
                    feature_var("ckv", 6, rtmp_b, 256)
                if n == 21:
                    go(dve.tensor_copy(pick[:, :], tab[H, C_ID:C_ID + SSM_H]))
                    go(dve.tensor_copy(acum_h[H, :], acum[H, :]))
                    go(dve.tensor_tensor(acum_l[H, :], acum[H, :], acum_h[H, :].bitcast(F32), ALU.subtract), S("acum_split"))
                if n == 22:
                    rotate(krT)
                if n == 23:
                    dve.wait_ge(S("dt_turned").sem, 1)
                    go(dve.tensor_copy(small[:, s_cols:s_cols + 60], bank[6][:, 0:60]), S("dt_cols_ready"))
                if n == 23:
                    feature_scale("cq", cq_raw[:, 0:4, :], 4, rtmp_a)
                conv_rest(n)
                if n == 24:
                    feature_scale("ckv", cq_raw[:, 4:6, :], 2, rtmp_b)
            split(N_QKV + 2)
            feature_lo("cq", cq_raw, 4, ch, cl, V_CQ)
            for g in range(2):
                dve.wait_ge(S("cb_done").sem, g + 1)
                go(dve.tensor_tensor(cbm[:, g, :], bank[6 + g][:, 0:384], tab[:, C_CAUSAL:C_CAUSAL + 384], ALU.mult), S("cb_masked"))
            split(N_QKV + 3)
            feature_lo("ckv", cq_raw[:, 4:6, :], 2, ch[:, 4:6, :], cl[:, 4:6, :], V_CKV)

            def ssd_seg(h):
                na0, na1, ea0 = (small[:, s_cols + 12 * k + h:s_cols + 12 * k + h + 1] for k in (2, 3, 4))
                b, e = bank[3 + h % 2], dec[:, h % 4, :]
                dve.wait_ge(S("acum_spread").sem, h + 1)
                if h >= 4:
                    dve.wait_ge(S("ssd_used").sem, h - 3)
                d.mark(dve.tensor_scalar(e[:, 0:P], b[:, 0:P], na0, 0.0, ALU.add, ALU.min), step)
                d.mark(dve.tensor_scalar(e[:, P:T], b[:, P:T], ea0, 0.0, ALU.add, ALU.min), step)
                d.mark(dve.tensor_scalar(e[:, T:T + P], b[:, P:T], na1, 0.0, ALU.add, ALU.min), S("seg_ready"))

            def ssd_weigh(h):
                dt0, dt1 = (small[:, s_cols + 12 * k + h:s_cols + 12 * k + h + 1] for k in (0, 1))
                e, g = dec[:, h % 4, :], h // 6
                dve.wait_ge(S("decay_ready").sem, h + 1)
                d.mark(dve.scalar_tensor_tensor(out=e[:, 0:T], in0=e[:, 0:T], scalar=dt0, in1=cbm[:, g, 0:T],
                                                op0=ALU.mult, op1=ALU.mult), step)
                d.mark(dve.scalar_tensor_tensor(out=e[:, T:T + P], in0=e[:, T:T + P], scalar=dt1, in1=cbm[:, g, T:T + P],
                                                op0=ALU.mult, op1=ALU.mult), S("ssd_weights"))

            def take_y(pair):
                dve.wait_ge(S("ssd_used").sem, 2 * pair + 2)
                d.mark(dve.scalar_tensor_tensor(out=yT[:, pair, :], in0=xbcT[:, pair, :], scalar=small[:, s_dcol + pair:s_dcol + pair + 1],
                                                in1=bank[5 + pair % 2][:, 0:T], op0=ALU.mult, op1=ALU.add), S("y_taken"))

            def take_vm(t):
                dve.wait_ge(S("products_done").sem, products(N_U + 2) + t + 1)
                d.mark(dve.tensor_copy(vm[:, t, 0:512], bank[3 + 2 * t][:, :]), S("vm_ready"))
                d.mark(dve.tensor_copy(vm[:, t, 512:768], bank[4 + 2 * t][:, 0:256]), S("vm_ready"))

            for n in range(N_SSD, N_OUT + 1):
                if n < N_SSD + 6:
                    for h in (2 * (n - N_SSD), 2 * (n - N_SSD) + 1):
                        ssd_seg(h)
                if n == N_PAIR:
                    dve.wait_ge(S("v_turned").sem, 1)
                    d.mark(dve.tensor_copy(v_tok[:, :, :], bank[7][:, 0:T].rearrange("p (t c) -> p t c", c=P)), S("v_tok_ready"))
                if n == N_U + 3:
                    take_vm(0)
                pair = pair_of(n)
                if pair is not None:
                    for j in (2 * pair, 2 * pair + 1):
                        attend_mask(j)
                split(n + 2)
                if n < N_SSD + 6:
                    for h in (2 * (n - N_SSD), 2 * (n - N_SSD) + 1):
                        ssd_weigh(h)
                if N_SSD < n <= N_SSD + 6:
                    take_y(n - N_SSD - 1)
                if pair is not None:
                    for j in (2 * pair, 2 * pair + 1):
                        attend_norm(j)
                if N_U + 2 <= n <= N_ZB:
                    k = n - N_U - 2
                    dve.wait_ge(S("tile_taken").sem, TAKEN_U + 7 + k)
                    rotate(qr[:, k, :])
                if n == N_U + 3:
                    take_vm(1)
                if n == 39:
                    feature_lo("swa", o_swa, 4, ch, cl, V_SWA)

            def mixed_rsqrt(name, groups):
                dve.wait_ge(S(f"{name}_ss").sem, len(groups))
                for c, dim in groups:
                    ins = dve.tensor_scalar(mixed[:, 0, c:c + 2], bank[0][:, c:c + 2], 1.0 / dim, EPS, ALU.mult, ALU.add)
                    d.mark(ins, step if (c, dim) != groups[-1] else S(f"{name}_var"))
                d.settle()
                dve.wait_ge(S(f"{name}_std").sem, 1)
                v, sd, r_, t_ = (mixed[:, k, groups[0][0]:groups[-1][0] + 2] for k in range(4))
                go(dve.reciprocal(r_, sd))
                newton(r_, v, t_)

            def add_mixed(n, pair, cb, c):
                dve.wait_ge(S("products_done").sem, products(n))
                for t in range(TT):
                    block_ = hres[:, t, cb * 512:(cb + 1) * 512]
                    d.mark(dve.scalar_tensor_tensor(out=block_, in0=bank[2 * pair + t][:, :], scalar=mixed[:, 2, c + t:c + t + 1],
                                                    in1=block_, op0=ALU.mult, op1=ALU.add), S("mix_added"))

            dve.wait_ge(S("gate_ready").sem, 1)
            go(dve.tensor_tensor(yT[:, :, :], yT[:, :, :], zT[:, :, :], ALU.mult), S("y_gated"))
            for n in range(N_OUT + 1, N_OUT + 16):
                cb, step_ = (n - N_OUT - 4) // 3, (n - N_OUT - 4) % 3
                if n == N_OUT + 4:
                    feature_lo("ssm", yT, 6, ch, cl, V_SSM)
                split(n + 2)
                if n == N_OUT + 1:
                    feature_lo("mla", o_mla, 6, uh[:, 10:16, :], ul[:, 10:16, :], V_MLA)
                    mixed_rsqrt("heads", ((0, 512), (2, 768)))
                if n == N_OUT + 2:
                    mixed_rsqrt("ssm", ((4, 768),))
                    dve.wait_ge(S("residual_landed").sem, 32)
                    add_mixed(N_OUT, 1, 0, 0)
                    add_mixed(N_OUT + 1, 2, 1, 0)
                if n == N_OUT + 3:
                    add_mixed(N_OUT + 2, 3, 2, 0)
                if n == N_OUT + 4:
                    d.settle()
                    add_mixed(N_OUT + 3, 0, 3, 0)
                if cb >= 0 and step_ == 2:
                    if cb == 0:
                        d.settle()
                    add_mixed(n - 1, (2 * cb + 1) % 4, cb, 2)
                if cb >= 1 and step_ == 0:
                    d.settle()
                    add_mixed(n - 1, 2 * cb % 4, cb - 1, 4)
                if cb >= 1 and step_ == 1:
                    for g in (2 * cb - 2, 2 * cb - 1):
                        token_lo("hx", g, V_CROSS, hx_bank(g))

            def add_bank(b, t, cb, signal):
                d.mark(dve.tensor_tensor(hres[:, t, cb * 512:(cb + 1) * 512], hres[:, t, cb * 512:(cb + 1) * 512], bank[b][:, :],
                                         ALU.add), signal)

            d.settle()
            add_mixed(N_OUT + 15, 0, 3, 4)
            split(N_WQ + 2)
            for g in (6, 7):
                token_lo("hx", g, V_CROSS, hx_bank(g))
            sum_parts("hx")
            token_rsqrt("hx")
            go(dve.tensor_scalar(small[:, s_t:s_t + 2], small[:, s_r:s_r + 2], X_D ** -0.5, None, ALU.mult))
            for n in range(N_WQ + 1, N_WQ + 4):
                if n == N_WQ + 2:
                    attend_mask(A_X)
                    attend_mask(A_X + 1)
                split(n + 2)
                if n == N_WQ + 2:
                    attend_norm(A_X)
                    attend_norm(A_X + 1)

            def cross_lo(k):
                dve.wait_ge(S("out_copied").sem, A_X // 2 + k + 1)
                d.mark(dve.tensor_tensor(cl[:, 2 * k:2 * k + 2, :], bank[7][:, :].rearrange("p (a b) -> p a b", b=T),
                                         ch[:, 2 * k:2 * k + 2, :].bitcast(F32), ALU.subtract), S("cross_lo"))

            cross_lo(0)
            attend_mask(A_X + 2)
            attend_mask(A_X + 3)
            attend_norm(A_X + 2)
            attend_norm(A_X + 3)
            cross_lo(1)
            for n in range(N_WO, N_WO + 4):
                cb = n - N_WO
                split(n + 2)
                if cb >= 2:
                    for g in (2 * cb - 4, 2 * cb - 3):
                        token_lo("hf", g, V_FFN, g)
                dve.wait_ge(S("products_done").sem, products(n))
                for t in range(TT):
                    add_bank(2 * cb + t, t, cb, S("cross_added"))
            for g in range(4, 8):
                token_lo("hf", g, V_FFN, g)
            sum_parts("hf")
            token_rsqrt("hf")
            diagonal("hf", hf_diag)
            split(N_FFN + 2)
            dve.wait_ge(S("hf_spread").sem, 1)
            go(dve.tensor_copy(hf_scale, bank[3][:, 0:T]))
            dve.sem_inc(S("prod_ready").sem, 4)
            dve.sem_inc(S("fconv_raw").sem, 2)

            def ffn_group(i, first=False, last=False):
                def at_turn(v, per):
                    return i * per + v

                def filter_rest(c):
                    s, v, k = c % 4, c % 2, c // 2
                    dve.wait_ge(S("fconv_first").sem, at_turn(c + 1, 8))
                    d.settle()
                    for tap in (1, 2):
                        col = at_turn(v * FT + k + (V_FW + (2 - tap) * 2 * FT), 4)
                        go(dve.scalar_tensor_tensor(out=cacc[:, s, tap:T], in0=craw[:, s, 0:T - tap], scalar=vecs[:, bass.ds(col, 1)],
                                                    in1=cacc[:, s, tap:T], op0=ALU.mult, op1=ALU.add),
                           S("fconv_done") if tap == 2 else None)
                    if v == 1:
                        dve.wait_ge(S("silu_ready").sem, at_turn(k + 1, 4))
                        go(dve.tensor_tensor(prod[:, :], sil[:, :], cacc[:, s, :], ALU.mult), S("prod_ready"))

                for c in range(GROUP):
                    n = N_FFN + c
                    if c == 8:
                        filter_rest(7)
                        gated_lo(3, at_turn)
                    if c in (3, 5, 7):
                        gated_lo((c - 3) // 2, at_turn)
                    if not (last and c >= GROUP - 2) and not (first and c == 0):
                        split(n + 2, i, GROUP)
                    if c < 8:
                        dve.wait_ge(S("products_done").sem, at_turn(products(n), GROUP))
                        d.mark(dve.tensor_tensor(craw[:, c % 4, :], bank[c % 2][:, 0:T], hf_scale, ALU.mult), S("fconv_raw"))
                    if 0 < c < 8:
                        filter_rest(c - 1)
                    if c >= 9:
                        for cb in ((c - 9,) if c < 11 else (2, 3)):
                            dve.wait_ge(S("products_done").sem, at_turn(products(N_FFN + 8 + cb), GROUP))
                            for t in range(TT):
                                add_bank(FFN_BANKS[cb] + t, t, cb, S("ffn_added"))
                            if last:
                                d.settle()
                                for t in range(TT):
                                    cols = slice(cb * 512, (cb + 1) * 512)
                                    d.mark(dve.tensor_tensor(hwork[:, t, cols], hres[:, t, cols], gfin[:, cols], ALU.mult), step)

            def gated_lo(k, at_turn):
                dve.wait_ge(S("gated_hi").sem, at_turn(k + 1, 4))
                d.mark(dve.tensor_tensor(cl[:, k, :], prod[:, :], ch[:, k, :].bitcast(F32), ALU.subtract), S("gated_lo"))

            per = {S("lo_ready"): GROUP, S("fconv_done"): 8, S("prod_ready"): 4, S("gated_lo"): 4, S("ffn_added"): 8,
                   S("fconv_raw"): 8, step: 8}
            start = {s: s.n for s in per}
            start[S("prod_ready")], start[S("fconv_raw")] = 4, 2
            for s in per:
                s.n = start[s]
            ffn_group(0, first=True)
            start[S("lo_ready")] -= 1
            with dve.Fori(1, GROUPS - 1) as i:
                for s in per:
                    s.n = i * per[s] + start[s]
                ffn_group(i)
            for s in per:
                s.n = start[s] + per[s] * (GROUPS - 1)
            dve.wait_ge(S("gfin_landed").sem, 16)
            ffn_group(GROUPS - 1, last=True)
            sum_parts("final")
            token_rsqrt("final", S("final_r"))
            for cb in range(4):
                c = slice(cb * 512, (cb + 1) * 512)
                d.mark(dve.tensor_scalar(hwork[:, 1, c], hwork[:, 1, c], small[:, s_r + 1:s_r + 2], None, ALU.mult), S("out_ready1"))

        @block.tensor
        def _(pe):
            done = S("products_done").sem

            def ready(n, i=None, per=0):
                pe.wait_ge(S("lo_ready").sem, n + 1 if i is None else i * per + n + 1)

            def three(dst, wh, wl, xh, xl, start, stop, stationary_x=False):
                if stationary_x:
                    pe.matmul(dst, xh, wh, start=start, stop=False)
                    pe.matmul(dst, xh, wl, start=False, stop=False)
                    return pe.matmul(dst, xl, wh, start=False, stop=stop)
                pe.matmul(dst, wh, xh, start=start, stop=False)
                pe.matmul(dst, wh, xl, start=False, stop=False)
                return pe.matmul(dst, wl, xh, start=False, stop=stop)

            def tile_product(n, b, cols=P, mid=None, lo_signal=None, ks=(0, KD)):
                s = n % RING
                for k in range(*ks):
                    if k == KD // 2 and mid:
                        mid()
                    if lo_signal and k % 2 == 0:
                        pe.wait_ge(S(lo_signal).sem, k + 2)
                    last = three(bank[b][0:cols, 0:T], hi[:, s, k * P:k * P + cols], lo[:, s, k * P:k * P + cols],
                                 uh[:, k, :], ul[:, k, :], k == 0, k == KD - 1)
                if ks[1] == KD:
                    last.then_inc(done, 1)

            def row_product(n, xh, xl, k0, b0, start, stop, signal=True, ks=range(4), mid=None):
                s = n % RING
                for t in range(TT):
                    if t == 1 and mid:
                        mid()
                    for k in ks:
                        last = three(bank[b0 + t][:, :], hi[:, s, k * 512:(k + 1) * 512], lo[:, s, k * 512:(k + 1) * 512],
                                     xh[:, k0 + k, t * P:(t + 1) * P], xl[:, k0 + k, t * P:(t + 1) * P],
                                     start and k == ks[0], stop and k == ks[-1], stationary_x=True)
                if signal:
                    last.then_inc(done, 1)

            def turn_group(name, src, g, b):
                for k in (2 * g, 2 * g + 1):
                    for t in range(TT):
                        o = (k % 2) * T + t * P
                        last = pe.transpose(bank[b][:, o:o + P], src[:, t, k * P:(k + 1) * P], ident)
                last.then_inc(S(f"{name}_turned").sem, 1)

            def turn_block(name, added, cb, count, bank_of):
                pe.wait_ge(S(added).sem, count)
                for g in (2 * cb, 2 * cb + 1):
                    for k in (2 * g, 2 * g + 1):
                        for t in range(TT):
                            o = (k % 2) * T + t * P
                            last = pe.transpose(bank[bank_of(g)][:, o:o + P], hres[:, t, k * P:(k + 1) * P], ident)
                    last.then_inc(S(f"{name}_turned").sem, 1)

            def turn_scaled(name, src, diag, g, b):
                pe.wait_ge(S(f"{name}_diagonal").sem, TT)
                for k in (2 * g, 2 * g + 1):
                    for t in range(TT):
                        o = (k % 2) * T + t * P
                        last = pe.matmul(bank[b][:, o:o + P], src[:, t, k * P:(k + 1) * P], diag[:, t, :], start=True, stop=True)
                last.then_inc(S(f"{name}_turned").sem, 1)

            def spread_scale(name, diag, b):
                pe.wait_ge(S(f"{name}_diagonal").sem, TT)
                for t in range(TT):
                    last = pe.matmul(bank[b][:, t * P:(t + 1) * P], ones, diag[:, t, :], start=True, stop=True)
                last.then_inc(S(f"{name}_spread").sem, 1)

            def token_sums(name, sq, n, col):
                for t in range(TT):
                    for k in range(n):
                        last = pe.matmul(bank[0][:, col + t:col + t + 1], sq[:, k * T + t * P:k * T + (t + 1) * P], ones[:, 0:1],
                                         start=(k == 0), stop=(k == n - 1))
                last.then_inc(S(f"{name}_ss").sem, 1)

            def square_sum(name, sq, n, b):
                pe.wait_ge(S(f"{name}_sq").sem, 1)
                for k in range(n):
                    last = pe.matmul(bank[b][:, 0:T], ones, sq[:, k * T:(k + 1) * T], start=(k == 0), stop=(k == n - 1))
                last.then_inc(S(f"{name}_ss").sem, 1)

            def scores(j):
                b = bank[3 + j % 2]
                if j >= 2:
                    pe.wait_ge(S("scores_taken").sem, j - 1)
                if j < A_MLA:
                    r = 64 * (j % 2)
                    key = swa_k if (j // 4) == (j % 2) else swa_kswap
                    pairs = [(swa_q[r:r + 64, j // 2, :], key[r:r + 64, :])]
                elif j < A_X:
                    h = j - A_MLA
                    r = 64 * (h % 2)
                    pairs = [(qn[:, h, :], kn[:, h, :]), (qr[r:r + 64, h // 2, :], krT[r:r + 64, :])]
                else:
                    h = j - A_X
                    pairs = [(q_x[:, h, :], kxT[:, h, :])]
                for t in range(TT):
                    c0, c1 = span(j, t)
                    for m, (q, k) in enumerate(pairs):
                        last = pe.matmul(b[:, c0:c1], q[:, t * P:(t + 1) * P], k[:, 0:c1 - c0], start=(m == 0), stop=(m == len(pairs) - 1))
                last.then_inc(S("scores_done").sem, 1)

            def turn_probs(j):
                pe.wait_ge(S("probs_ready").sem, j + 1)
                if j >= 2:
                    pe.wait_ge(S("probsT_copied").sem, j - 1)
                blocks = [(0, 0), (P, P), (2 * P, 2 * P)] if j < A_X else [(0, 0), (T, P), (P, T), (T + P, T + P)]
                for src, dst in blocks:
                    last = pe.transpose(bank[5 + j % 2][:, dst:dst + P], ssb[:, j % 2, src:src + P], ident)
                last.then_inc(S("probsT_done").sem, 1)

            def head_out(j):
                pe.wait_ge(S("probsT_copied").sem, j + 1)
                if j >= 2 and j % 2 == 0:
                    pe.wait_ge(S("out_copied").sem, j // 2)
                if j == A_X + 2:
                    pe.wait_ge(S("cross_lo").sem, 1)
                if j < A_X:
                    parts_ = [(0, 0, P, 0, True, True), (0, P, T, P, True, False), (1, P, T, 2 * P, False, True)]
                else:
                    parts_ = [(0, 0, T, 0, True, False), (1, 0, T, T, False, True)]
                for kt, q0, q1, c, start, stop in parts_:
                    if j < A_MLA:
                        r, g = 64 * (j % 2), j // 4
                        v, o = v_tok[:, kt, 64 * g:64 * g + 64], bank[7][r:r + 64, q0:q1]
                    else:
                        h = j - A_MLA if j < A_X else j - A_X
                        v, o = (vm if j < A_X else vx)[:, kt, h * P:(h + 1) * P], bank[7][:, T * (j % 2) + q0:T * (j % 2) + q1]
                    last = pe.matmul(o, v, pts[:, j % 2, c:c + q1 - q0], start=start, stop=stop)
                last.then_inc(S("out_done").sem, 1)

            def both(f, pair):
                f(2 * pair)
                f(2 * pair + 1)

            pe.wait_ge(S("consts_landed").sem, 32)
            pe.transpose(bank[7][:, V_MEM:V_ALL], mem_rows[0:16, :], tab[0:16, C_ID:C_ID + 16]).then_inc(S("vecs_turned").sem, 1)
            for g in range(8):
                pe.wait_ge(S(f"mem_landed{g // 2}").sem, 16)
                if g == 7:
                    pe.wait_ge(S("vecs_ready").sem, 1)
                turn_group("mem", mems, g, g)
            for n in range(N_XK, N_XK + 4):
                if n == 0:
                    pe.wait_ge(S("first_lo").sem, 1)
                    tile_product(n, n, lo_signal="mem_lo", ks=(0, KD // 2))
                    ready(n)
                    tile_product(n, n, lo_signal="mem_lo", ks=(KD // 2, KD))
                else:
                    ready(n)
                    tile_product(n, KEY_BANKS[n], mid=(lambda: spread_scale("mem", mem_diag, 4)) if n == 2 else None)
                if n == 2:
                    pe.wait_ge(S("vectors_landed").sem, N_VECTORS)
                    for k, (r, col) in enumerate(((V_ROWS_A, 0), (40, V_CW), (88, V_FW), (88, V_FW + 88), (88, V_FW + 176), (88, V_FB))):
                        last = pe.transpose(bank[3][:, col:col + r], vrows[0:r, k, :], tab[0:r, C_ID:C_ID + r])
                    last.then_inc(S("vecs_turned").sem, 1)
            for n in range(N_XV, N_XV + 4):
                ready(n)
                g = n - N_XV
                row_product(n, uh, ul, 4 * g, 4, g == 0, g == 3)
                if g == 0:
                    pe.wait_ge(S("key_taken").sem, 2)
                    pe.wait_ge(S("vecs_ready").sem, 2)
                if g == 1:
                    pe.wait_ge(S("key_taken").sem, 4)
                if g == 2:
                    pe.wait_ge(S("x_lo").sem, 2)
                if g == 3:
                    pe.wait_ge(S("x_lo").sem, 6)
                for gg in (2 * g, 2 * g + 1):
                    turn_scaled("x", xs, x_diag, gg, X_BANKS[gg])
            with_lo = "x_lo"
            for n in range(N_CQ, N_CQ + 6):
                ready(n)
                if n >= N_CQ + 3:
                    pe.wait_ge(S("tile_taken").sem, n - N_CQ - 2)
                tile_product(n, n % 3, lo_signal=with_lo)
                with_lo = None
            ready(N_KRDT)
            pe.wait_ge(S("tile_taken").sem, 4)
            tile_product(N_KRDT, N_KRDT % 3, ROPE + SSM_H)

            def w_in_tile(n, mid=None):
                ready(n)
                pe.wait_ge(S("tile_taken").sem, TAKEN_XBC + n - N_XBC - 2)
                tile_product(n, n % 3, mid=mid)

            def turn_x(b):
                pe.wait_ge(S("xbc_ready").sem, 2 * b + 2)
                for k in (2 * b, 2 * b + 1):
                    for t in range(TT):
                        o = (k % 2) * T + t * P
                        last = pe.transpose(bank[3 + b][:, o:o + P], xbcT[:, k, t * P:(t + 1) * P], ident)
                last.then_inc(S("xbc_turned").sem, 1)

            for n in range(N_XBC, N_QKV + 2):
                if n == 21:
                    square_sum("cq", sq_cq, 4, 7)
                    square_sum("ckv", sq_ckv, 2, 6)
                if n == 23:
                    pe.wait_ge(S("dt_rows_ready").sem, 1)
                    pe.wait_ge(S("ckv_var").sem, 1)
                    for k, (row, t) in enumerate(((0, 0), (0, 1), (2, 0), (2, 1), (3, 0))):
                        last = pe.transpose(bank[6][:, 12 * k:12 * k + 12], dt_rows[0:SSM_H, row, t * P:(t + 1) * P],
                                            tab[0:SSM_H, C_ID:C_ID + SSM_H])
                    last.then_inc(S("dt_turned").sem, 1)
                if n in (22, 23, 24):
                    pe.wait_ge(S("vx_ready").sem, 2)
                    turn_x(n - 22)
                if n == 26:
                    pe.wait_ge(S("dt_cols_ready").sem, 1)
                    pe.wait_ge(S("xbc_ready").sem, 10)
                    for g in range(2):
                        b = bank[6 + g]
                        pe.matmul(b[:, 0:T], xbcT[:, 6 + g, 0:P], xbcT[:, 8 + g, :], start=True, stop=True)
                        pe.matmul(b[:, T:T + P], xbcT[:, 6 + g, P:T], xbcT[:, 8 + g, P:T], start=True, stop=True).then_inc(S("cb_done").sem, 1)
                w_in_tile(n)

            def spread(h):
                if h < 2:
                    pe.wait_ge(S("acum_split").sem, 1)
                    pe.wait_ge(S("x_tok_ready").sem, 6)
                else:
                    pe.wait_ge(S("seg_ready").sem, h - 1)
                one = pick[:, h:h + 1].to_broadcast([SSM_H, P])
                pe.matmul(bank[3 + h % 2][:, 0:T], one, acum_h[0:SSM_H, :], start=True, stop=False)
                pe.matmul(bank[3 + h % 2][:, 0:T], one, acum_l[0:SSM_H, :], start=False, stop=True).then_inc(S("acum_spread").sem, 1)

            def ssd_y(h):
                pair, r = h // 2, 64 * (h % 2)
                b = bank[5 + pair % 2]
                if h % 2 == 0:
                    if pair < 2:
                        pe.wait_ge(S("dt_cols_ready").sem, 1)
                    else:
                        pe.wait_ge(S("y_taken").sem, pair - 1)
                pe.wait_ge(S("ssd_weights").sem, h + 1)
                e = dec[:, h % 4, :]
                pe.matmul(b[r:r + 64, 0:P], x_tok[:, 0, h * 64:(h + 1) * 64], e[:, 0:P], start=True, stop=True)
                pe.matmul(b[r:r + 64, P:T], x_tok[:, 0, h * 64:(h + 1) * 64], e[:, P:T], start=True, stop=False)
                pe.matmul(b[r:r + 64, P:T], x_tok[:, 1, h * 64:(h + 1) * 64], e[:, T:T + P], start=False, stop=True).then_inc(S("ssd_used").sem, 1)

            def latent_tile(index, w0, wcols, k0, kn_, s):
                pe.wait_ge(S("tile_taken").sem, TAKEN_U + index - 2)
                b = bank[(products(N_U - 1) + index) % 3]
                for k in range(kn_):
                    o = w0 + k * wcols
                    last = three(b[:, 0:T], hi[:, s, o:o + P], lo[:, s, o:o + P], ch[:, k0 + k, :], cl[:, k0 + k, :], k == 0, k == kn_ - 1)
                last.then_inc(done, 1)

            def latent_values(t, s):
                for b, c0, c1 in ((3 + 2 * t, 0, 512), (4 + 2 * t, 512, 768)):
                    for k in range(2):
                        o = k * MLA_H * VD
                        last = three(bank[b][:, 0:c1 - c0], hi[:, s, o + c0:o + c1], lo[:, s, o + c0:o + c1],
                                     ch[:, 4 + k, t * P:(t + 1) * P], cl[:, 4 + k, t * P:(t + 1) * P], k == 0, k == 1,
                                     stationary_x=True)
                last.then_inc(done, 1)

            for n in range(N_SSD, N_OUT):
                s = n % RING
                if n < N_SSD + 6:
                    both(spread, n - N_SSD)
                turn, new = pair_of(n - 1), pair_of(n)
                if n == N_PAIR:
                    pe.wait_ge(S("tile_taken").sem, TAKEN_XBC + 16)
                    for t in range(TT):
                        last = pe.transpose(bank[7][:, t * P:(t + 1) * P], swa_v[:, t * P:(t + 1) * P], ident)
                    last.then_inc(S("v_turned").sem, 1)
                    pe.wait_ge(S("seg_ready").sem, SSM_H)
                if n == N_PAIR + 1:
                    pe.wait_ge(S("y_taken").sem, 6)
                    pe.wait_ge(S("v_tok_ready").sem, 1)
                if n >= N_ZB:
                    pe.wait_ge(S("vm_ready").sem, 2 if n == N_ZB else 4)
                if turn is not None:
                    both(turn_probs, turn)
                if n >= N_ZB:
                    pe.wait_ge(S("rotated").sem, 2 + n - N_ZB)
                if new is not None:
                    both(scores, new)

                def mid():
                    if N_SSD < n <= N_SSD + 6:
                        both(ssd_y, n - N_SSD - 1)
                    if turn is not None:
                        both(head_out, turn)

                ready(n)
                if n < N_ZA:
                    w_in_tile(n, mid)
                elif n < N_U:
                    pe.wait_ge(S("tile_taken").sem, TAKEN_XBC + n - N_XBC - 2)
                    tile_product(n, z_bank(n), mid=mid)
                elif n == N_U:
                    pe.wait_ge(S("ckv_lo").sem, 2)
                    for h in range(4):
                        if h == 2:
                            mid()
                        latent_tile(h, h * NOPE, 4 * NOPE, 0, 4, s)
                elif n == N_U + 1:
                    for h in range(2):
                        latent_tile(4 + h, h * NOPE, 2 * NOPE, 0, 4, s)
                    mid()
                    for h in range(2):
                        latent_tile(6 + h, 1024 + h * P, 4 * ROPE, 0, 4, s)
                elif n == N_U + 2:
                    latent_tile(8, 0, P, 0, 4, s)
                    for h in range(6):
                        if h == 2:
                            mid()
                        latent_tile(9 + h, 512 + h * NOPE, 6 * NOPE, 4, 2, s)
                elif n == N_U + 3:
                    pe.wait_ge(S("scores_taken").sem, A_MLA)
                    latent_values(0, s)
                    mid()
                    latent_values(1, s)
                else:
                    pe.wait_ge(S("tile_taken").sem, TAKEN_U + 15 + (n - N_ZB) - 2)
                    tile_product(n, z_bank(n), mid=mid)

            both(turn_probs, A_X // 2 - 1)

            def last_heads():
                both(head_out, A_X // 2 - 1)

            def head_sums():
                pe.wait_ge(S("tile_taken").sem, TAKEN_U + 18)
                pe.wait_ge(S("mla_sq").sem, 1)
                token_sums("heads", sq_swa, 4, 0)
                token_sums("heads", sq_mla, 6, 2)

            def ssm_sums():
                pe.wait_ge(S("ssm_sq").sem, 1)
                pe.wait_ge(S("heads_var").sem, 1)
                token_sums("ssm", sq_ssm, 6, 4)

            mids = (last_heads, head_sums, None, None)
            pe.wait_ge(S("swa_lo").sem, 4)
            for cb in range(4):
                n = N_OUT + cb
                ready(n)
                if cb == 3:
                    ssm_sums()
                    pe.wait_ge(S("ssm_var").sem, 1)
                row_product(n, ch, cl, 0, 2 * ((cb + 1) % 4), True, True, mid=mids[cb])
            for cb in range(4):
                n = N_OUT + 4 + 3 * cb
                mla_b, ssm_b = 2 * ((2 * cb + 1) % 4), 2 * ((2 * cb + 2) % 4)
                ready(n)
                if cb == 0:
                    pe.wait_ge(S("mla_lo").sem, 6)
                pe.wait_ge(S("mix_added").sem, 4 * cb + 2)
                row_product(n, uh, ul, 10, mla_b, True, False)
                if cb > 0:
                    turn_block("hx", "mix_added", cb - 1, 8 + 4 * cb, hx_bank)
                ready(n + 1)
                row_product(n + 1, uh, ul, 14, mla_b, False, True, signal=False, ks=(0, 1))
                if cb == 0:
                    pe.wait_ge(S("ssm_lo").sem, 6)
                if cb >= 2:
                    pe.wait_ge(S("hx_lo").sem, 4 * cb - 4)
                pe.wait_ge(S("mix_added").sem, 4 * cb + 4)
                row_product(n + 1, ch, cl, -2, ssm_b, True, False, ks=(2, 3))
                ready(n + 2)
                row_product(n + 2, ch, cl, 2, ssm_b, False, True)
            ready(N_WQ)
            pe.wait_ge(S("hx_lo").sem, 12)
            tile_product(N_WQ, WQ_BANKS[0], ks=(0, 12))
            turn_block("hx", "mix_added", 3, 24, hx_bank)
            ready(N_WQ + 1)
            tile_product(N_WQ + 1, WQ_BANKS[1], ks=(0, 12))
            pe.wait_ge(S("hx_lo").sem, 16)
            tile_product(N_WQ, WQ_BANKS[0], ks=(12, 16))
            tile_product(N_WQ + 1, WQ_BANKS[1], ks=(12, 16))
            for n in (N_WQ + 2, N_WQ + 3):
                ready(n)

                def mid():
                    if n == N_WQ + 2:
                        pe.wait_ge(S("tile_taken").sem, TAKEN_U + 20)
                        both(scores, A_X // 2)
                    if n == N_WQ + 3:
                        both(turn_probs, A_X // 2)
                tile_product(n, WQ_BANKS[n - N_WQ], mid=mid)
            both(head_out, A_X // 2)
            pe.wait_ge(S("tile_taken").sem, TAKEN_U + 22)
            both(scores, A_X // 2 + 1)
            pe.wait_ge(S("cross_lo").sem, 1)
            ready(N_WO)
            row_product(N_WO, ch, cl, 0, 0, True, False, signal=False, ks=range(2))
            both(turn_probs, A_X // 2 + 1)
            ready(N_WO + 1)
            row_product(N_WO + 1, ch, cl, 0, 2, True, False, signal=False, ks=range(2))
            both(head_out, A_X // 2 + 1)
            pe.wait_ge(S("cross_lo").sem, 2)
            for cb in (0, 1):
                row_product(N_WO + cb, ch, cl, 0, 2 * cb, False, True, ks=range(2, 4))
            def turn_hf(cb):
                turn_block("hf", "cross_added", cb, TT * cb + TT, lambda g: g)

            for cb in (2, 3):
                ready(N_WO + cb)
                row_product(N_WO + cb, ch, cl, 0, 2 * cb, True, True, mid=lambda: turn_hf(cb - 2))
            turn_hf(2)

            def ffn_group(i, first=False):
                for c in range(8):
                    n = N_FFN + c
                    if first and c == 0:
                        ready(N_FFN)
                        pe.wait_ge(S("hf_lo").sem, 8)
                        tile_product(N_FFN, 0, ks=(0, 8))
                        turn_hf(3)
                        pe.wait_ge(S("hf_lo").sem, 12)
                        tile_product(N_FFN, 0, ks=(8, 12))
                        ready(N_FFN + 1)
                        tile_product(N_FFN + 1, 1, ks=(0, 12))
                        pe.wait_ge(S("hf_lo").sem, 16)
                        tile_product(N_FFN, 0, ks=(12, KD))
                        spread_scale("hf", hf_diag, 3)
                        tile_product(N_FFN + 1, 1, ks=(12, KD))
                    if first and c < 2:
                        continue
                    ready(n, i, GROUP)
                    pe.wait_ge(S("fconv_raw").sem, i * 8 + (c + 1))
                    tile_product(n, c % 2)
                for c in (8, 9):
                    pe.wait_ge(S("gated_lo").sem, i * 4 + 3)
                    ready(N_FFN + c, i, GROUP)
                    row_product(N_FFN + c, ch, cl, 0, FFN_BANKS[c - 8], True, False, signal=False, ks=range(3))
                pe.wait_ge(S("gated_lo").sem, i * 4 + 4)
                for c in (8, 9):
                    row_product(N_FFN + c, ch, cl, 0, FFN_BANKS[c - 8], False, True, ks=range(3, 4))
                for c in (10, 11):
                    ready(N_FFN + c, i, GROUP)
                    if c == 11:
                        pe.wait_ge(S("ffn_added").sem, i * 8 + 2)
                    row_product(N_FFN + c, ch, cl, 0, FFN_BANKS[c - 8], True, True)

            ffn_group(0, True)
            with pe.Fori(1, GROUPS) as i:
                ffn_group(i)


KEY_BANKS = (0, 1, 2, 7)
X_BANKS = (1, 3, 6, 7, 0, 1, 3, 6)
FFN_BANKS = (2, 4, 6, 2)
WQ_BANKS = (2, 7, 0, 1)
OUT_CHUNKS = [(3, cb) for cb in range(4)] + [(g, cb) for cb in range(4) for g in range(3)]
N_VECTORS = 16 * (1 + 9 + 1 + 3 + 1)
TAKEN_XBC = 7
TAKEN_U = TAKEN_XBC + 16 + 3
N_SSD = 27
N_PAIR = 33


def z_bank(n):
    return n % 3 if n < N_U else (n - N_ZB + 1) % 3


def hx_bank(g):
    return (4, 5, 0, 1)[g % 4]


def pair_of(n):
    if N_PAIR <= n < N_PAIR + A_MLA // 2:
        return n - N_PAIR
    if N_ZB <= n < N_OUT:
        return n - N_ZB + A_MLA // 2
    return None


def span(j, t):
    if j >= A_X:
        return t * 256, (t + 1) * 256
    return (0, 128) if t == 0 else (128, 384)


def ssd_exp(h, act, a, S, dec):
    act.wait_ge(S("seg_ready").sem, h + 1)
    a.mark(act.activation(dec[:, h % 4, :], dec[:, h % 4, :], ACT.Exp), S("decay_ready"))


_INS = ['x', 'mem', 'positions', 'norm_mix', 'w_in', 'mla_q_norm', 'mla_w_uq', 'mla_kv_norm', 'mla_w_ukv',
        'mla_out_norm', 'ssm_conv_w', 'ssm_conv_b', 'ssm_dt_bias', 'ssm_a_log', 'ssm_d', 'ssm_norm', 'swa_sinks',
        'swa_out_norm', 'w_out', 'norm_cross', 'norm_mem', 'cross_wq', 'cross_wkv', 'cross_wo', 'norm_ffn',
        'ffn_w_up', 'ffn_conv_w', 'ffn_conv_b', 'ffn_w_down', 'norm_final']


def kernel(**inputs):
    import numpy as _np
    import concourse.bacc as _bacc
    from concourse import mybir as _mybir
    from concourse.bass_utils import run_bass_kernel_spmd as _run

    nc = _bacc.Bacc("TRN2", target_bir_lowering=False, num_devices=1)
    arrays, args = {}, []
    for name in _INS:
        arr = _np.ascontiguousarray(inputs[name])
        arrays[f"in_{name}_dram"] = arr
        args.append(nc.dram_tensor(f"in_{name}_dram", arr.shape, _mybir.dt.from_np(arr.dtype), kind="ExternalInput").ap())
    arrays["table_dram"] = constant_table()
    args.append(nc.dram_tensor("table_dram", (P, C_ALL), F32, kind="ExternalInput").ap())
    args.append(nc.dram_tensor("out_0_dram", (1, T, D), F32, kind="ExternalOutput").ap())
    encoder(nc, *args)
    r = _run(nc, [arrays], core_ids=[0])
    return r.results[0]["out_0_dram"]
```
